# Optimizing a Trainium2 kernel written in Bass

```python
import math
import jax, jax.numpy as jnp
from jax import lax
import numpy as np

D_MODEL = 1024
BATCH = 1
SEQ = 128
DEPTH = 1
DEC_BATCH = 1
DEC_SEQ = 1024
PAST_LEN = 128

GRID_W = 64
CHUNK = 128
A_GROUPS = 4
A_GROUP_DIM = 128
A_WIDTH = A_GROUPS * A_GROUP_DIM
MLA_HEADS = 4
QK_NOPE = 128
QK_ROPE = 64
ROPE_DIM = QK_ROPE
V_DIM = 128
Q_RANK = 384
KV_RANK = 256
B_WIDTH = MLA_HEADS * V_DIM
Q_BLOCK = 128
ROPE_THETA = 10000.0
IN_COLS = 2 * A_WIDTH + Q_RANK + KV_RANK + ROPE_DIM
SPLITS = (A_WIDTH, 2 * A_WIDTH, 2 * A_WIDTH + Q_RANK, 2 * A_WIDTH + Q_RANK + KV_RANK)
MIX_WIDTH = A_WIDTH + B_WIDTH
N_KEYS = 128
N_EXPERTS = N_KEYS * N_KEYS
PEER_HEADS = 8
PEER_HALF = 128
PEER_QDIM = 2 * PEER_HALF
PEER_TOPK = 16
PEER_BLOCK = 128
ALPHA = (2.0 * DEPTH) ** 0.25
BETA = (8.0 * DEPTH) ** -0.25
EPS = 1e-6

kernel_name = "hybrid_diffusion_chunkmlp_mla_peer_step"

def layer_norm(x, g, b):
    xf = x.astype(jnp.float32)
    mu = jnp.mean(xf, -1, keepdims=True)
    var = jnp.mean(jnp.square(xf - mu), -1, keepdims=True)
    y = (xf - mu) * lax.rsqrt(var + EPS)
    return (y * g.astype(jnp.float32) + b.astype(jnp.float32)).astype(x.dtype)

def standardize(x):
    xf = x.astype(jnp.float32)
    mu = jnp.mean(xf, -1, keepdims=True)
    var = jnp.mean(jnp.square(xf - mu), -1, keepdims=True)
    return ((xf - mu) * lax.rsqrt(var + EPS)).astype(x.dtype)

def rms_norm(x, g):
    xf = x.astype(jnp.float32)
    y = xf * lax.rsqrt(jnp.mean(jnp.square(xf), -1, keepdims=True) + EPS)
    return (y * g.astype(jnp.float32)).astype(x.dtype)

def rope_1d(x, pos):
    f = x.shape[-1] // 2
    freqs = 1.0 / (ROPE_THETA ** (jnp.arange(f, dtype=jnp.float32) / f))
    ang = pos[:, None] * freqs[None, :]
    ang = ang.reshape((ang.shape[0],) + (1,) * (x.ndim - 3) + (f,))
    cos, sin = jnp.cos(ang).astype(x.dtype), jnp.sin(ang).astype(x.dtype)
    x1, x2 = x[..., :f], x[..., f:]
    return jnp.concatenate([x1 * cos - x2 * sin, x1 * sin + x2 * cos], axis=-1)

def rope_2d(x, row, col):
    half = x.shape[-1] // 2
    return jnp.concatenate([rope_1d(x[..., :half], row), rope_1d(x[..., half:], col)], axis=-1)

def chunk_sgu(u, v, w_s, b_s):
    B, N, _ = u.shape
    v = standardize(v.reshape(B, N // CHUNK, CHUNK, A_GROUPS, A_GROUP_DIM))
    mixed = jnp.einsum('gpq,bcqgd->bcpgd', w_s, v) + b_s.T[:, :, None]
    return u * mixed.reshape(B, N, A_WIDTH)

def mla_attention(q_nope, q_rope, k_nope, k_rope, v):
    B, N, H, _ = q_nope.shape
    nb = N // Q_BLOCK
    scale = 1.0 / math.sqrt(QK_NOPE + QK_ROPE)
    qn = jnp.moveaxis(q_nope.reshape(B, nb, Q_BLOCK, H, QK_NOPE), 1, 0)
    qr = jnp.moveaxis(q_rope.reshape(B, nb, Q_BLOCK, H, QK_ROPE), 1, 0)

    def one_block(blk):
        bn, br = blk
        s = (jnp.einsum('bqhd,bkhd->bhqk', bn, k_nope)
             + jnp.einsum('bqhr,bkr->bhqk', br, k_rope))
        p = jax.nn.softmax(s.astype(jnp.float32) * scale, axis=-1).astype(v.dtype)
        return jnp.einsum('bhqk,bkhd->bqhd', p, v)

    o = lax.map(one_block, (qn, qr))
    return jnp.moveaxis(o, 0, 1).reshape(B, N, H * V_DIM)

def peer(h, w_pq, sub_keys, u_tab, v_tab):
    B, N, D = h.shape
    T = B * N
    hf = h.reshape(T, D)
    q = (hf @ w_pq).reshape(T, PEER_HEADS, 2, PEER_HALF)
    s = jnp.einsum('thsd,hskd->thsk', q, sub_keys)
    s_top, i_top = lax.top_k(s, PEER_TOPK)
    cand_s = (s_top[:, :, 0, :, None] + s_top[:, :, 1, None, :]).reshape(T, PEER_HEADS, PEER_TOPK * PEER_TOPK)
    cand_i = (i_top[:, :, 0, :, None] * N_KEYS + i_top[:, :, 1, None, :]).reshape(T, PEER_HEADS, PEER_TOPK * PEER_TOPK)
    f_s, f_pos = lax.top_k(cand_s, PEER_TOPK)
    ids = jnp.take_along_axis(cand_i, f_pos, axis=-1)
    g = jax.nn.softmax(f_s.astype(jnp.float32), axis=-1).astype(h.dtype)
    nb = T // PEER_BLOCK
    hb = hf.reshape(nb, PEER_BLOCK, D)
    ib = ids.reshape(nb, PEER_BLOCK, PEER_HEADS * PEER_TOPK)
    gb = g.reshape(nb, PEER_BLOCK, PEER_HEADS * PEER_TOPK)

    def one_block(blk):
        xb, eb, wb = blk
        u = jnp.take(u_tab, eb, axis=0)
        a = jax.nn.gelu(jnp.einsum('tkd,td->tk', u, xb), approximate=False)
        vv = jnp.take(v_tab, eb, axis=0)
        return jnp.einsum('tk,tkd->td', wb * a, vv)

    out = lax.map(one_block, (hb, ib, gb))
    return out.reshape(B, N, D)

def trunk_layer(x, mod, ctx_ckv, ctx_krope, is_latent, w_in, w_s, b_s, g_q, w_qb, g_kv, w_kvb,
                w_o, ln1_g, ln1_b, w_pq, sub_keys, u_tab, v_tab, ln2_g, ln2_b):
    B, N, _ = x.shape
    shift1, scale1, gate1, shift2, scale2, gate2 = [mod[:, i][:, None, :] for i in range(6)]
    h = x * (1.0 + scale1) + shift1
    z = h @ w_in
    ua, va, q_lat, kv_lat, k_rope = jnp.split(z, SPLITS, axis=-1)
    a_out = chunk_sgu(jax.nn.gelu(ua, approximate=False), jax.nn.gelu(va, approximate=False), w_s, b_s)
    q = (rms_norm(q_lat, g_q) @ w_qb).reshape(B, N, MLA_HEADS, QK_NOPE + QK_ROPE)
    q_nope, q_rope = q[..., :QK_NOPE], q[..., QK_NOPE:]
    ckv = rms_norm(kv_lat, g_kv)
    if is_latent:
        rows = N // GRID_W
        row = jnp.repeat(jnp.arange(rows, dtype=jnp.float32), GRID_W)
        col = jnp.tile(jnp.arange(GRID_W, dtype=jnp.float32), rows)
        q_rope = rope_2d(q_rope, row, col)
        k_rope = rope_2d(k_rope, row, col)
        keys_ckv = jnp.concatenate([ctx_ckv, ckv], axis=1)
        keys_kr = jnp.concatenate([ctx_krope, k_rope], axis=1)
    else:
        keys_ckv, keys_kr = ckv, k_rope
    M = keys_ckv.shape[1]
    kv = (keys_ckv @ w_kvb).reshape(B, M, MLA_HEADS, QK_NOPE + V_DIM)
    k_nope, v = kv[..., :QK_NOPE], kv[..., QK_NOPE:]
    b_out = mla_attention(q_nope, q_rope, k_nope, keys_kr, v)
    mix = jnp.concatenate([a_out, b_out], axis=-1) @ w_o
    x = layer_norm(ALPHA * x + gate1 * mix, ln1_g, ln1_b)
    h2 = x * (1.0 + scale2) + shift2
    x = layer_norm(ALPHA * x + gate2 * peer(h2, w_pq, sub_keys, u_tab, v_tab), ln2_g, ln2_b)
    return x, ckv, k_rope

def setup_inputs(seed: int = 0) -> dict:
    key = jax.random.key(seed)
    ks = jax.random.split(key, 32)
    f32 = jnp.float32
    nrm = lambda k, shape, s: jax.random.normal(k, shape, f32) * s
    L, D = DEPTH, D_MODEL
    return {
        "x_prompt": nrm(ks[0], (BATCH, SEQ, D), 1.0),
        "x_sample": nrm(ks[1], (DEC_BATCH, DEC_SEQ, D), 1.0),
        "cache_ckv": nrm(ks[2], (DEC_BATCH, L, PAST_LEN, KV_RANK), 1.0),
        "cache_krope": nrm(ks[3], (DEC_BATCH, L, PAST_LEN, ROPE_DIM), 1.0),
        "c": nrm(ks[4], (DEC_BATCH, D), 1.0),
        "c_ctx": nrm(ks[5], (D,), 1.0),
        "w_mod": nrm(ks[6], (L, D, 6 * D), D ** -0.5),
        "b_mod": nrm(ks[7], (L, 6 * D), 0.01),
        "w_in": nrm(ks[8], (L, D, IN_COLS), D ** -0.5),
        "w_s": nrm(ks[9], (L, A_GROUPS, CHUNK, CHUNK), CHUNK ** -0.5),
        "b_s": 1.0 + nrm(ks[10], (L, A_GROUPS, CHUNK), 0.01),
        "g_q": 1.0 + nrm(ks[11], (L, Q_RANK), 0.01),
        "w_qb": nrm(ks[12], (L, Q_RANK, MLA_HEADS * (QK_NOPE + QK_ROPE)), Q_RANK ** -0.5),
        "g_kv": 1.0 + nrm(ks[13], (L, KV_RANK), 0.01),
        "w_kvb": nrm(ks[14], (L, KV_RANK, MLA_HEADS * (QK_NOPE + V_DIM)), KV_RANK ** -0.5),
        "w_o": nrm(ks[15], (L, MIX_WIDTH, D), BETA * MIX_WIDTH ** -0.5),
        "ln1_g": 1.0 + nrm(ks[16], (L, D), 0.01),
        "ln1_b": nrm(ks[17], (L, D), 0.01),
        "w_pq": nrm(ks[18], (L, D, PEER_HEADS * PEER_QDIM), D ** -0.5),
        "sub_keys": nrm(ks[19], (L, PEER_HEADS, 2, N_KEYS, PEER_HALF), PEER_HALF ** -0.5),
        "u_tab": nrm(ks[20], (L, N_EXPERTS, D), D ** -0.5),
        "v_tab": nrm(ks[21], (L, N_EXPERTS, D), BETA),
        "ln2_g": 1.0 + nrm(ks[22], (L, D), 0.01),
        "ln2_b": nrm(ks[23], (L, D), 0.01),
    }

def reference(x_prompt, x_sample, cache_ckv, cache_krope, c, c_ctx, w_mod, b_mod, w_in, w_s, b_s,
              g_q, w_qb, g_kv, w_kvb, w_o, ln1_g, ln1_b, w_pq, sub_keys, u_tab, v_tab, ln2_g, ln2_b):
    y_p = x_prompt
    new_ckv_list, new_krope_list = [], []
    for l in range(DEPTH):
        mod_ctx = (jax.nn.silu(c_ctx)[None, :] @ w_mod[l] + b_mod[l]).reshape(1, 6, D_MODEL)
        y_p, ckv_l, kr_l = trunk_layer(
            y_p, mod_ctx, None, None, False, w_in[l], w_s[l], b_s[l], g_q[l], w_qb[l], g_kv[l],
            w_kvb[l], w_o[l], ln1_g[l], ln1_b[l], w_pq[l], sub_keys[l], u_tab[l], v_tab[l],
            ln2_g[l], ln2_b[l])
        new_ckv_list.append(ckv_l)
        new_krope_list.append(kr_l)
    new_ckv = jnp.stack(new_ckv_list, axis=1)
    new_krope = jnp.stack(new_krope_list, axis=1)

    y_s = x_sample
    for l in range(DEPTH):
        mod_lat = (jax.nn.silu(c) @ w_mod[l] + b_mod[l]).reshape(c.shape[0], 6, D_MODEL)
        y_s, _, _ = trunk_layer(
            y_s, mod_lat, cache_ckv[:, l], cache_krope[:, l], True, w_in[l], w_s[l], b_s[l], g_q[l],
            w_qb[l], g_kv[l], w_kvb[l], w_o[l], ln1_g[l], ln1_b[l], w_pq[l], sub_keys[l], u_tab[l],
            v_tab[l], ln2_g[l], ln2_b[l])
    return (y_p, y_s, new_ckv, new_krope)


_drawn_inputs = setup_inputs


def setup_inputs(seed=0):
    import zlib

    import numpy as np

    out = dict(_drawn_inputs(seed))
    spreads = {}
    factors = {'cache_ckv': 4.936,
     'cache_krope': 6.761,
     'b_s': 6.266,
     'g_q': 8.0,
     'g_kv': 5.393,
     'ln2_g': 5.634,
     'ln2_b': 5.816}
    for name, (base, spread) in spreads.items():
        noise = np.random.default_rng([zlib.crc32(name.encode()), seed]).standard_normal(out[name].shape)
        drawn = base * np.exp(spread * noise) if base else spread * noise
        out[name] = __import__('jax').numpy.asarray(drawn.astype(out[name].dtype))
    for name, factor in factors.items():
        out[name] = (out[name] * factor).astype(out[name].dtype)
    return out
```

```python
import math
from contextlib import ExitStack

import numpy as np

import concourse.bass as bass
from concourse import mybir

F32 = mybir.dt.float32
F32R = mybir.dt.float32r
U32 = mybir.dt.uint32
ALU = mybir.AluOpType
ACT = mybir.ActivationFunctionType
AX = mybir.AxisListType

P = 128
D = 1024
DK = D // P
SEQ, DEC, PAST = 128, 1024, 128
T = SEQ + DEC
NT = T // P
G, GD = 4, 128
AW = G * GD
H, NOPE, ROPE, VD = 4, 128, 64, 128
QR, KVR = 384, 256
QK, KK = QR // P, KVR // P
IN_COLS = 2 * AW + QR + KVR + ROPE
Z = ((0, AW), (AW, AW), (2 * AW, QR), (2 * AW + QR, KVR + ROPE))
KT = NT + 1
NKS = (KT - 1) * P
CW = 384
SCALE = 1.0 / math.sqrt(NOPE + ROPE)
PH, NKEY, TOPK = 8, 128, 16
HS = 2 * PH
PAIRS = PH * TOPK
NE = NKEY * NKEY
ALPHA = 2.0 ** 0.25
EPS = 1e-6
GRID_W = 64
LOW = -3.0e38
CT = CW // P
NC = T // CW
TB = 64
NTB = T // TB
CB = CW // TB
UB = 4


class Count:

    def __init__(self, eng, sem):
        self.eng, self.sem, self.n = eng, sem, 0
        eng.sem_inc(sem, 1)
        eng.sem_clear(sem)

    def step(self, ins):
        self.n += 1
        ins.then_inc(self.sem, 1)
        self.eng.wait_ge(self.sem, self.n)


def build(nc, a):
    es = ExitStack()
    used = set()

    def sb(stack, name, shape, dt=F32):
        return stack.enter_context(nc.sbuf_tensor(name, shape, dt))

    def sem(name):
        assert name not in used
        used.add(name)
        return es.enter_context(nc.semaphore(name))

    with es:
        x1_dram = nc.dram_tensor("x1_scratch", [T, D], F32, kind="Internal").ap()
        g_dram = nc.dram_tensor("g_scratch", [NTB, P, NKEY, TB], F32, kind="Internal").ap()
        PS = [es.enter_context(nc.psum_tensor(f"bank{b}", [P, 512], F32)) for b in range(8)]
        ident = sb(es, "ident", [P, P])
        modc = sb(es, "modc", [P, 6 * DK, 2])
        sp1 = sb(es, "sp1", [P, 2, DK, 2])
        big = sb(es, "big", [P, KT * H * P * 2])
        kT = big[:, 0:KT * H * P].rearrange("p (h k) -> p h k", h=H)
        vv = big[:, KT * H * P:2 * KT * H * P].rearrange("p (t c) -> p t c", t=KT)
        h2T = big[:, 0:DK * T].rearrange("p (k t) -> p k t", k=DK)
        modulation(nc, a, sb, sem, PS, ident, modc, sp1)
        with ExitStack() as mid:
            aoT = sb(mid, "aoT", [P, G, T])
            boT = sb(mid, "boT", [P, H, T])
            with ExitStack() as att:
                qT = sb(att, "qT", [P, H, T])
                qrT = sb(att, "qrT", [P, 2, T])
                krT = sb(att, "krT", [P, KT * P])
                mixer_inputs(nc, a, sb, sem, PS, ident, modc, sp1, aoT, qT, qrT, krT, kT, vv)
                attention(nc, a, sb, sem, PS, ident, boT, qT, qrT, krT, kT, vv)
            residual_one(nc, a, sb, sem, PS, ident, modc, sp1, aoT, boT, h2T, x1_dram)
        with ExitStack() as mid:
            idxT = sb(mid, "idxT", [P, 3, T])
            routing(nc, a, sb, sem, PS, ident, h2T, idxT)
            scatter(nc, a, sb, sem, PS, idxT, g_dram)
        experts(nc, a, sb, sem, PS, ident, modc, h2T, x1_dram, g_dram)


def modulation(nc, a, sb, sem, PS, ident, modc, sp1):
    NJ = 6 * DK
    NW = 4
    with ExitStack() as c:
        cond = sb(c, "cond", [P, DK, 2])
        silu = sb(c, "silu", [P, DK, 2])
        bmod = sb(c, "bmod", [P, NJ])
        wm = sb(c, "wm", [P, NW, DK, P])
        loaded = sem("m_loaded")
        w_in = [sem(f"m_w{i}") for i in range(NW)]
        w_used, silu_ready, made, id0, id1, mod_ready = (sem(f"m_{n}") for n in (
            "w_used", "silu", "made", "id0", "id1", "mod_ready"))
        with nc.Block() as block:
            @block.sync
            def _(sp):
                sp.dma_start(cond[:, :, :], a["cond"]).then_inc(loaded, 16)
                sp.dma_start(bmod[:, :], a["b_mod"]).then_inc(loaded, 16)
                with sp.Fori(0, NJ // NW) as j:
                    for s in range(NW):
                        sp.wait_ge(w_used, j * NW + s + 1)
                        sp.dma_start(wm[:, s, :, :], a["w_mod"][j * NW + s, :, :, :]).then_inc(w_in[s], 16)

            @block.gpsimd
            def _(pool):
                pool.memset(ident[:, :], 0.0).then_inc(id0, 1)
                pool.wait_ge(id0, 1)
                pool.affine_select(out=ident[:, :], in_=ident[:, :], compare_op=ALU.not_equal, fill=1.0,
                                   base=0, pattern=[[-1, P]], channel_multiplier=1).then_inc(id1, 1)
                pool.wait_ge(id1, 1)

            @block.scalar
            def _(act):
                act.wait_ge(loaded, 32)
                act.activation(silu[:, :, :], cond[:, :, :], ACT.Silu).then_inc(silu_ready, 1)

            @block.tensor
            def _(pe):
                pe.sem_inc(w_used, NW)
                pe.wait_ge(silu_ready, 1)
                out = PS[0][:, 0:2 * NJ].rearrange("p (j c) -> p j c", c=2)
                with pe.Fori(0, NJ // NW) as j:
                    for s in range(NW):
                        pe.wait_ge(w_in[s], (j + 1) * 16)
                        for k in range(DK):
                            mm = pe.matmul(out[:, j * NW + s, :], wm[:, s, k, :], silu[:, k, :],
                                           start=(k == 0), stop=(k == DK - 1))
                        mm.then_inc(w_used, 1)

            @block.vector
            def _(dve):
                dve.wait_ge(w_used, NJ + NW)
                bc = bmod[:, :].rearrange("p (j o) -> p j o", o=1).to_broadcast([P, NJ, 2])
                dve.tensor_tensor(modc[:, :, :], PS[0][:, 0:2 * NJ].rearrange("p (j c) -> p j c", c=2), bc,
                                  ALU.add).then_inc(made, 1)
                dve.wait_ge(made, 1)
                for n, at in enumerate((DK, 4 * DK)):
                    dve.tensor_scalar(sp1[:, n, :, :], modc[:, at:at + DK, :], 1.0, None,
                                      ALU.add).then_inc(mod_ready, 1)
                dve.wait_ge(mod_ready, 2)


def mixer_inputs(nc, a, sb, sem, PS, ident, modc, sp1, aoT, qT, qrT, krT, kT, vv):
    with ExitStack() as c:
        w_in = sb(c, "w_in", [P, DK, IN_COLS])
        w_s = sb(c, "w_s", [P, G, P])
        b_s = sb(c, "b_s", [P, G])
        g_q = sb(c, "g_q", [P, QK])
        g_kv = sb(c, "g_kv", [P, KVR])
        w_qn = sb(c, "w_qn", [P, QK, H * NOPE])
        w_qr = sb(c, "w_qr", [P, QK, H * ROPE])
        w_kn = sb(c, "w_kn", [P, KK, H * NOPE])
        w_v = sb(c, "w_v", [P, KK, H * VD])
        cckT = sb(c, "cckT", [P, KK, P])
        xt = sb(c, "xt", [P, DK, P])
        hT = sb(c, "hT", [P, DK, P])
        rot = sb(c, "rot", [P, 2, ROPE])
        u = sb(c, "u", [P, AW])
        vg = sb(c, "vg", [P, AW])
        vst = vg
        aout = u
        ql = sb(c, "ql", [P, QR])
        ckv = sb(c, "ckv", [P, KVR])
        kr = sb(c, "kr", [P, 2, ROPE])
        t1 = sb(c, "t1", [P, H * ROPE])
        t2 = sb(c, "t2", [P, H * ROPE])
        qr = sb(c, "qr", [P, H * ROPE])
        qlT = sb(c, "qlT", [P, QK, P])
        ckT = sb(c, "ckT", [P, KK, P])
        junk = sb(c, "junk", [P, QR])
        st = sb(c, "st", [P, G, 6])
        mv = sb(c, "mv", [P, G, 2])
        var = sb(c, "var", [P, G + 2])
        ssq = sb(c, "ssq", [P, 2])
        sd = sb(c, "sd", [P, G + 2])
        rs = sb(c, "rs", [P, G + 2])

        wl = sem("a_weights")
        xl, rl = sem("a_x"), sem("a_rot")
        h_ready, z_ready, z_used = sem("a_h"), sem("a_z"), sem("a_z_used")
        gelu_u, gelu_v, sq_q, sq_kv, sd_ready = (sem(f"a_{n}") for n in ("gu", "gv", "sqq", "sqkv", "sd"))
        chain, var_ready, v_std, lat_ready, gate_ready, mixed = (sem(f"a_{n}") for n in (
            "chain", "var", "vstd", "lat", "gate", "mixed"))
        trl, tra, trq, qlT_ready, ao_ev, q_ev, k_ev, v_ev, qr_ready, qr_ev = (sem(f"a_{n}") for n in (
            "trl", "tra", "trq", "qlT", "ao", "qev", "kev", "vev", "qr", "qrev"))
        q_mm, k_mm, v_mm, r_mm = sem("a_qmm"), sem("a_kmm"), sem("a_vmm"), sem("a_rmm")
        stored, kr_st = sem("a_stored"), sem("a_krst")
        kr_ev = sem("a_krev")
        nw = 12

        with nc.Block() as block:
            @block.sync
            def _(sp):
                for dst, src in ((w_in, "w_in"), (w_s, "w_s"), (w_qn, "w_qn"), (w_qr, "w_qr"),
                                 (w_kn, "w_kn"), (w_v, "w_v"), (cckT, "cckT")):
                    sp.dma_start(dst[:, :, :], a[src]).then_inc(wl, 16)
                for dst, src in ((b_s, "b_s"), (g_q, "g_q"), (g_kv, "g_kv")):
                    sp.dma_start(dst[:, :], a[src]).then_inc(wl, 16)
                for half in range(2):
                    sp.dma_start(krT[half * ROPE:(half + 1) * ROPE, P:2 * P], a["ckrT"]).then_inc(wl, 16)
                with sp.Fori(0, NT) as i:
                    sp.wait_ge(h_ready, i)
                    sp.dma_start(xt[:, :, :], a["xT"][i, :, :, :]).then_inc(xl, 16)
                    sp.wait_ge(qr_ready, i)
                    sp.dma_start(rot[:, :, :], a["rot"][i, :, :, :]).then_inc(rl, 16)
                sp.wait_ge(stored, 16)
                sp.wait_ge(kr_st, 16)

            def mod_h(dve, i, m, ch):
                dve.wait_ge(xl, (i + 1) * 16)
                for k in range(DK):
                    ins = dve.tensor_scalar(hT[:, k, :], xt[:, k, :], sp1[:, 0, k, m:m + 1], modc[:, k, m:m + 1],
                                            ALU.mult, ALU.add)
                ins.then_inc(h_ready, 1)

            def dve_tile(dve, i, m):
                ch = Count(dve, chain)
                dve.wait_ge(z_ready, i * 4 + 4)
                dve.wait_ge(gelu_v, i + 1)
                for g in range(G):
                    ins = dve.bn_stats(st[:, g, :], vg[:, g * GD:(g + 1) * GD])
                ch.step(ins)
                for g in range(G):
                    ins = dve.bn_aggr(mv[:, g, :], st[:, g, :])
                ch.step(ins)
                dve.tensor_scalar(var[:, 0:G], mv[:, :, 1], EPS, None, ALU.add)
                dve.wait_ge(sq_kv, i + 1)
                dve.tensor_scalar(var[:, G:G + 1], ssq[:, 0:1], 1.0 / QR, EPS, ALU.mult, ALU.add)
                dve.tensor_scalar(var[:, G + 1:G + 2], ssq[:, 1:2], 1.0 / KVR, EPS, ALU.mult,
                                  ALU.add).then_inc(var_ready, 1)
                dve.wait_ge(sd_ready, i + 1)
                ch.step(dve.reciprocal(rs[:, :], sd[:, :]))
                for g in range(G):
                    part = vg[:, g * GD:(g + 1) * GD]
                    ins = dve.tensor_scalar(part, part, mv[:, g, 0:1], rs[:, g:g + 1], ALU.subtract, ALU.mult)
                ins.then_inc(v_std, 1)
                dve.tensor_scalar(ql[:, :], PS[2][:, 0:QR], rs[:, G:G + 1], None, ALU.mult)
                if m == 0:
                    dve.wait_ge(rl, 16)
                    for half in range(2):
                        ins = dve.tensor_copy(kr[:, half, :], PS[3][:, KVR:KVR + ROPE])
                else:
                    dve.wait_ge(rl, (i + 1) * 16)
                    ps = PS[3][:, KVR:KVR + ROPE]
                    dve.tensor_tensor(t1[:, 0:ROPE], ps, rot[:, 0, :], ALU.mult)
                    ch.step(rotate(dve, t2, ps, 1))
                    for half in range(2):
                        ins = dve.tensor_tensor(kr[:, half, :], t1[:, 0:ROPE], t2[:, 0:ROPE], ALU.add)
                dve.scalar_tensor_tensor(ckv[:, :], PS[3][:, 0:KVR], rs[:, G + 1:G + 2], g_kv[:, :],
                                         ALU.mult, ALU.mult).then_inc(lat_ready, 1)
                dve.wait_ge(mixed, i + 1)
                dve.wait_ge(gelu_u, i + 1)
                for g in range(G):
                    sl = slice(g * GD, (g + 1) * GD)
                    ins = dve.scalar_tensor_tensor(aout[:, sl], PS[4][:, sl], b_s[:, g:g + 1], u[:, sl],
                                                   ALU.add, ALU.mult)
                ins.then_inc(gate_ready, 1)
                dve.wait_ge(trl, i + 1)
                for k in range(QK):
                    dve.tensor_scalar(qlT[:, k, :], PS[6][:, k * P:(k + 1) * P], g_q[:, k:k + 1], None, ALU.mult)
                dve.tensor_copy(ckT[:, :, :], PS[7][:, 0:KK * P].rearrange("p (k t) -> p k t", k=KK))
                dst = krT[:, 0:P] if m == 0 else krT[:, bass.ds(i * P + P, P)]
                dve.tensor_copy(dst, PS[6][:, QK * P:(QK + 1) * P]).then_inc(qlT_ready, 1)
                dve.wait_ge(r_mm, i + 1)
                ps = PS[7][:, 0:H * ROPE]
                if m == 0:
                    dve.tensor_copy(qr[:, :], ps).then_inc(qr_ready, 1)
                else:
                    cosb = rot[:, 0:1, :].to_broadcast([P, H, ROPE])
                    dve.tensor_tensor(t1[:, :].rearrange("p (h r) -> p h r", h=H),
                                      ps.rearrange("p (h r) -> p h r", h=H), cosb, ALU.mult)
                    ch.step(rotate(dve, t2, ps, H))
                    dve.tensor_tensor(qr[:, :], t1[:, :], t2[:, :], ALU.add).then_inc(qr_ready, 1)

            def rotate(dve, out, ps, heads):
                for half in range(2):
                    for part in range(heads):
                        o = out[:, part * ROPE:(part + 1) * ROPE].rearrange("p (a b f) -> p a b f", a=2, b=2)
                        s = ps[:, part * ROPE:(part + 1) * ROPE].rearrange("p (a b f) -> p a b f", a=2, b=2)
                        w = rot[:, 1, :].rearrange("p (a b f) -> p a b f", a=2, b=2)
                        ins = dve.tensor_tensor(o[:, :, half, :], s[:, :, 1 - half, :], w[:, :, half, :], ALU.mult)
                return ins

            @block.vector
            def _(dve):
                dve.wait_ge(wl, nw * 16)
                mod_h(dve, 0, 0, None)
                dve_tile(dve, 0, 0)
                with dve.Fori(1, NT) as i:
                    mod_h(dve, i, 1, None)
                    dve_tile(dve, i, 1)

            def act_tile(act, i, first):
                act.wait_ge(z_ready, i * 4 + 1)
                act.wait_ge(tra, i)
                act.activation(u[:, :], PS[0][:, :], ACT.Gelu).then_inc(gelu_u, 1)
                act.wait_ge(z_ready, i * 4 + 2)
                act.wait_ge(mixed, i)
                act.activation(vg[:, :], PS[1][:, :], ACT.Gelu).then_inc(gelu_v, 1)
                act.wait_ge(z_ready, i * 4 + 3)
                act.activation(junk[:, 0:QR], PS[2][:, 0:QR], ACT.Square, accum_out=ssq[:, 0:1]).then_inc(sq_q, 1)
                act.wait_ge(z_ready, i * 4 + 4)
                act.wait_ge(sq_q, i + 1)
                act.activation(junk[:, 0:KVR], PS[3][:, 0:KVR], ACT.Square,
                               accum_out=ssq[:, 1:2]).then_inc(sq_kv, 1)
                act.wait_ge(var_ready, i + 1)
                act.activation(sd[:, :], var[:, :], ACT.Sqrt).then_inc(sd_ready, 1)
                key = 0 if first else i * P + P
                act.wait_ge(tra, i + 1)
                act.activation(aoT[:, :, bass.ds(i * P, P)], PS[5][:, :].rearrange("p (g t) -> p g t", g=G),
                               ACT.Copy).then_inc(ao_ev, 1)
                act.wait_ge(q_mm, i + 1)
                act.activation(qT[:, :, bass.ds(i * P, P)], PS[4][:, :].rearrange("p (h t) -> p h t", h=H),
                               ACT.Copy).then_inc(q_ev, 1)
                act.wait_ge(k_mm, i + 2)
                act.activation(kT[:, :, bass.ds(key, P)], PS[5][:, :].rearrange("p (h t) -> p h t", h=H),
                               ACT.Copy).then_inc(k_ev, 1)
                act.wait_ge(v_mm, i + 2)
                row = 0 if first else i + 1
                act.activation(vv[:, row, :], PS[6][:, :], ACT.Copy).then_inc(v_ev, 1)
                act.wait_ge(trq, i + 1)
                act.activation(qrT[:, :, bass.ds(i * P, P)], PS[4][:, 0:2 * P].rearrange("p (h t) -> p h t", h=2),
                               ACT.Copy).then_inc(qr_ev, 1)

            @block.scalar
            def _(act):
                act.wait_ge(k_mm, 1)
                act.activation(kT[:, :, P:2 * P], PS[5][:, :].rearrange("p (h t) -> p h t", h=H),
                               ACT.Copy).then_inc(k_ev, 1)
                act.wait_ge(v_mm, 1)
                act.activation(vv[:, 1, :], PS[6][:, :], ACT.Copy).then_inc(v_ev, 1)
                act_tile(act, 0, True)
                act.wait_ge(lat_ready, 1)
                act.dma_start(a["new_ckv"], ckv[:, :]).then_inc(stored, 16)
                act.dma_start(a["new_krope"], kr[:, 0, :]).then_inc(kr_st, 16)
                act.wait_ge(stored, 16)
                act.wait_ge(kr_st, 16)
                with act.Fori(1, NT) as i:
                    act_tile(act, i, False)

            def keys_values(pe, ckT_):
                for h in range(H):
                    for k in range(KK):
                        mm = pe.matmul(PS[5][:, h * P:(h + 1) * P], w_kn[:, k, h * NOPE:(h + 1) * NOPE],
                                       ckT_[:, k, :], start=(k == 0), stop=(k == KK - 1))
                mm.then_inc(k_mm, 1)

            def values(pe, ckT_):
                for k in range(KK):
                    mm = pe.matmul(PS[6][:, :], ckT_[:, k, :], w_v[:, k, :], start=(k == 0), stop=(k == KK - 1))
                mm.then_inc(v_mm, 1)

            def pe_tile(pe, i):
                pe.wait_ge(h_ready, i + 1)
                for n, (at, w) in enumerate(Z):
                    if n == 0:
                        pe.wait_ge(gelu_u, i)
                    elif n == 1:
                        pe.wait_ge(gelu_v, i)
                    else:
                        pe.wait_ge(lat_ready, i)
                    for k in range(DK):
                        mm = pe.matmul(PS[n][:, 0:w], hT[:, k, :], w_in[:, k, at:at + w],
                                       start=(k == 0), stop=(k == DK - 1))
                    mm.then_inc(z_ready, 1)
                pe.wait_ge(v_std, i + 1)
                pe.wait_ge(qr_ev, i)
                for g in range(G):
                    mm = pe.matmul(PS[4][:, g * GD:(g + 1) * GD], w_s[:, g, :], vst[:, g * GD:(g + 1) * GD],
                                   start=True, stop=True)
                mm.then_inc(mixed, 1)
                pe.wait_ge(lat_ready, i + 1)
                pe.wait_ge(v_ev, i + 1)
                for k in range(QK):
                    pe.transpose(PS[6][:, k * P:(k + 1) * P], ql[:, k * P:(k + 1) * P], ident[:, :])
                pe.transpose(PS[6][:, QK * P:(QK + 1) * P], kr[:, :, :].rearrange("p a r -> p (a r)"), ident[:, :])
                pe.wait_ge(qr_ready, i)
                for k in range(KK):
                    mm = pe.transpose(PS[7][:, k * P:(k + 1) * P], ckv[:, k * P:(k + 1) * P], ident[:, :])
                mm.then_inc(trl, 1)
                pe.wait_ge(gate_ready, i + 1)
                pe.wait_ge(k_ev, i + 1)
                for g in range(G):
                    mm = pe.transpose(PS[5][:, g * P:(g + 1) * P], aout[:, g * GD:(g + 1) * GD], ident[:, :])
                mm.then_inc(tra, 1)
                pe.wait_ge(qlT_ready, i + 1)
                for h in range(H):
                    for k in range(QK):
                        mm = pe.matmul(PS[4][:, h * P:(h + 1) * P], w_qn[:, k, h * NOPE:(h + 1) * NOPE],
                                       qlT[:, k, :], start=(k == 0), stop=(k == QK - 1))
                mm.then_inc(q_mm, 1)
                for k in range(QK):
                    mm = pe.matmul(PS[7][:, 0:H * ROPE], qlT[:, k, :], w_qr[:, k, :],
                                   start=(k == 0), stop=(k == QK - 1))
                mm.then_inc(r_mm, 1)
                pe.wait_ge(ao_ev, i + 1)
                keys_values(pe, ckT)
                values(pe, ckT)
                pe.wait_ge(qr_ready, i + 1)
                pe.wait_ge(q_ev, i + 1)
                for pair in range(2):
                    mm = pe.transpose(PS[4][:, pair * P:(pair + 1) * P], qr[:, pair * P:(pair + 1) * P], ident[:, :])
                mm.then_inc(trq, 1)

            @block.tensor
            def _(pe):
                pe.wait_ge(wl, nw * 16)
                keys_values(pe, cckT)
                values(pe, cckT)
                pe_tile(pe, 0)
                with pe.Fori(1, NT) as i:
                    pe_tile(pe, i)


def attention(nc, a, sb, sem, PS, ident, boT, qT, qrT, krT, kT, vv):
    with ExitStack() as c:
        qc = sb(c, "qc", [P, H, P])
        qrc = sb(c, "qrc", [P, 2, P])
        pr = sb(c, "pr", [P, 2, NKS])
        prT = sb(c, "prT", [P, NKS])
        mx = sb(c, "mx", [P, 2])
        nb = sb(c, "nb", [P, 2])
        sm = sb(c, "sm", [P, 2])
        ri = sb(c, "ri", [P, 2])
        q_ready, s_ready, m_ready, b_ready, e_ready, r_ready, p_ready, t_ready, tc1, tc2, o_ready, o_ev = (
            sem(f"b_{n}") for n in ("q", "s", "m", "b", "e", "r", "p", "t", "tc1", "tc2", "o", "oev"))

        with nc.Block() as block:
            def chunks(n):
                return [(b, min(CW, n - b * CW)) for b in range((n + CW - 1) // CW)]

            def scores(pe, h, n, first, nkeys, key0):
                pe.wait_ge(e_ready, n)
                half = (h % 2) * ROPE
                for b, w in chunks(nkeys):
                    ks = slice(key0 + b * CW, key0 + b * CW + w)
                    pe.matmul(PS[b][:, 0:w], qc[:, h, :], kT[:, h, ks], start=True, stop=False)
                    mm = pe.matmul(PS[b][:, 0:w], qrc[half:half + ROPE, h // 2, :], krT[half:half + ROPE, ks],
                                   start=False, stop=True)
                mm.then_inc(s_ready, 1)

            def outputs(pe, h, n, nkeys, kt0):
                nk = nkeys // P
                pe.wait_ge(p_ready, n + 1)
                pe.wait_ge(tc1, n)
                pe.wait_ge(tc2, n)
                for k in range(nk):
                    mm = pe.transpose(PS[3 + k // 4][:, (k % 4) * P:(k % 4 + 1) * P],
                                      pr[:, h % 2, k * P:(k + 1) * P], ident[:, :])
                mm.then_inc(t_ready, 1)
                pe.wait_ge(o_ev, n)
                pe.wait_ge(tc1, n + 1)
                pe.wait_ge(tc2, n + 1)
                for k in range(nk):
                    mm = pe.matmul(PS[6][:, 0:P], vv[:, kt0 + k, h * VD:(h + 1) * VD], prT[:, k * P:(k + 1) * P],
                                   start=(k == 0), stop=(k == nk - 1))
                mm.then_inc(o_ready, 1)

            def pe_tile(pe, i, nkeys, key0):
                pe.wait_ge(q_ready, i + 1)
                scores(pe, 0, i * H, False, nkeys, key0)
                for h in range(1, H):
                    scores(pe, h, i * H + h, False, nkeys, key0)
                    outputs(pe, h - 1, i * H + h - 1, nkeys, key0 // P)
                outputs(pe, H - 1, i * H + H - 1, nkeys, key0 // P)

            @block.tensor
            def _(pe):
                pe_tile(pe, 0, P, 0)
                with pe.Fori(1, NT) as i:
                    pe_tile(pe, i, NKS, P)

            def dve_tile(dve, i, nkeys):
                dve.wait_ge(s_ready, i * H)
                dve.tensor_copy(qc[:, :, :], qT[:, :, bass.ds(i * P, P)])
                dve.tensor_copy(qrc[:, :, :], qrT[:, :, bass.ds(i * P, P)]).then_inc(q_ready, 1)
                nb_ = (nkeys + CW - 1) // CW
                for h in range(H):
                    n, s = i * H + h, h % 2
                    dve.wait_ge(s_ready, n + 1)
                    for b in range(nb_):
                        ins = dve.reduce_max(part[:, b:b + 1], PS[b][:, 0:min(CW, nkeys)], AX.X)
                    ins.then_inc(m_ready, 1)
                    dve.wait_ge(m_ready, 2 * n + 1)
                    dve.reduce_max(mx[:, s:s + 1], part[:, 0:nb_], AX.X).then_inc(m_ready, 1)
                    dve.wait_ge(m_ready, 2 * n + 2)
                    dve.tensor_scalar(nb[:, s:s + 1], mx[:, s:s + 1], -SCALE, None, ALU.mult).then_inc(b_ready, 1)
                    dve.wait_ge(e_ready, n + 1)
                    dve.reduce_sum(sm[:, s:s + 1], es_[:, s, 0:nb_], AX.X).then_inc(r_ready, 1)
                    dve.wait_ge(r_ready, 2 * n + 1)
                    dve.reciprocal(ri[:, s:s + 1], sm[:, s:s + 1]).then_inc(r_ready, 1)
                    dve.wait_ge(r_ready, 2 * n + 2)
                    dve.tensor_scalar(pr[:, s, 0:nkeys], pr[:, s, 0:nkeys], ri[:, s:s + 1], None,
                                      ALU.mult).then_inc(p_ready, 1)
                    dve.wait_ge(t_ready, n + 1)
                    w = min(nkeys, 4 * P)
                    dve.wait_ge(o_ready, n)
                    ins = dve.tensor_copy(prT[:, 0:w], PS[3][:, 0:w])
                    if nkeys > 8 * P:
                        ins = dve.tensor_copy(prT[:, 8 * P:nkeys], PS[5][:, 0:nkeys - 8 * P])
                    ins.then_inc(tc1, 1)

            part = sb(c, "part", [P, 3])
            es_ = sb(c, "es", [P, 2, 3])

            @block.vector
            def _(dve):
                dve_tile(dve, 0, P)
                with dve.Fori(1, NT) as i:
                    dve_tile(dve, i, NKS)

            def act_tile(act, i, nkeys):
                for h in range(H):
                    n, s = i * H + h, h % 2
                    act.wait_ge(b_ready, n + 1)
                    act.wait_ge(t_ready, n - 1 if h else n)
                    for b in range((nkeys + CW - 1) // CW):
                        w = min(CW, nkeys)
                        ins = act.activation(pr[:, s, b * w:(b + 1) * w], PS[b][:, 0:w], ACT.Exp, bias=nb[:, s:s + 1],
                                             scale=SCALE, accum_out=es_[:, s, b:b + 1])
                    ins.then_inc(e_ready, 1)
                    act.wait_ge(t_ready, n + 1)
                    act.wait_ge(o_ready, n)
                    if nkeys > 4 * P:
                        act.activation(prT[:, 4 * P:8 * P], PS[4][:, :], ACT.Copy).then_inc(tc2, 1)
                    else:
                        act.sem_inc(tc2, 1)
                    act.wait_ge(o_ready, n + 1)
                    act.activation(boT[:, h, bass.ds(i * P, P)], PS[6][:, 0:P], ACT.Copy).then_inc(o_ev, 1)

            @block.scalar
            def _(act):
                act_tile(act, 0, P)
                with act.Fori(1, NT) as i:
                    act_tile(act, i, NKS)


def residual_one(nc, a, sb, sem, PS, ident, modc, sp1, aoT, boT, h2T, x1_dram):
    with ExitStack() as c:
        w_o = sb(c, "w_o", [P, DK, D])
        ln_g = sb(c, "ln1_g", [P, D])
        ln_b = sb(c, "ln1_b", [P, D])
        gate = sb(c, "gate1", [P, 2, D])
        gcol = sb(c, "gcol1", [P, 2, P])
        ones = sb(c, "ones1", [P, P])
        mc = sb(c, "mc", [P, DK, P])
        xt = sb(c, "xr", [P, D])
        r = sb(c, "r1", [P, D])
        y = sb(c, "y1", [P, D])
        x1 = sb(c, "x1", [P, D])
        st = sb(c, "st1", [P, 2, 6])
        mv = sb(c, "mv1", [P, 2])
        ve = sb(c, "ve1", [P, 1])
        sd = sb(c, "sd1", [P, 1])
        rs = sb(c, "rs1", [P, 1])
        wl, xl, ones_ready, g_col, g_mm, g_ev = (sem(f"c_{n}") for n in ("w", "x", "ones", "gcol", "gmm", "gev"))
        m_ready, mm_ready, xa_ready, ve_ready, sd_ready, chain, x1_ready, tr_ready, h_ev, st1, bank_read = (
            sem(f"c_{n}") for n in ("m", "mm", "xa", "ve", "sd", "chain", "x1", "tr", "hev", "st", "bank"))
        with nc.Block() as block:
            @block.sync
            def _(sp):
                sp.dma_start(w_o[:, :, :], a["w_o"]).then_inc(wl, 16)
                sp.dma_start(ln_g[:, :], a["ln1_g"]).then_inc(wl, 16)
                sp.dma_start(ln_b[:, :], a["ln1_b"]).then_inc(wl, 16)
                with sp.Fori(0, NT) as i:
                    sp.wait_ge(xa_ready, i)
                    sp.dma_start(xt[:, :], a["x"][bass.ds(i * P, P), :]).then_inc(xl, 16)
                    sp.wait_ge(x1_ready, i + 1)
                    sp.dma_start(x1_dram[bass.ds(i * P, P), :], x1[:, :]).then_inc(st1, 16)
                sp.wait_ge(st1, NT * 16)

            @block.gpsimd
            def _(pool):
                pool.memset(ones[:, :], 1.0).then_inc(ones_ready, 1)

            gate_rows_engines = gate_rows(2 * DK, gate, gcol, ones, modc, ident, PS, g_col, g_mm, g_ev)

            @block.tensor
            def _(pe):
                gate_rows_engines[0](pe)
                pe.wait_ge(wl, 48)
                with pe.Fori(0, NT) as i:
                    pe.wait_ge(m_ready, i + 1)
                    pe.wait_ge(bank_read, i)
                    for n in range(2):
                        for k in range(DK):
                            mm = pe.matmul(PS[n][:, :], mc[:, k, :], w_o[:, k, n * 512:(n + 1) * 512],
                                           start=(k == 0), stop=(k == DK - 1))
                    mm.then_inc(mm_ready, 1)
                    pe.wait_ge(x1_ready, i + 1)
                    pe.wait_ge(h_ev, i)
                    for k in range(DK):
                        mm = pe.transpose(PS[2 + k // 4][:, (k % 4) * P:(k % 4 + 1) * P], x1[:, k * P:(k + 1) * P],
                                          ident[:, :])
                    mm.then_inc(tr_ready, 1)

            def act_tile(act, i, m):
                act.wait_ge(ve_ready, i + 1)
                act.activation(sd[:, :], ve[:, :], ACT.Sqrt).then_inc(sd_ready, 1)
                act.wait_ge(tr_ready, i + 1)
                for k in range(DK):
                    ins = act.activation(h2T[:, k, bass.ds(i * P, P)], PS[2 + k // 4][:, (k % 4) * P:(k % 4 + 1) * P],
                                         ACT.Identity, bias=modc[:, 3 * DK + k, m:m + 1],
                                         scale=sp1[:, 1, k, m:m + 1])
                ins.then_inc(h_ev, 1)

            @block.scalar
            def _(act):
                gate_rows_engines[1](act)
                act_tile(act, 0, 0)
                with act.Fori(1, NT) as i:
                    act_tile(act, i, 1)

            def dve_tile(dve, i, m):
                ch = Count(dve, chain)
                dve.wait_ge(mm_ready, i)
                dve.tensor_copy(mc[:, 0:G, :], aoT[:, :, bass.ds(i * P, P)])
                dve.tensor_copy(mc[:, G:DK, :], boT[:, :, bass.ds(i * P, P)]).then_inc(m_ready, 1)
                dve.wait_ge(mm_ready, i + 1)
                for n in range(2):
                    sl = slice(n * 512, (n + 1) * 512)
                    ins = dve.tensor_tensor(r[:, sl], gate[:, m, sl], PS[n][:, :], ALU.mult)
                ins.then_inc(bank_read, 1)
                dve.wait_ge(bank_read, i + 1)
                dve.wait_ge(xl, (i + 1) * 16)
                dve.scalar_tensor_tensor(y[:, :], xt[:, :], ALPHA, r[:, :], ALU.mult, ALU.add).then_inc(xa_ready, 1)
                dve.wait_ge(xa_ready, i + 1)
                for n in range(2):
                    ins = dve.bn_stats(st[:, n, :], y[:, n * 512:(n + 1) * 512])
                ch.step(ins)
                ch.step(dve.bn_aggr(mv[:, :], st[:, :, :].rearrange("p a b -> p (a b)")))
                dve.tensor_scalar(ve[:, :], mv[:, 1:2], EPS, None, ALU.add).then_inc(ve_ready, 1)
                dve.wait_ge(sd_ready, i + 1)
                ch.step(dve.reciprocal(rs[:, :], sd[:, :]))
                ch.step(dve.tensor_scalar(r[:, :], y[:, :], mv[:, 0:1], rs[:, 0:1], ALU.subtract, ALU.mult))
                ch.step(dve.tensor_tensor(y[:, :], r[:, :], ln_g[:, :], ALU.mult))
                dve.wait_ge(tr_ready, i)
                dve.wait_ge(st1, i * 16)
                dve.tensor_tensor(x1[:, :], y[:, :], ln_b[:, :], ALU.add).then_inc(x1_ready, 1)
                dve.wait_ge(x1_ready, i + 1)

            @block.vector
            def _(dve):
                dve.wait_ge(ones_ready, 1)
                gate_rows_engines[2](dve)
                dve.wait_ge(wl, 48)
                dve_tile(dve, 0, 0)
                with dve.Fori(1, NT) as i:
                    dve_tile(dve, i, 1)


def gate_rows(at, gate, gcol, ones, modc, ident, PS, g_col, g_mm, g_ev):
    def pe_part(pe):
        for n in range(2 * DK):
            m, k = divmod(n, DK)
            pe.wait_ge(g_col, n + 1)
            if n % 4 == 0 and n >= 4:
                pe.wait_ge(g_ev, n // 4)
            pe.matmul(PS[7][:, (n % 4) * P:(n % 4 + 1) * P], gcol[:, n % 2, :], ident[:, :],
                      start=True, stop=True).then_inc(g_mm, 1)

    def act_part(act):
        for q in range(2 * DK // 4):
            act.wait_ge(g_mm, 4 * q + 4)
            m, half = divmod(q, 2)
            act.activation(gate[:, m, half * 512:(half + 1) * 512], PS[7][:, :], ACT.Copy).then_inc(g_ev, 1)

    def dve_part(dve):
        for n in range(2 * DK):
            m, k = divmod(n, DK)
            if n >= 2:
                dve.wait_ge(g_mm, n - 1)
            dve.tensor_scalar(gcol[:, n % 2, :], ones[:, :], modc[:, at + k, m:m + 1], None,
                              ALU.mult).then_inc(g_col, 1)
        dve.wait_ge(g_ev, 4)

    return pe_part, act_part, dve_part


def routing(nc, a, sb, sem, PS, ident, h2T, idxT):
    with ExitStack() as c:
        w_pq = sb(c, "w_pq", [P, DK, HS * P])
        keys = sb(c, "keys", [P, HS, NKEY])
        qs = sb(c, "qs", [P, 2, CW])
        s = sb(c, "s", [P, HS, CT, NKEY])
        top = sb(c, "top", [P, HS, TOPK])
        it = sb(c, "it", [P, HS, TOPK], U32)
        itf = sb(c, "itf", [P, HS, TOPK])
        cand = sb(c, "cand", [P, PH, TOPK * TOPK])
        fs = sb(c, "fs", [P, PH, TOPK])
        fp = sb(c, "fp", [P, PH, TOPK], U32)
        ab = sb(c, "ab", [P, 2, PAIRS], U32)
        abf = sb(c, "abf", [P, 2, PAIRS])
        eq = sb(c, "eq", [P, PAIRS, TOPK])
        i16 = sb(c, "i16", [P, TOPK])
        out = sb(c, "out", [P, 3, PAIRS])
        ex = sb(c, "ex", [P, PH, TOPK])
        sm = sb(c, "smr", [P, PH])
        ri = sb(c, "rir", [P, PH])
        wl, i_ready, q_mm, q_ev, s_mm, s_ev, s_used, chain, e_in, e_out, o_ready, tr, tr_ev = (sem(f"d_{n}") for n in (
            "w", "i", "qmm", "qev", "smm", "sev", "sused", "chain", "ein", "eout", "o", "tr", "trev"))

        with nc.Block() as block:
            @block.sync
            def _(sp):
                sp.dma_start(w_pq[:, :, :], a["w_pq"]).then_inc(wl, 16)
                sp.dma_start(keys[:, :, :], a["keys"]).then_inc(wl, 16)

            @block.gpsimd
            def _(pool):
                pool.iota(i16[:, :], pattern=[[1, TOPK]], base=0, channel_multiplier=0,
                          allow_small_or_imprecise_dtypes=True).then_inc(i_ready, 1)

            @block.tensor
            def _(pe):
                pe.wait_ge(wl, 32)
                with pe.Fori(0, NC) as n:
                    for l in range(HS + 1):
                        if l < HS:
                            pe.wait_ge(q_ev, n * HS + max(l - 1, 0))
                            for k in range(DK):
                                mm = pe.matmul(PS[l % 2][:, 0:CW], w_pq[:, k, l * P:(l + 1) * P],
                                               h2T[:, k, bass.ds(n * CW, CW)], start=(k == 0), stop=(k == DK - 1))
                            mm.then_inc(q_mm, 1)
                        if l >= 1:
                            j = l - 1
                            pe.wait_ge(q_ev, n * HS + j + 1)
                            pe.wait_ge(s_ev, n * HS + max(j - 1, 0))
                            for t in range(CT):
                                mm = pe.matmul(PS[2 + j % 2][:, t * NKEY:(t + 1) * NKEY],
                                               qs[:, j % 2, t * P:(t + 1) * P], keys[:, j, :], start=True, stop=True)
                            mm.then_inc(s_mm, 1)
                    for t in range(CT):
                        pe.wait_ge(o_ready, n * CT + t + 1)
                        pe.wait_ge(tr_ev, n * CT + t)
                        for w in range(3):
                            mm = pe.transpose(PS[4][:, w * P:(w + 1) * P], out[:, w, :], ident[:, :])
                        mm.then_inc(tr, 1)

            @block.scalar
            def _(act):
                with act.Fori(0, NC) as n:
                    for l in range(HS + 1):
                        if l < HS:
                            act.wait_ge(q_mm, n * HS + l + 1)
                            if l >= 2:
                                act.wait_ge(s_mm, n * HS + l - 1)
                            act.activation(qs[:, l % 2, :], PS[l % 2][:, 0:CW], ACT.Copy).then_inc(q_ev, 1)
                        if l >= 1:
                            act.wait_ge(s_mm, n * HS + l)
                            act.wait_ge(s_used, n * CT)
                            act.activation(s[:, l - 1, :, :],
                                           PS[2 + (l - 1) % 2][:, 0:CT * NKEY].rearrange("p (t k) -> p t k", t=CT),
                                           ACT.Copy).then_inc(s_ev, 1)
                    for t in range(CT):
                        act.wait_ge(e_in, n * CT + t + 1)
                        act.activation(ex[:, :, :], fs[:, :, :], ACT.Exp).then_inc(e_out, 1)
                        act.wait_ge(tr, n * CT + t + 1)
                        act.activation(idxT[:, :, bass.ds(n * CW + t * P, P)],
                                       PS[4][:, 0:3 * P].rearrange("p (w t) -> p w t", w=3), ACT.Copy).then_inc(tr_ev, 1)

            @block.vector
            def _(dve):
                dve.wait_ge(i_ready, 1)
                with dve.Fori(0, NC) as n:
                    dve.wait_ge(s_ev, n * HS + HS)
                    for t in range(CT):
                        ch = Count(dve, chain)
                        for half in range(2):
                            sl = slice(half * 8, half * 8 + 8)
                            for l in range(HS):
                                ins = dve.max(top[:, l, sl], s[:, l, t, :])
                            ch.step(ins)
                            for l in range(HS):
                                ins = dve.max_index(it[:, l, sl], top[:, l, sl], s[:, l, t, :])
                            ch.step(ins)
                            if half == 0:
                                for l in range(HS):
                                    ins = dve.match_replace(s[:, l, t, :], top[:, l, sl], s[:, l, t, :], LOW)
                                ch.step(ins)
                        dve.sem_inc(s_used, 1)
                        tv = top[:, :, :].rearrange("p (h two) k -> p h two k", two=2)
                        for h in range(PH):
                            ins = dve.tensor_tensor(
                                cand[:, h, :].rearrange("p (a b) -> p a b", a=TOPK),
                                tv[:, h, 0, :].rearrange("p (a o) -> p a o", o=1).to_broadcast([P, TOPK, TOPK]),
                                tv[:, h, 1:2, :].to_broadcast([P, TOPK, TOPK]), ALU.add)
                        dve.tensor_copy(itf[:, :, :], it[:, :, :])
                        ch.step(ins)
                        for half in range(2):
                            sl = slice(half * 8, half * 8 + 8)
                            for h in range(PH):
                                ins = dve.max(fs[:, h, sl], cand[:, h, :])
                            ch.step(ins)
                            for h in range(PH):
                                ins = dve.max_index(fp[:, h, sl], fs[:, h, sl], cand[:, h, :])
                            ch.step(ins)
                            if half == 0:
                                for h in range(PH):
                                    ins = dve.match_replace(cand[:, h, :], fs[:, h, sl], cand[:, h, :], LOW)
                                ch.step(ins)
                        ch.step(dve.tensor_copy(sm[:, :], fs[:, :, 0]))
                        dve.tensor_tensor(fs[:, :, :], fs[:, :, :],
                                          sm[:, :].rearrange("p (h o) -> p h o", o=1).to_broadcast([P, PH, TOPK]),
                                          ALU.subtract).then_inc(e_in, 1)
                        fpf = fp[:, :, :].rearrange("p h k -> p (h k)")
                        dve.tensor_scalar(ab[:, 0, :], fpf, 4, None, ALU.logical_shift_right)
                        ch.step(dve.tensor_scalar(ab[:, 1, :], fpf, TOPK - 1, None, ALU.bitwise_and))
                        ch.step(dve.tensor_copy(abf[:, :, :], ab[:, :, :]))
                        dve.wait_ge(tr, n * CT + t)
                        iv = itf[:, :, :].rearrange("p (h two) k -> p h two k", two=2)
                        for w in range(2):
                            ch.step(dve.tensor_tensor(
                                eq[:, :, :], i16[:, :].rearrange("p (o k) -> p o k", o=1).to_broadcast([P, PAIRS, TOPK]),
                                abf[:, w, :].rearrange("p (q o) -> p q o", o=1).to_broadcast([P, PAIRS, TOPK]),
                                ALU.is_equal))
                            for h in range(PH):
                                part = eq[:, h * TOPK:(h + 1) * TOPK, :]
                                ins = dve.tensor_tensor(part, part, iv[:, h, w:w + 1, :].to_broadcast([P, TOPK, TOPK]),
                                                        ALU.mult)
                            ch.step(ins)
                            ch.step(dve.tensor_reduce(out[:, w, :], eq[:, :, :], axis=AX.X, op=ALU.add))
                        dve.wait_ge(e_out, n * CT + t + 1)
                        ch.step(dve.tensor_reduce(sm[:, :], ex[:, :, :], axis=AX.X, op=ALU.add))
                        ch.step(dve.reciprocal(ri[:, :], sm[:, :]))
                        dve.tensor_tensor(out[:, 2, :].rearrange("p (h k) -> p h k", h=PH), ex[:, :, :],
                                          ri[:, :].rearrange("p (h o) -> p h o", o=1).to_broadcast([P, PH, TOPK]),
                                          ALU.mult).then_inc(o_ready, 1)
                        dve.wait_ge(o_ready, n * CT + t + 1)


def scatter(nc, a, sb, sem, PS, idxT, g_dram):
    R = 4
    U = 2 * R
    with ExitStack() as c:
        iota = sb(c, "iota", [P, P])
        idc = sb(c, "idc", [P, 2, 3, U])
        ra = sb(c, "ra", [P, U, P])
        cb = sb(c, "cb", [P, U, P])
        stage = sb(c, "stage", [P, 2, NKEY, TB])
        i_ready, c_ready, hot, mm_done, ev, bank_free = (sem(f"e_{n}") for n in ("i", "c", "hot", "mm", "ev", "bf"))
        out = [sem(f"e_out{s}") for s in range(2)]
        STEPS = TB // U
        with nc.Block() as block:
            @block.gpsimd
            def _(pool):
                pool.iota(iota[:, :], pattern=[[1, P]], base=0, channel_multiplier=0,
                          allow_small_or_imprecise_dtypes=True).then_inc(i_ready, 1)

            @block.vector
            def _(dve):
                dve.wait_ge(i_ready, 1)
                with dve.Fori(0, T // U) as q:
                    dve.wait_ge(hot, q * 2)
                    dve.tensor_copy(idc[:, 0, :, :], idxT[:, :, bass.ds(q * U, U)]).then_inc(c_ready, 1)
                    dve.wait_ge(c_ready, q + 1)
                    for g in range(2):
                        dve.wait_ge(mm_done, q * 2 + g)
                        for t in range(g * R, (g + 1) * R):
                            dve.tensor_scalar(ra[:, t, :], iota[:, :], idc[:, 0, 0, t:t + 1], None, ALU.is_equal)
                            ins = dve.tensor_scalar(cb[:, t, :], iota[:, :], idc[:, 0, 1, t:t + 1],
                                                    idc[:, 0, 2, t:t + 1], ALU.is_equal, ALU.mult)
                        ins.then_inc(hot, 1)

            @block.tensor
            def _(pe):
                pe.sem_inc(mm_done, 1)
                with pe.Fori(0, T // U) as q:
                    for g in range(2):
                        pe.wait_ge(hot, q * 2 + g + 1)
                        pe.wait_ge(ev, q * 2 + g)
                        for t in range(R):
                            mm = pe.matmul(PS[g][:, t * P:(t + 1) * P], cb[:, g * R + t, :], ra[:, g * R + t, :],
                                           start=True, stop=True)
                        mm.then_inc(mm_done, 1)

            @block.scalar
            def _(act):
                act.sem_inc(ev, 1)
                with act.Fori(0, NTB // 2) as o:
                    for b in range(2):
                        act.wait_ge(out[b], o * 16)
                        with act.Fori(0, STEPS) as q:
                            for g in range(2):
                                act.wait_ge(mm_done, (o * 2 + b) * (2 * STEPS) + q * 2 + g + 2)
                                dst = stage[:, b, :, bass.ds(q * U + g * R, R)].rearrange("p i t -> p t i")
                                act.activation(dst, PS[g][:, :].rearrange("p (t i) -> p t i", t=R),
                                               ACT.Copy).then_inc(ev, 1)

            @block.sync
            def _(sp):
                with sp.Fori(0, NTB // 2) as o:
                    for b in range(2):
                        sp.wait_ge(ev, (o * 2 + b + 1) * (2 * STEPS) + 1)
                        sp.dma_start(g_dram[o * 2 + b, :, :, :], stage[:, b, :, :]).then_inc(out[b], 16)
                for b in range(2):
                    sp.wait_ge(out[b], NTB // 2 * 16)


def experts(nc, a, sb, sem, PS, ident, modc, h2T, x1_dram, g_dram):
    NEt = NE // P
    with ExitStack() as c:
        ln_g = sb(c, "ln2_g", [P, D])
        ln_b = sb(c, "ln2_b", [P, D])
        gate = sb(c, "gate2", [P, 2, D])
        gcol = sb(c, "gcol2", [P, 2, P])
        ones = sb(c, "ones2", [P, P])
        zero = sb(c, "zero", [P, 512], F32R)
        hR = sb(c, "hR", [P, DK, CW], F32R)
        hL = sb(c, "hL", [P, DK, CW], F32R)
        uw = sb(c, "uw", [P, 2, DK, P])
        vw = sb(c, "vw", [P, 2, D])
        uR = sb(c, "uR", [P, 2, DK, P], F32R)
        uL = sb(c, "uL", [P, 2, DK, P], F32R)
        vR = sb(c, "vR", [P, 2, D], F32R)
        vL = sb(c, "vL", [P, 2, D], F32R)
        gw = sb(c, "gw", [P, 2, CB, UB, TB])
        ga = sb(c, "ga", [P, CW])
        cf = sb(c, "cf", [P, CW])
        cR = sb(c, "cR", [P, 2, CW], F32R)
        cL = sb(c, "cL", [P, 2, CW], F32R)
        x1 = sb(c, "x1b", [P, D])
        r = sb(c, "r2", [P, D])
        y = sb(c, "y2", [P, D])
        st = sb(c, "st2", [P, 2, 6])
        mv = sb(c, "mv2", [P, 2])
        ve = sb(c, "ve2", [P, 1])
        sd = sb(c, "sd2", [P, 1])
        rs = sb(c, "rs2", [P, 1])
        lw, ones_ready, g_col, g_mm, g_ev = (sem(f"f_{n}") for n in ("lw", "ones", "gcol", "gmm", "gev"))
        ul = [sem(f"f_u{s}") for s in range(2)]
        vl = [sem(f"f_v{s}") for s in range(2)]
        gl = [sem(f"f_g{s}") for s in range(2)]
        zr, hr1, hr2, ur, uls, vr, vls, a_mm, a_ev, gm, cr, c_ready, v_mm = (sem(f"f_{n}") for n in (
            "zr", "hr1", "hr2", "ur", "uls", "vr", "vls", "amm", "aev", "gm", "cr", "c", "vmm"))
        acc_done, acc_read, x1l, x1u, ve_ready, sd_ready, chain, y_ready, stored = (sem(f"f_{n}") for n in (
            "acc", "accr", "x1l", "x1u", "ve", "sd", "chain", "y", "st"))
        A = [PS[0], PS[1]]
        ACC = PS[2:8]

        with nc.Block() as block:
            @block.sync
            def _(sp):
                sp.dma_start(ln_g[:, :], a["ln2_g"]).then_inc(lw, 16)
                sp.dma_start(ln_b[:, :], a["ln2_b"]).then_inc(lw, 16)
                with sp.Fori(0, NC) as n:
                    with sp.Fori(0, NEt // (2 * UB)) as b:
                        for gs in range(2):
                            m0 = n * NEt + b * (2 * UB) + gs * UB
                            sp.wait_ge(gm, m0)
                            sp.dma_start(
                                gw[:, gs, :, :, :].rearrange("p c u t -> p c (u t)"),
                                g_dram[bass.ds(n * CB, CB), :, bass.ds(b * (2 * UB) + gs * UB, UB), :].rearrange(
                                    "c p u t -> p c (u t)")).then_inc(gl[gs], 16)
                            for q in range(UB):
                                s = q % 2
                                sp.wait_ge(uls, m0 + q)
                                sp.dma_start(uw[:, s, :, :], a["u"][b * (2 * UB) + gs * UB + q, :, :, :]).then_inc(ul[s], 16)
                                sp.wait_ge(vls, m0 + q)
                                sp.dma_start(vw[:, s, :], a["v"][bass.ds((b * (2 * UB) + gs * UB + q) * P, P), :]
                                             ).then_inc(vl[s], 16)
                    with sp.Fori(0, CT) as t:
                        sp.wait_ge(x1u, n * CT + t)
                        sp.dma_start(x1[:, :], x1_dram[bass.ds(n * CW + t * P, P), :]).then_inc(x1l, 16)

            gate_engines = gate_rows(5 * DK, gate, gcol, ones, modc, ident, PS, g_col, g_mm, g_ev)

            @block.gpsimd
            def _(pool):
                pool.memset(ones[:, :], 1.0).then_inc(ones_ready, 1)
                pool.memset(zero[:, :].bitcast(F32), 0.0).then_inc(zr, 1)
                pool.sem_inc(vls, 1)
                with pool.Fori(0, NC * NEt // 2) as b:
                    for s in range(2):
                        pool.wait_ge(vr, b * 2 + s + 1)
                        pool.tensor_tensor(vL[:, s, :], vw[:, s, :], vR[:, s, :].bitcast(F32),
                                           ALU.subtract).then_inc(vls, 1)

            @block.scalar
            def _(act):
                gate_engines[1](act)
                with act.Fori(0, NC) as n:
                    with act.Fori(0, NEt // 2) as b:
                        for s in range(2):
                            m = n * NEt + b * 2 + s
                            act.wait_ge(ul[s], (n * (NEt // 2) + b + 1) * 16)
                            act.wait_ge(a_mm, n * NEt + b * 2)
                            act.activation(uR[:, s, :, :], uw[:, s, :, :], ACT.Copy).then_inc(ur, 1)
                            act.wait_ge(vl[s], (n * (NEt // 2) + b + 1) * 16)
                            act.wait_ge(v_mm, m)
                            act.activation(vR[:, s, :], vw[:, s, :], ACT.Copy).then_inc(vr, 1)
                            act.wait_ge(a_mm, m + 1)
                            act.wait_ge(gm, m + UB)
                            act.activation(ga[:, :], A[s][:, 0:CW], ACT.Gelu).then_inc(a_ev, 1)
                    with act.Fori(0, CT) as t:
                        act.wait_ge(ve_ready, n * CT + t + 1)
                        act.activation(sd[:, :], ve[:, :], ACT.Sqrt).then_inc(sd_ready, 1)
                        act.wait_ge(y_ready, n * CT + t + 1)
                        act.dma_start(a["y"][bass.ds(n * CW + t * P, P), :], y[:, :]).then_inc(stored, 16)
                act.wait_ge(stored, NT * 16)

            @block.tensor
            def _(pe):
                gate_engines[0](pe)
                pe.wait_ge(zr, 1)
                pe.sem_inc(v_mm, 1)

                def hidden(m, s):
                    pe.wait_ge(uls, m + 2)
                    pe.wait_ge(a_ev, m - s)
                    for k in range(DK):
                        for w, h in ((uR, hR), (uR, hL), (uL, hR)):
                            mm = pe.matmul(A[s][:, 0:CW], w[:, s, k, :], h[:, k, :],
                                           start=(k == 0 and w is uR and h is hR),
                                           stop=(k == DK - 1 and w is uL))
                    mm.then_inc(a_mm, 1)

                def down(m, s):
                    pe.wait_ge(c_ready, m + 1)
                    pe.wait_ge(vls, m + 2)
                    for t in range(CT):
                        for w, v in ((cR, vR), (cR, vL), (cL, vR)):
                            for half in range(2):
                                mm = pe.matmul(ACC[2 * t + half][:, :], w[:, s, t * P:(t + 1) * P],
                                               v[:, s, half * 512:(half + 1) * 512], start=False, stop=False,
                                               skip_group_check=True)
                    mm.then_inc(v_mm, 1)

                with pe.Fori(0, NC) as n:
                    pe.wait_ge(hr2, n + 1)
                    pe.wait_ge(acc_read, n * CT)
                    for bank in ACC:
                        pe.matmul(bank[:, :], zero[:, 0:P], zero[:, :], start=True, stop=False, skip_group_check=True)
                    base = n * NEt
                    hidden(base, 0)
                    with pe.Fori(0, NEt // 2 - 1) as b:
                        hidden(base + b * 2 + 1, 1)
                        down(base + b * 2, 0)
                        hidden(base + b * 2 + 2, 0)
                        down(base + b * 2 + 1, 1)
                    hidden(base + NEt - 1, 1)
                    down(base + NEt - 2, 0)
                    down(base + NEt - 1, 1)
                    for bank in ACC:
                        mm = pe.matmul(bank[:, :], zero[:, 0:P], zero[:, :], start=False, stop=True,
                                       skip_group_check=True)
                    mm.then_inc(acc_done, 1)

            @block.vector
            def _(dve):
                dve.wait_ge(ones_ready, 1)
                gate_engines[2](dve)
                dve.wait_ge(lw, 32)
                dve.sem_inc(uls, 1)
                dve.sem_inc(gm, UB)
                with dve.Fori(0, NC) as n:
                    for k in range(DK):
                        ins = dve.tensor_copy(hR[:, k, :], h2T[:, k, bass.ds(n * CW, CW)])
                    ins.then_inc(hr1, 1)
                    dve.wait_ge(hr1, n + 1)
                    for k in range(DK):
                        ins = dve.tensor_tensor(hL[:, k, :], h2T[:, k, bass.ds(n * CW, CW)],
                                                hR[:, k, :].bitcast(F32), ALU.subtract)
                    ins.then_inc(hr2, 1)
                    with dve.Fori(0, NEt // (2 * UB)) as b:
                        for gs in range(2):
                            for q in range(UB):
                                s = q % 2
                                m = n * NEt + b * (2 * UB) + gs * UB + q
                                dve.wait_ge(ur, m + 1)
                                dve.tensor_tensor(uL[:, s, :, :], uw[:, s, :, :], uR[:, s, :, :].bitcast(F32),
                                                  ALU.subtract).then_inc(uls, 1)
                                if q == 0:
                                    dve.wait_ge(gl[gs], (n * (NEt // UB // 2) * 16) + (b * 16) + 16)
                                dve.wait_ge(a_ev, m + 1)
                                dve.tensor_tensor(cf[:, :].rearrange("p (c t) -> p c t", c=CB),
                                                  ga[:, :].rearrange("p (c t) -> p c t", c=CB),
                                                  gw[:, gs, :, q, :], ALU.mult).then_inc(gm, 1)
                                dve.wait_ge(gm, m + UB + 1)
                                dve.wait_ge(v_mm, m)
                                dve.tensor_copy(cR[:, s, :], cf[:, :]).then_inc(cr, 1)
                                dve.wait_ge(cr, m + 1)
                                dve.tensor_tensor(cL[:, s, :], cf[:, :], cR[:, s, :].bitcast(F32),
                                                  ALU.subtract).then_inc(c_ready, 1)
                                dve.wait_ge(c_ready, m + 1)
                    dve.wait_ge(acc_done, n + 1)
                    for t in range(CT):
                        i = n * CT + t
                        ch = Count(dve, chain)
                        dve.wait_ge(stored, i * 16)
                        row = 0 if t == 0 else 1
                        for half in range(2):
                            sl = slice(half * 512, (half + 1) * 512)
                            ins = dve.tensor_tensor(r[:, sl], gate[:, row, sl], ACC[2 * t + half][:, :], ALU.mult)
                        ins.then_inc(acc_read, 1)
                        dve.wait_ge(acc_read, i + 1)
                        dve.wait_ge(x1l, (i + 1) * 16)
                        ch.step(dve.scalar_tensor_tensor(y[:, :], x1[:, :], ALPHA, r[:, :], ALU.mult, ALU.add))
                        dve.sem_inc(x1u, 1)
                        for half in range(2):
                            ins = dve.bn_stats(st[:, half, :], y[:, half * 512:(half + 1) * 512])
                        ch.step(ins)
                        ch.step(dve.bn_aggr(mv[:, :], st[:, :, :].rearrange("p a b -> p (a b)")))
                        dve.tensor_scalar(ve[:, :], mv[:, 1:2], EPS, None, ALU.add).then_inc(ve_ready, 1)
                        dve.wait_ge(sd_ready, i + 1)
                        ch.step(dve.reciprocal(rs[:, :], sd[:, :]))
                        ch.step(dve.tensor_scalar(r[:, :], y[:, :], mv[:, 0:1], rs[:, 0:1], ALU.subtract, ALU.mult))
                        ch.step(dve.tensor_tensor(r[:, :], r[:, :], ln_g[:, :], ALU.mult))
                        dve.tensor_tensor(y[:, :], r[:, :], ln_b[:, :], ALU.add).then_inc(y_ready, 1)
                        dve.wait_ge(y_ready, i + 1)
                        if t == 0:
                            ch.step(dve.tensor_copy(gate[:, 0, :], gate[:, 1, :]))


SHAPES = {"y": [T, D], "new_ckv": [SEQ, KVR], "new_krope": [SEQ, ROPE]}


def kernel(x_prompt, x_sample, cache_ckv, cache_krope, c, c_ctx, w_mod, b_mod, w_in, w_s, b_s,
           g_q, w_qb, g_kv, w_kvb, w_o, ln1_g, ln1_b, w_pq, sub_keys, u_tab, v_tab, ln2_g, ln2_b):
    import concourse.bacc as bacc
    from concourse.bass_utils import run_bass_kernel_spmd

    def rows(w, k):
        return w.reshape(k, P, -1).transpose(1, 0, 2)

    def every_row(v):
        return np.broadcast_to(v.reshape(1, -1), (P, v.size))

    n = {k: np.asarray(v) for k, v in dict(locals()).items() if not callable(v)}
    x = np.concatenate([n["x_prompt"][0], n["x_sample"][0]], axis=0)
    wqb = n["w_qb"][0].reshape(QR, H, NOPE + ROPE)
    wkvb = n["w_kvb"][0].reshape(KVR, H, NOPE + VD)
    f = ROPE // 4
    freq = (1.0 / (np.float32(10000.0) ** (np.arange(f, dtype=np.float32) / np.float32(f)))).astype(np.float32)
    tok = np.arange(DEC)
    ang = [np.float32(v)[:, None] * freq[None, :] for v in ((tok // GRID_W).astype(np.float32),
                                                            (tok % GRID_W).astype(np.float32))]
    cos, sin = [np.cos(v).astype(np.float32) for v in ang], [np.sin(v).astype(np.float32) for v in ang]
    table = np.zeros((NT, P, 2, ROPE), np.float32)
    table[1:, :, 0] = np.concatenate([cos[0], cos[0], cos[1], cos[1]], 1).reshape(NT - 1, P, ROPE)
    table[1:, :, 1] = np.concatenate([-sin[0], sin[0], -sin[1], sin[1]], 1).reshape(NT - 1, P, ROPE)
    arrays = {
        "x": x,
        "xT": x.reshape(NT, P, DK, P).transpose(0, 3, 2, 1),
        "cond": np.stack([n["c_ctx"].reshape(DK, P), n["c"].reshape(DK, P)], -1).transpose(1, 0, 2),
        "w_mod": n["w_mod"][0].reshape(DK, P, 6 * DK, P).transpose(2, 1, 0, 3),
        "b_mod": n["b_mod"][0].reshape(6 * DK, P).T,
        "w_in": rows(n["w_in"][0], DK),
        "w_s": n["w_s"][0].transpose(2, 0, 1),
        "b_s": n["b_s"][0].T,
        "g_q": n["g_q"][0].reshape(QK, P).T,
        "g_kv": every_row(n["g_kv"][0]),
        "w_qn": rows(wqb[:, :, :NOPE].reshape(QR, -1), QK),
        "w_qr": rows(wqb[:, :, NOPE:].reshape(QR, -1), QK),
        "w_kn": rows(wkvb[:, :, :NOPE].reshape(KVR, -1), KK),
        "w_v": rows(wkvb[:, :, NOPE:].reshape(KVR, -1), KK),
        "cckT": rows(n["cache_ckv"][0, 0].T, KK),
        "ckrT": n["cache_krope"][0, 0].T,
        "rot": table,
        "w_o": rows(n["w_o"][0], DK),
        "ln1_g": every_row(n["ln1_g"][0]),
        "ln1_b": every_row(n["ln1_b"][0]),
        "w_pq": rows(n["w_pq"][0], DK),
        "keys": n["sub_keys"][0].reshape(HS, NKEY, P).transpose(2, 0, 1),
        "u": n["u_tab"][0].reshape(NE // P, P, DK, P).transpose(0, 3, 2, 1),
        "v": n["v_tab"][0],
        "ln2_g": every_row(n["ln2_g"][0]),
        "ln2_b": every_row(n["ln2_b"][0]),
    }
    nc = bacc.Bacc("TRN2", target_bir_lowering=False, num_devices=1)
    ins, aps = {}, {}
    for name, v in arrays.items():
        v = np.ascontiguousarray(v)
        ins[f"in_{name}"] = v
        aps[name] = nc.dram_tensor(f"in_{name}", v.shape, mybir.dt.from_np(v.dtype), kind="ExternalInput").ap()
    for name, shape in SHAPES.items():
        aps[name] = nc.dram_tensor(f"out_{name}", shape, F32, kind="ExternalOutput").ap()
    build(nc, aps)
    got = run_bass_kernel_spmd(nc, [ins], core_ids=[0]).results[0]
    y = got["out_y"]
    return (y[:SEQ].reshape(1, SEQ, D), y[SEQ:].reshape(1, DEC, D),
            got["out_new_ckv"].reshape(1, 1, SEQ, KVR), got["out_new_krope"].reshape(1, 1, SEQ, ROPE))
```

```python
import math
from contextlib import ExitStack

import numpy as np

import concourse.bass as bass
from concourse import mybir

F32 = mybir.dt.float32
F32R = mybir.dt.float32r
U32 = mybir.dt.uint32
ALU = mybir.AluOpType
ACT = mybir.ActivationFunctionType
AX = mybir.AxisListType

P = 128
D = 1024
DK = D // P
SEQ, DEC, PAST = 128, 1024, 128
T = SEQ + DEC
NT = T // P
G, GD = 4, 128
AW = G * GD
H, NOPE, ROPE, VD = 4, 128, 64, 128
QR, KVR = 384, 256
QK, KK = QR // P, KVR // P
IN_COLS = 2 * AW + QR + KVR + ROPE
Z = ((0, AW), (AW, AW), (2 * AW, QR), (2 * AW + QR, KVR + ROPE))
KT = NT + 1
NKS = (KT - 1) * P
CW = 384
SCALE = 1.0 / math.sqrt(NOPE + ROPE)
PH, NKEY, TOPK = 8, 128, 16
HS = 2 * PH
PAIRS = PH * TOPK
NE = NKEY * NKEY
ALPHA = 2.0 ** 0.25
EPS = 1e-6
GRID_W = 64
LOW = -3.0e38
CT = CW // P
NC = T // CW
TB = 32
NTB = T // TB
CB = CW // TB
UB = 4


class Count:

    def __init__(self, eng, sem):
        self.eng, self.sem, self.n = eng, sem, 0
        eng.sem_inc(sem, 1)
        eng.sem_clear(sem)

    def step(self, ins):
        self.n += 1
        ins.then_inc(self.sem, 1)
        self.eng.wait_ge(self.sem, self.n)


def build(nc, a):
    es = ExitStack()
    used = set()

    def sb(stack, name, shape, dt=F32):
        return stack.enter_context(nc.sbuf_tensor(name, shape, dt))

    def sem(name):
        assert name not in used
        used.add(name)
        return es.enter_context(nc.semaphore(name))

    with es:
        x1_dram = nc.dram_tensor("x1_scratch", [T, D], F32, kind="Internal").ap()
        g_dram = nc.dram_tensor("g_scratch", [NTB, P, NKEY, TB], F32, kind="Internal").ap()
        gate_dram = nc.dram_tensor("gate_scratch", [NC + 1, P, D], F32, kind="Internal").ap()
        PS = [es.enter_context(nc.psum_tensor(f"bank{b}", [P, 512], F32)) for b in range(8)]
        ident = sb(es, "ident", [P, P])
        modc = sb(es, "modc", [P, 6 * DK, 2])
        sp1 = sb(es, "sp1", [P, 2, DK, 2])
        big = sb(es, "big", [P, KT * H * P * 2])
        kT = big[:, 0:KT * H * P].rearrange("p (h k) -> p h k", h=H)
        vv = big[:, KT * H * P:2 * KT * H * P].rearrange("p (t c) -> p t c", t=KT)
        h2T = big[:, 0:DK * T].rearrange("p (k t) -> p k t", k=DK)
        modulation(nc, a, sb, sem, PS, ident, modc, sp1)
        with ExitStack() as mid:
            aoT = sb(mid, "aoT", [P, G, T])
            boT = sb(mid, "boT", [P, H, T])
            with ExitStack() as att:
                qT = sb(att, "qT", [P, H, T])
                qrT = sb(att, "qrT", [P, 2, T])
                krT = sb(att, "krT", [P, KT * P])
                mixer_inputs(nc, a, sb, sem, PS, ident, modc, sp1, aoT, qT, qrT, krT, kT, vv)
                attention(nc, a, sb, sem, PS, ident, boT, qT, qrT, krT, kT, vv)
            residual_one(nc, a, sb, sem, PS, ident, modc, sp1, aoT, boT, h2T, x1_dram, gate_dram)
        experts(nc, a, sb, sem, PS, ident, big, h2T, x1_dram, g_dram, gate_dram)


def modulation(nc, a, sb, sem, PS, ident, modc, sp1):
    NJ = 6 * DK
    NW = 4
    with ExitStack() as c:
        cond = sb(c, "cond", [P, DK, 2])
        silu = sb(c, "silu", [P, DK, 2])
        bmod = sb(c, "bmod", [P, NJ])
        wm = sb(c, "wm", [P, NW, DK, P])
        loaded = sem("m_loaded")
        w_in = [sem(f"m_w{i}") for i in range(NW)]
        w_used, silu_ready, made, id0, id1, mod_ready = (sem(f"m_{n}") for n in (
            "w_used", "silu", "made", "id0", "id1", "mod_ready"))
        with nc.Block() as block:
            @block.sync
            def _(sp):
                sp.dma_start(cond[:, :, :], a["cond"]).then_inc(loaded, 16)
                sp.dma_start(bmod[:, :], a["b_mod"]).then_inc(loaded, 16)
                with sp.Fori(0, NJ // NW) as j:
                    for s in range(NW):
                        sp.wait_ge(w_used, j * NW + s + 1)
                        sp.dma_start(wm[:, s, :, :], a["w_mod"][j * NW + s, :, :, :]).then_inc(w_in[s], 16)

            @block.gpsimd
            def _(pool):
                pool.memset(ident[:, :], 0.0).then_inc(id0, 1)
                pool.wait_ge(id0, 1)
                pool.affine_select(out=ident[:, :], in_=ident[:, :], compare_op=ALU.not_equal, fill=1.0,
                                   base=0, pattern=[[-1, P]], channel_multiplier=1).then_inc(id1, 1)
                pool.wait_ge(id1, 1)

            @block.scalar
            def _(act):
                act.wait_ge(loaded, 32)
                act.activation(silu[:, :, :], cond[:, :, :], ACT.Silu).then_inc(silu_ready, 1)

            @block.tensor
            def _(pe):
                pe.sem_inc(w_used, NW)
                pe.wait_ge(silu_ready, 1)
                out = PS[0][:, 0:2 * NJ].rearrange("p (j c) -> p j c", c=2)
                with pe.Fori(0, NJ // NW) as j:
                    for s in range(NW):
                        pe.wait_ge(w_in[s], (j + 1) * 16)
                        for k in range(DK):
                            mm = pe.matmul(out[:, j * NW + s, :], wm[:, s, k, :], silu[:, k, :],
                                           start=(k == 0), stop=(k == DK - 1))
                        mm.then_inc(w_used, 1)

            @block.vector
            def _(dve):
                dve.wait_ge(w_used, NJ + NW)
                bc = bmod[:, :].rearrange("p (j o) -> p j o", o=1).to_broadcast([P, NJ, 2])
                dve.tensor_tensor(modc[:, :, :], PS[0][:, 0:2 * NJ].rearrange("p (j c) -> p j c", c=2), bc,
                                  ALU.add).then_inc(made, 1)
                dve.wait_ge(made, 1)
                for n, at in enumerate((DK, 4 * DK)):
                    dve.tensor_scalar(sp1[:, n, :, :], modc[:, at:at + DK, :], 1.0, None,
                                      ALU.add).then_inc(mod_ready, 1)
                dve.wait_ge(mod_ready, 2)


def mixer_inputs(nc, a, sb, sem, PS, ident, modc, sp1, aoT, qT, qrT, krT, kT, vv):
    with ExitStack() as c:
        w_in = sb(c, "w_in", [P, DK, IN_COLS])
        w_s = sb(c, "w_s", [P, G, P])
        b_s = sb(c, "b_s", [P, G])
        g_q = sb(c, "g_q", [P, QK])
        g_kv = sb(c, "g_kv", [P, KVR])
        w_qn = sb(c, "w_qn", [P, QK, H * NOPE])
        w_qr = sb(c, "w_qr", [P, QK, H * ROPE])
        w_kn = sb(c, "w_kn", [P, KK, H * NOPE])
        w_v = sb(c, "w_v", [P, KK, H * VD])
        cckT = sb(c, "cckT", [P, KK, P])
        xt = sb(c, "xt", [P, DK, P])
        hT = sb(c, "hT", [P, DK, P])
        rot = sb(c, "rot", [P, 2, ROPE])
        u = sb(c, "u", [P, AW])
        vg = sb(c, "vg", [P, AW])
        vst = vg
        aout = u
        ql = sb(c, "ql", [P, QR])
        ckv = sb(c, "ckv", [P, KVR])
        kr = sb(c, "kr", [P, 2, ROPE])
        t1 = sb(c, "t1", [P, H * ROPE])
        t2 = sb(c, "t2", [P, H * ROPE])
        qr = sb(c, "qr", [P, H * ROPE])
        qlT = sb(c, "qlT", [P, QK, P])
        ckT = sb(c, "ckT", [P, KK, P])
        junk = sb(c, "junk", [P, QR])
        st = sb(c, "st", [P, G, 6])
        mv = sb(c, "mv", [P, G, 2])
        var = sb(c, "var", [P, G + 2])
        ssq = sb(c, "ssq", [P, 2])
        sd = sb(c, "sd", [P, G + 2])
        rs = sb(c, "rs", [P, G + 2])

        wl = sem("a_weights")
        xl, rl = sem("a_x"), sem("a_rot")
        h_ready, z_ready, z_used = sem("a_h"), sem("a_z"), sem("a_z_used")
        gelu_u, gelu_v, sq_q, sq_kv, sd_ready = (sem(f"a_{n}") for n in ("gu", "gv", "sqq", "sqkv", "sd"))
        chain, var_ready, v_std, lat_ready, gate_ready, mixed = (sem(f"a_{n}") for n in (
            "chain", "var", "vstd", "lat", "gate", "mixed"))
        trl, tra, trq, qlT_ready, ao_ev, q_ev, k_ev, v_ev, qr_ready, qr_ev = (sem(f"a_{n}") for n in (
            "trl", "tra", "trq", "qlT", "ao", "qev", "kev", "vev", "qr", "qrev"))
        q_mm, k_mm, v_mm, r_mm = sem("a_qmm"), sem("a_kmm"), sem("a_vmm"), sem("a_rmm")
        stored, kr_st = sem("a_stored"), sem("a_krst")
        kr_ev = sem("a_krev")
        nw = 12

        with nc.Block() as block:
            @block.sync
            def _(sp):
                for dst, src in ((w_in, "w_in"), (w_s, "w_s"), (w_qn, "w_qn"), (w_qr, "w_qr"),
                                 (w_kn, "w_kn"), (w_v, "w_v"), (cckT, "cckT")):
                    sp.dma_start(dst[:, :, :], a[src]).then_inc(wl, 16)
                for dst, src in ((b_s, "b_s"), (g_q, "g_q"), (g_kv, "g_kv")):
                    sp.dma_start(dst[:, :], a[src]).then_inc(wl, 16)
                for half in range(2):
                    sp.dma_start(krT[half * ROPE:(half + 1) * ROPE, P:2 * P], a["ckrT"]).then_inc(wl, 16)
                sp.dma_start(xt[:, :, :], a["xT"][0, :, :, :]).then_inc(xl, 16)
                sp.dma_start(rot[:, :, :], a["rot"][0, :, :, :]).then_inc(rl, 16)
                with sp.Fori(1, NT) as i:
                    sp.wait_ge(h_ready, i)
                    sp.dma_start(xt[:, :, :], a["xT"][i, :, :, :]).then_inc(xl, 16)
                    sp.wait_ge(qr_ready, i)
                    sp.dma_start(rot[:, :, :], a["rot"][i, :, :, :]).then_inc(rl, 16)
                sp.wait_ge(stored, 16)
                sp.wait_ge(kr_st, 16)

            def mod_h(dve, i, m, ch):
                dve.wait_ge(xl, (i + 1) * 16)
                for k in range(DK):
                    ins = dve.tensor_scalar(hT[:, k, :], xt[:, k, :], sp1[:, 0, k, m:m + 1], modc[:, k, m:m + 1],
                                            ALU.mult, ALU.add)
                ins.then_inc(h_ready, 1)

            def dve_tile(dve, i, m):
                ch = Count(dve, chain)
                dve.wait_ge(z_ready, i * 4 + 4)
                dve.wait_ge(gelu_v, i + 1)
                for g in range(G):
                    ins = dve.bn_stats(st[:, g, :], vg[:, g * GD:(g + 1) * GD])
                ch.step(ins)
                for g in range(G):
                    ins = dve.bn_aggr(mv[:, g, :], st[:, g, :])
                ch.step(ins)
                dve.tensor_scalar(var[:, 0:G], mv[:, :, 1], EPS, None, ALU.add)
                dve.wait_ge(sq_kv, i + 1)
                dve.tensor_scalar(var[:, G:G + 1], ssq[:, 0:1], 1.0 / QR, EPS, ALU.mult, ALU.add)
                dve.tensor_scalar(var[:, G + 1:G + 2], ssq[:, 1:2], 1.0 / KVR, EPS, ALU.mult,
                                  ALU.add).then_inc(var_ready, 1)
                dve.wait_ge(sd_ready, i + 1)
                ch.step(dve.reciprocal(rs[:, :], sd[:, :]))
                for g in range(G):
                    part = vg[:, g * GD:(g + 1) * GD]
                    ins = dve.tensor_scalar(part, part, mv[:, g, 0:1], rs[:, g:g + 1], ALU.subtract, ALU.mult)
                ins.then_inc(v_std, 1)
                dve.tensor_scalar(ql[:, :], PS[2][:, 0:QR], rs[:, G:G + 1], None, ALU.mult)
                if m == 0:
                    dve.wait_ge(rl, 16)
                    for half in range(2):
                        ins = dve.tensor_copy(kr[:, half, :], PS[3][:, KVR:KVR + ROPE])
                else:
                    dve.wait_ge(rl, (i + 1) * 16)
                    ps = PS[3][:, KVR:KVR + ROPE]
                    dve.tensor_tensor(t1[:, 0:ROPE], ps, rot[:, 0, :], ALU.mult)
                    ch.step(rotate(dve, t2, ps, 1))
                    for half in range(2):
                        ins = dve.tensor_tensor(kr[:, half, :], t1[:, 0:ROPE], t2[:, 0:ROPE], ALU.add)
                dve.scalar_tensor_tensor(ckv[:, :], PS[3][:, 0:KVR], rs[:, G + 1:G + 2], g_kv[:, :],
                                         ALU.mult, ALU.mult).then_inc(lat_ready, 1)
                dve.wait_ge(mixed, i + 1)
                dve.wait_ge(gelu_u, i + 1)
                for g in range(G):
                    sl = slice(g * GD, (g + 1) * GD)
                    ins = dve.scalar_tensor_tensor(aout[:, sl], PS[4][:, sl], b_s[:, g:g + 1], u[:, sl],
                                                   ALU.add, ALU.mult)
                ins.then_inc(gate_ready, 1)
                dve.wait_ge(trl, i + 1)
                for k in range(QK):
                    dve.tensor_scalar(qlT[:, k, :], PS[6][:, k * P:(k + 1) * P], g_q[:, k:k + 1], None, ALU.mult)
                dve.tensor_copy(ckT[:, :, :], PS[7][:, 0:KK * P].rearrange("p (k t) -> p k t", k=KK))
                dst = krT[:, 0:P] if m == 0 else krT[:, bass.ds(i * P + P, P)]
                dve.tensor_copy(dst, PS[6][:, QK * P:(QK + 1) * P]).then_inc(qlT_ready, 1)
                dve.wait_ge(r_mm, i + 1)
                ps = PS[7][:, 0:H * ROPE]
                if m == 0:
                    dve.tensor_copy(qr[:, :], ps).then_inc(qr_ready, 1)
                else:
                    cosb = rot[:, 0:1, :].to_broadcast([P, H, ROPE])
                    dve.tensor_tensor(t1[:, :].rearrange("p (h r) -> p h r", h=H),
                                      ps.rearrange("p (h r) -> p h r", h=H), cosb, ALU.mult)
                    ch.step(rotate(dve, t2, ps, H))
                    dve.tensor_tensor(qr[:, :], t1[:, :], t2[:, :], ALU.add).then_inc(qr_ready, 1)

            def rotate(dve, out, ps, heads):
                for half in range(2):
                    for part in range(heads):
                        o = out[:, part * ROPE:(part + 1) * ROPE].rearrange("p (a b f) -> p a b f", a=2, b=2)
                        s = ps[:, part * ROPE:(part + 1) * ROPE].rearrange("p (a b f) -> p a b f", a=2, b=2)
                        w = rot[:, 1, :].rearrange("p (a b f) -> p a b f", a=2, b=2)
                        ins = dve.tensor_tensor(o[:, :, half, :], s[:, :, 1 - half, :], w[:, :, half, :], ALU.mult)
                return ins

            @block.vector
            def _(dve):
                dve.wait_ge(wl, nw * 16)
                mod_h(dve, 0, 0, None)
                dve_tile(dve, 0, 0)
                with dve.Fori(1, NT) as i:
                    mod_h(dve, i, 1, None)
                    dve_tile(dve, i, 1)

            def act_tile(act, i, first):
                act.wait_ge(z_ready, i * 4 + 1)
                act.wait_ge(tra, i)
                act.activation(u[:, :], PS[0][:, :], ACT.Gelu).then_inc(gelu_u, 1)
                act.wait_ge(z_ready, i * 4 + 2)
                act.wait_ge(mixed, i)
                act.activation(vg[:, :], PS[1][:, :], ACT.Gelu).then_inc(gelu_v, 1)
                act.wait_ge(z_ready, i * 4 + 3)
                act.activation(junk[:, 0:QR], PS[2][:, 0:QR], ACT.Square, accum_out=ssq[:, 0:1]).then_inc(sq_q, 1)
                act.wait_ge(z_ready, i * 4 + 4)
                act.wait_ge(sq_q, i + 1)
                act.activation(junk[:, 0:KVR], PS[3][:, 0:KVR], ACT.Square,
                               accum_out=ssq[:, 1:2]).then_inc(sq_kv, 1)
                act.wait_ge(var_ready, i + 1)
                act.activation(sd[:, :], var[:, :], ACT.Sqrt).then_inc(sd_ready, 1)
                key = 0 if first else i * P + P
                act.wait_ge(tra, i + 1)
                act.activation(aoT[:, :, bass.ds(i * P, P)], PS[5][:, :].rearrange("p (g t) -> p g t", g=G),
                               ACT.Copy).then_inc(ao_ev, 1)
                act.wait_ge(q_mm, i + 1)
                act.activation(qT[:, :, bass.ds(i * P, P)], PS[4][:, :].rearrange("p (h t) -> p h t", h=H),
                               ACT.Copy).then_inc(q_ev, 1)
                act.wait_ge(k_mm, i + 2)
                act.activation(kT[:, :, bass.ds(key, P)], PS[5][:, :].rearrange("p (h t) -> p h t", h=H),
                               ACT.Copy).then_inc(k_ev, 1)
                act.wait_ge(v_mm, i + 2)
                row = 0 if first else i + 1
                act.activation(vv[:, row, :], PS[6][:, :], ACT.Copy).then_inc(v_ev, 1)
                act.wait_ge(trq, i + 1)
                act.activation(qrT[:, :, bass.ds(i * P, P)], PS[4][:, 0:2 * P].rearrange("p (h t) -> p h t", h=2),
                               ACT.Copy).then_inc(qr_ev, 1)

            @block.scalar
            def _(act):
                act.wait_ge(k_mm, 1)
                act.activation(kT[:, :, P:2 * P], PS[5][:, :].rearrange("p (h t) -> p h t", h=H),
                               ACT.Copy).then_inc(k_ev, 1)
                act.wait_ge(v_mm, 1)
                act.activation(vv[:, 1, :], PS[6][:, :], ACT.Copy).then_inc(v_ev, 1)
                act_tile(act, 0, True)
                act.wait_ge(lat_ready, 1)
                act.dma_start(a["new_ckv"], ckv[:, :]).then_inc(stored, 16)
                act.dma_start(a["new_krope"], kr[:, 0, :]).then_inc(kr_st, 16)
                act.wait_ge(stored, 16)
                act.wait_ge(kr_st, 16)
                with act.Fori(1, NT) as i:
                    act_tile(act, i, False)

            def keys_values(pe, ckT_):
                for h in range(H):
                    for k in range(KK):
                        mm = pe.matmul(PS[5][:, h * P:(h + 1) * P], w_kn[:, k, h * NOPE:(h + 1) * NOPE],
                                       ckT_[:, k, :], start=(k == 0), stop=(k == KK - 1))
                mm.then_inc(k_mm, 1)

            def values(pe, ckT_):
                for k in range(KK):
                    mm = pe.matmul(PS[6][:, :], ckT_[:, k, :], w_v[:, k, :], start=(k == 0), stop=(k == KK - 1))
                mm.then_inc(v_mm, 1)

            def pe_tile(pe, i):
                pe.wait_ge(h_ready, i + 1)
                for n, (at, w) in enumerate(Z):
                    if n == 0:
                        pe.wait_ge(gelu_u, i)
                    elif n == 1:
                        pe.wait_ge(gelu_v, i)
                    else:
                        pe.wait_ge(lat_ready, i)
                    for k in range(DK):
                        mm = pe.matmul(PS[n][:, 0:w], hT[:, k, :], w_in[:, k, at:at + w],
                                       start=(k == 0), stop=(k == DK - 1))
                    mm.then_inc(z_ready, 1)
                pe.wait_ge(v_std, i + 1)
                pe.wait_ge(qr_ev, i)
                for g in range(G):
                    mm = pe.matmul(PS[4][:, g * GD:(g + 1) * GD], w_s[:, g, :], vst[:, g * GD:(g + 1) * GD],
                                   start=True, stop=True)
                mm.then_inc(mixed, 1)
                pe.wait_ge(lat_ready, i + 1)
                pe.wait_ge(v_ev, i + 1)
                for k in range(QK):
                    pe.transpose(PS[6][:, k * P:(k + 1) * P], ql[:, k * P:(k + 1) * P], ident[:, :])
                pe.transpose(PS[6][:, QK * P:(QK + 1) * P], kr[:, :, :].rearrange("p a r -> p (a r)"), ident[:, :])
                pe.wait_ge(qr_ready, i)
                for k in range(KK):
                    mm = pe.transpose(PS[7][:, k * P:(k + 1) * P], ckv[:, k * P:(k + 1) * P], ident[:, :])
                mm.then_inc(trl, 1)
                pe.wait_ge(gate_ready, i + 1)
                pe.wait_ge(k_ev, i + 1)
                for g in range(G):
                    mm = pe.transpose(PS[5][:, g * P:(g + 1) * P], aout[:, g * GD:(g + 1) * GD], ident[:, :])
                mm.then_inc(tra, 1)
                pe.wait_ge(qlT_ready, i + 1)
                for h in range(H):
                    for k in range(QK):
                        mm = pe.matmul(PS[4][:, h * P:(h + 1) * P], w_qn[:, k, h * NOPE:(h + 1) * NOPE],
                                       qlT[:, k, :], start=(k == 0), stop=(k == QK - 1))
                mm.then_inc(q_mm, 1)
                for k in range(QK):
                    mm = pe.matmul(PS[7][:, 0:H * ROPE], qlT[:, k, :], w_qr[:, k, :],
                                   start=(k == 0), stop=(k == QK - 1))
                mm.then_inc(r_mm, 1)
                pe.wait_ge(ao_ev, i + 1)
                keys_values(pe, ckT)
                values(pe, ckT)
                pe.wait_ge(qr_ready, i + 1)
                pe.wait_ge(q_ev, i + 1)
                for pair in range(2):
                    mm = pe.transpose(PS[4][:, pair * P:(pair + 1) * P], qr[:, pair * P:(pair + 1) * P], ident[:, :])
                mm.then_inc(trq, 1)

            @block.tensor
            def _(pe):
                pe.wait_ge(wl, nw * 16)
                keys_values(pe, cckT)
                values(pe, cckT)
                pe_tile(pe, 0)
                with pe.Fori(1, NT) as i:
                    pe_tile(pe, i)


def attention(nc, a, sb, sem, PS, ident, boT, qT, qrT, krT, kT, vv):
    with ExitStack() as c:
        qc = sb(c, "qc", [P, H, P])
        qrc = sb(c, "qrc", [P, 2, P])
        pr = sb(c, "pr", [P, 2, NKS])
        prT = sb(c, "prT", [P, NKS])
        mx = sb(c, "mx", [P, 2])
        nb = sb(c, "nb", [P, 2])
        sm = sb(c, "sm", [P, 2])
        ri = sb(c, "ri", [P, 2])
        q_ready, s_ready, m_ready, b_ready, e_ready, r_ready, p_ready, t_ready, tc1, tc2, o_ready, o_ev = (
            sem(f"b_{n}") for n in ("q", "s", "m", "b", "e", "r", "p", "t", "tc1", "tc2", "o", "oev"))

        with nc.Block() as block:
            def chunks(n):
                return [(b, min(CW, n - b * CW)) for b in range((n + CW - 1) // CW)]

            def scores(pe, h, n, first, nkeys, key0):
                pe.wait_ge(e_ready, n)
                half = (h % 2) * ROPE
                for b, w in chunks(nkeys):
                    ks = slice(key0 + b * CW, key0 + b * CW + w)
                    pe.matmul(PS[b][:, 0:w], qc[:, h, :], kT[:, h, ks], start=True, stop=False)
                    mm = pe.matmul(PS[b][:, 0:w], qrc[half:half + ROPE, h // 2, :], krT[half:half + ROPE, ks],
                                   start=False, stop=True)
                mm.then_inc(s_ready, 1)

            def outputs(pe, h, n, nkeys, kt0):
                nk = nkeys // P
                pe.wait_ge(p_ready, n + 1)
                pe.wait_ge(tc1, n)
                pe.wait_ge(tc2, n)
                for k in range(nk):
                    mm = pe.transpose(PS[3 + k // 4][:, (k % 4) * P:(k % 4 + 1) * P],
                                      pr[:, h % 2, k * P:(k + 1) * P], ident[:, :])
                mm.then_inc(t_ready, 1)
                pe.wait_ge(o_ev, n)
                pe.wait_ge(tc1, n + 1)
                pe.wait_ge(tc2, n + 1)
                for k in range(nk):
                    mm = pe.matmul(PS[6][:, 0:P], vv[:, kt0 + k, h * VD:(h + 1) * VD], prT[:, k * P:(k + 1) * P],
                                   start=(k == 0), stop=(k == nk - 1))
                mm.then_inc(o_ready, 1)

            def pe_tile(pe, i, nkeys, key0):
                pe.wait_ge(q_ready, i + 1)
                scores(pe, 0, i * H, False, nkeys, key0)
                for h in range(1, H):
                    scores(pe, h, i * H + h, False, nkeys, key0)
                    outputs(pe, h - 1, i * H + h - 1, nkeys, key0 // P)
                outputs(pe, H - 1, i * H + H - 1, nkeys, key0 // P)

            @block.tensor
            def _(pe):
                pe_tile(pe, 0, P, 0)
                with pe.Fori(1, NT) as i:
                    pe_tile(pe, i, NKS, P)

            def dve_tile(dve, i, nkeys):
                dve.wait_ge(s_ready, i * H)
                dve.tensor_copy(qc[:, :, :], qT[:, :, bass.ds(i * P, P)])
                dve.tensor_copy(qrc[:, :, :], qrT[:, :, bass.ds(i * P, P)]).then_inc(q_ready, 1)
                nb_ = (nkeys + CW - 1) // CW
                for h in range(H):
                    n, s = i * H + h, h % 2
                    dve.wait_ge(s_ready, n + 1)
                    for b in range(nb_):
                        ins = dve.reduce_max(part[:, b:b + 1], PS[b][:, 0:min(CW, nkeys)], AX.X)
                    ins.then_inc(m_ready, 1)
                    dve.wait_ge(m_ready, 2 * n + 1)
                    dve.reduce_max(mx[:, s:s + 1], part[:, 0:nb_], AX.X).then_inc(m_ready, 1)
                    dve.wait_ge(m_ready, 2 * n + 2)
                    dve.tensor_scalar(nb[:, s:s + 1], mx[:, s:s + 1], -SCALE, None, ALU.mult).then_inc(b_ready, 1)
                    dve.wait_ge(e_ready, n + 1)
                    dve.reduce_sum(sm[:, s:s + 1], es_[:, s, 0:nb_], AX.X).then_inc(r_ready, 1)
                    dve.wait_ge(r_ready, 2 * n + 1)
                    dve.reciprocal(ri[:, s:s + 1], sm[:, s:s + 1]).then_inc(r_ready, 1)
                    dve.wait_ge(r_ready, 2 * n + 2)
                    dve.tensor_scalar(pr[:, s, 0:nkeys], pr[:, s, 0:nkeys], ri[:, s:s + 1], None,
                                      ALU.mult).then_inc(p_ready, 1)
                    dve.wait_ge(t_ready, n + 1)
                    w = min(nkeys, 4 * P)
                    dve.wait_ge(o_ready, n)
                    ins = dve.tensor_copy(prT[:, 0:w], PS[3][:, 0:w])
                    if nkeys > 8 * P:
                        ins = dve.tensor_copy(prT[:, 8 * P:nkeys], PS[5][:, 0:nkeys - 8 * P])
                    ins.then_inc(tc1, 1)

            part = sb(c, "part", [P, 3])
            es_ = sb(c, "es", [P, 2, 3])

            @block.vector
            def _(dve):
                dve_tile(dve, 0, P)
                with dve.Fori(1, NT) as i:
                    dve_tile(dve, i, NKS)

            def act_tile(act, i, nkeys):
                for h in range(H):
                    n, s = i * H + h, h % 2
                    act.wait_ge(b_ready, n + 1)
                    act.wait_ge(t_ready, n - 1 if h else n)
                    for b in range((nkeys + CW - 1) // CW):
                        w = min(CW, nkeys)
                        ins = act.activation(pr[:, s, b * w:(b + 1) * w], PS[b][:, 0:w], ACT.Exp, bias=nb[:, s:s + 1],
                                             scale=SCALE, accum_out=es_[:, s, b:b + 1])
                    ins.then_inc(e_ready, 1)
                    act.wait_ge(t_ready, n + 1)
                    act.wait_ge(o_ready, n)
                    if nkeys > 4 * P:
                        act.activation(prT[:, 4 * P:8 * P], PS[4][:, :], ACT.Copy).then_inc(tc2, 1)
                    else:
                        act.sem_inc(tc2, 1)
                    act.wait_ge(o_ready, n + 1)
                    act.activation(boT[:, h, bass.ds(i * P, P)], PS[6][:, 0:P], ACT.Copy).then_inc(o_ev, 1)

            @block.scalar
            def _(act):
                act_tile(act, 0, P)
                with act.Fori(1, NT) as i:
                    act_tile(act, i, NKS)


def residual_one(nc, a, sb, sem, PS, ident, modc, sp1, aoT, boT, h2T, x1_dram, gate_dram):
    with ExitStack() as c:
        w_o = sb(c, "w_o", [P, DK, D])
        ln_g = sb(c, "ln1_g", [P, D])
        ln_b = sb(c, "ln1_b", [P, D])
        gate = sb(c, "gate1", [P, 2, D])
        gcol = sb(c, "gcol1", [P, 2, P])
        ones = sb(c, "ones1", [P, P])
        mc = sb(c, "mc", [P, DK, P])
        xt = sb(c, "xr", [P, D])
        r = sb(c, "r1", [P, D])
        y = sb(c, "y1", [P, D])
        x1 = sb(c, "x1", [P, D])
        st = sb(c, "st1", [P, 2, 6])
        mv = sb(c, "mv1", [P, 2])
        ve = sb(c, "ve1", [P, 1])
        sd = sb(c, "sd1", [P, 1])
        rs = sb(c, "rs1", [P, 1])
        wl, xl, ones_ready, g_col, g_mm, g_ev, g_out = (sem(f"c_{n}") for n in (
            "w", "x", "ones", "gcol", "gmm", "gev", "gout"))
        m_ready, mm_ready, xa_ready, ve_ready, sd_ready, chain, x1_ready, tr_ready, h_ev, st1, bank_read = (
            sem(f"c_{n}") for n in ("m", "mm", "xa", "ve", "sd", "chain", "x1", "tr", "hev", "st", "bank"))
        with nc.Block() as block:
            @block.sync
            def _(sp):
                sp.dma_start(w_o[:, :, :], a["w_o"]).then_inc(wl, 16)
                sp.dma_start(ln_g[:, :], a["ln1_g"]).then_inc(wl, 16)
                sp.dma_start(ln_b[:, :], a["ln1_b"]).then_inc(wl, 16)
                sp.dma_start(xt[:, :], a["x"][0:P, :]).then_inc(xl, 16)
                with sp.Fori(1, NT) as i:
                    sp.wait_ge(xa_ready, i)
                    sp.dma_start(xt[:, :], a["x"][bass.ds(i * P, P), :]).then_inc(xl, 16)
                    sp.wait_ge(x1_ready, i)
                    sp.dma_start(x1_dram[bass.ds(i * P - P, P), :], x1[:, :]).then_inc(st1, 16)
                sp.wait_ge(x1_ready, NT)
                sp.dma_start(x1_dram[T - P:T, :], x1[:, :]).then_inc(st1, 16)
                sp.wait_ge(st1, NT * 16)

            @block.gpsimd
            def _(pool):
                pool.memset(ones[:, :], 1.0).then_inc(ones_ready, 1)

            late = gate_rows(5 * DK, 0, gate, gcol, ones, modc, ident, PS, g_col, g_mm, g_ev)
            early = gate_rows(2 * DK, 1, gate, gcol, ones, modc, ident, PS, g_col, g_mm, g_ev)

            @block.tensor
            def _(pe):
                late[0](pe)
                early[0](pe)
                pe.wait_ge(wl, 48)

                def tile(i):
                    pe.wait_ge(m_ready, i + 1)
                    pe.wait_ge(bank_read, i)
                    for n in range(2):
                        for k in range(DK):
                            mm = pe.matmul(PS[n][:, :], mc[:, k, :], w_o[:, k, n * 512:(n + 1) * 512],
                                           start=(k == 0), stop=(k == DK - 1))
                    mm.then_inc(mm_ready, 1)
                    pe.wait_ge(x1_ready, i + 1)
                    pe.wait_ge(h_ev, i)
                    for k in range(DK):
                        mm = pe.transpose(PS[2 + k // 4][:, (k % 4) * P:(k % 4 + 1) * P], x1[:, k * P:(k + 1) * P],
                                          ident[:, :])
                    mm.then_inc(tr_ready, 1)

                tile(0)
                with pe.Fori(1, NT) as i:
                    tile(i)

            def act_tile(act, i, m):
                act.wait_ge(ve_ready, i + 1)
                act.activation(sd[:, :], ve[:, :], ACT.Sqrt).then_inc(sd_ready, 1)
                act.wait_ge(tr_ready, i + 1)
                for k in range(DK):
                    ins = act.activation(h2T[:, k, bass.ds(i * P, P)], PS[2 + k // 4][:, (k % 4) * P:(k % 4 + 1) * P],
                                         ACT.Identity, bias=modc[:, 3 * DK + k, m:m + 1],
                                         scale=sp1[:, 1, k, m:m + 1])
                ins.then_inc(h_ev, 1)

            @block.scalar
            def _(act):
                late[1](act)
                act.wait_ge(g_ev, 4)
                for n in range(NC + 1):
                    act.dma_start(gate_dram[n, :, :], gate[:, min(n, 1), :]).then_inc(g_out, 16)
                act.wait_ge(g_out, (NC + 1) * 16)
                early[1](act)
                act_tile(act, 0, 0)
                with act.Fori(1, NT) as i:
                    act_tile(act, i, 1)

            def dve_tile(dve, i, m):
                ch = Count(dve, chain)
                dve.wait_ge(mm_ready, i)
                dve.tensor_copy(mc[:, 0:G, :], aoT[:, :, bass.ds(i * P, P)])
                dve.tensor_copy(mc[:, G:DK, :], boT[:, :, bass.ds(i * P, P)]).then_inc(m_ready, 1)
                dve.wait_ge(mm_ready, i + 1)
                for n in range(2):
                    sl = slice(n * 512, (n + 1) * 512)
                    ins = dve.tensor_tensor(r[:, sl], gate[:, m, sl], PS[n][:, :], ALU.mult)
                ins.then_inc(bank_read, 1)
                dve.wait_ge(bank_read, i + 1)
                dve.wait_ge(xl, (i + 1) * 16)
                dve.scalar_tensor_tensor(y[:, :], xt[:, :], ALPHA, r[:, :], ALU.mult, ALU.add).then_inc(xa_ready, 1)
                dve.wait_ge(xa_ready, i + 1)
                for n in range(2):
                    ins = dve.bn_stats(st[:, n, :], y[:, n * 512:(n + 1) * 512])
                ch.step(ins)
                ch.step(dve.bn_aggr(mv[:, :], st[:, :, :].rearrange("p a b -> p (a b)")))
                dve.tensor_scalar(ve[:, :], mv[:, 1:2], EPS, None, ALU.add).then_inc(ve_ready, 1)
                dve.wait_ge(sd_ready, i + 1)
                ch.step(dve.reciprocal(rs[:, :], sd[:, :]))
                ch.step(dve.tensor_scalar(r[:, :], y[:, :], mv[:, 0:1], rs[:, 0:1], ALU.subtract, ALU.mult))
                ch.step(dve.tensor_tensor(y[:, :], r[:, :], ln_g[:, :], ALU.mult))
                dve.wait_ge(tr_ready, i)
                dve.wait_ge(st1, i * 16)
                dve.tensor_tensor(x1[:, :], y[:, :], ln_b[:, :], ALU.add).then_inc(x1_ready, 1)
                dve.wait_ge(x1_ready, i + 1)

            @block.vector
            def _(dve):
                dve.wait_ge(ones_ready, 1)
                late[2](dve)
                early[2](dve)
                dve.wait_ge(wl, 48)
                dve_tile(dve, 0, 0)
                with dve.Fori(1, NT) as i:
                    dve_tile(dve, i, 1)


def gate_rows(at, before, gate, gcol, ones, modc, ident, PS, g_col, g_mm, g_ev):
    n0, q0 = before * 2 * DK, before * 4
    def pe_part(pe):
        for n in range(2 * DK):
            m, k = divmod(n, DK)
            pe.wait_ge(g_col, n0 + n + 1)
            if n % 4 == 0 and n0 + n >= 4:
                pe.wait_ge(g_ev, q0 + n // 4)
            pe.matmul(PS[7][:, (n % 4) * P:(n % 4 + 1) * P], gcol[:, n % 2, :], ident[:, :],
                      start=True, stop=True).then_inc(g_mm, 1)

    def act_part(act):
        for q in range(2 * DK // 4):
            act.wait_ge(g_mm, n0 + 4 * q + 4)
            m, half = divmod(q, 2)
            act.activation(gate[:, m, half * 512:(half + 1) * 512], PS[7][:, :], ACT.Copy).then_inc(g_ev, 1)

    def dve_part(dve):
        for n in range(2 * DK):
            m, k = divmod(n, DK)
            if n0 + n >= 2:
                dve.wait_ge(g_mm, n0 + n - 1)
            dve.tensor_scalar(gcol[:, n % 2, :], ones[:, :], modc[:, at + k, m:m + 1], None,
                              ALU.mult).then_inc(g_col, 1)
        dve.wait_ge(g_ev, q0 + 4)

    return pe_part, act_part, dve_part


def experts(nc, a, sb, sem, PS, ident, big, h2T, x1_dram, g_dram, gate_dram):
    NEt = NE // P
    S = 8
    U = 8
    UNITS = CW // U
    FILLS = 2 * HS + CT + 2 * UNITS
    F_HEAD, F_SCAT = 2 * HS, 2 * HS + CT
    ROUTE = [("list", HS // S), ("head", CT * PH // S), ("scatter", UNITS // S)]
    BUSY = sum(n for _, n in ROUTE)
    PLAN = [ROUTE + [("plain", NEt // S - BUSY)],
            [("norm", 1)] + ROUTE + [("plain", NEt // S - BUSY - 1)],
            [("norm", 1), ("plain", NEt // S - 1)]]
    with ExitStack() as c:
        zero = sb(c, "zero", [P, 512], F32R)
        hR = sb(c, "hR", [P, DK, CW], F32R)
        hL = sb(c, "hL", [P, DK, CW], F32R)
        uw = sb(c, "uw", [P, 2, DK, P])
        vw = sb(c, "vw", [P, 2, D])
        uR = sb(c, "uR", [P, 2, DK, P], F32R)
        uL = sb(c, "uL", [P, 2, DK, P], F32R)
        vR = sb(c, "vR", [P, 2, D], F32R)
        vL = sb(c, "vL", [P, 2, D], F32R)
        gw = sb(c, "gw", [P, 2, CB, UB, TB])
        ga = sb(c, "ga", [P, CW])
        cR = sb(c, "cR", [P, 2, CW], F32R)
        cL = sb(c, "cL", [P, 2, CW], F32R)
        stage = sb(c, "stage", [P, 2, NKEY, TB])
        flat = stage[:, :, :, :].rearrange("p b i t -> p (b i t)")
        ln_g, ln_b, gate_0, gate_1, x1 = (flat[:, n * D:(n + 1) * D] for n in range(5))
        r = flat[:, 5 * D:(5 + CT) * D].rearrange("p (t d) -> p t d", t=CT)
        wq = sb(c, "wq", [P, 2, DK + 1, P])
        qs = sb(c, "qs", [P, CW])
        s = sb(c, "s", [P, 2, CT, NKEY])
        tv = sb(c, "tv", [P, CT, TOPK])
        ti = sb(c, "ti", [P, CT, TOPK], U32)
        top = sb(c, "top", [P, CT, HS, TOPK])
        itf = sb(c, "itf", [P, CT, HS, TOPK])
        cand = sb(c, "cand", [P, TOPK * TOPK])
        fs = sb(c, "fs", [P, PH, TOPK])
        fp = sb(c, "fp", [P, PH, TOPK], U32)
        ab = sb(c, "ab", [P, 2, TOPK], U32)
        abf = sb(c, "abf", [P, 2, TOPK])
        eq = sb(c, "eq", [P, 2, TOPK, TOPK])
        i16 = sb(c, "i16", [P, TOPK])
        out = sb(c, "out", [P, 3, PAIRS])
        ex = sb(c, "ex", [P, PH, TOPK])
        sm = sb(c, "smr", [P, PH])
        ri = sb(c, "rir", [P, PH])
        idxT = sb(c, "idxT", [P, 3, CW])
        iota = sb(c, "iota", [P, P])
        idc = sb(c, "idc", [P, 3, U])
        ra = big[:, DK * T:DK * T + U * P].rearrange("p (t i) -> p t i", t=U)
        cb = sb(c, "cb", [P, U, P])
        st = sb(c, "st2", [P, 2, 6])
        mv = sb(c, "mv2", [P, 2])
        ve = sb(c, "ve2", [P, 1])
        sd = sb(c, "sd2", [P, 1])
        rs = sb(c, "rs2", [P, 1])

        ul, vl, gl, wl, stored_g = ([sem(f"f_{n}{k}") for k in range(2)] for n in ("u", "v", "g", "wq", "stg"))
        ln_in, x1_in, y_out = sem("f_ln"), sem("f_x1"), sem("f_yout")
        const, h_r, h_l, u_r, u_l, v_r, v_l = (sem(f"f_{n}") for n in ("const", "hr", "hl", "ur", "ul", "vr", "vl"))
        a_mm, a_ev, c_f, c_r, c_l, v_mm, acc_done, acc_read = (sem(f"f_{n}") for n in (
            "amm", "aev", "cf", "cr", "cl", "vmm", "acc", "accr"))
        filled, emptied, listed, e_in, e_out, o_ready, hot, idc_in = (sem(f"f_{n}") for n in (
            "fill", "empty", "listed", "ein", "eout", "o", "hot", "idc"))
        chain, x1_used, ve_ready, sd_ready, n_ready, y_mul, y_ready = (sem(f"f_{n}") for n in (
            "chain", "x1u", "ve", "sd", "n", "ym", "y"))
        heads, picked = sem("f_heads"), sem("f_picked")
        A, E, ACC = PS[0], PS[1], PS[2:8]

        def schedule(eng, n, step):
            at = 0
            for kind, count in PLAN[n]:
                last = at + count == NEt // S
                if count - last > 1:
                    with eng.Fori(0, count - last) as it:
                        for q in range(S):
                            step(kind, it, q, (it + at) * S + q)
                elif count - last == 1:
                    for q in range(S):
                        step(kind, 0, q, at * S + q)
                at += count
            for q in range(S):
                step("plain", 0, q, NEt - S + q)

        def routed(eng, step):
            for kind, count in ROUTE:
                with eng.Fori(0, count) as it:
                    for q in range(S):
                        step(kind, it, q)

        def fixed(m):
            return isinstance(m, int)

        with nc.Block() as block:
            @block.sync
            def _(sp):
                for b in range(2):
                    sp.sem_inc(stored_g[b], 16)

                def load_u(t, tile):
                    sp.dma_start(uw[:, t, :, :], a["u"][tile, :, :, :]).then_inc(ul[t], 16)

                def load_v(t, tile):
                    sp.dma_start(vw[:, t, :], a["v"][tile, :, :]).then_inc(vl[t], 16)

                def load_g(t, n, batch):
                    sp.dma_start(gw[:, t, :, :, :].rearrange("p c u t -> p c (u t)"),
                                 g_dram[n * CB:(n + 1) * CB, :, bass.ds(batch * UB, UB), :].rearrange(
                                     "c p u t -> p c (u t)")).then_inc(gl[t], 16)

                def load_list(t, l):
                    sp.dma_start(wq[:, t, :, :], a["w_pq"][l, :, :, :]).then_inc(wl[t], 16)

                def route(kind, it, q, cn):
                    f0 = cn * FILLS
                    if kind == "list":
                        sp.wait_ge(emptied, (it * S + q) * 2 + f0 + 1)
                        load_list((q + 1) % 2, it * S + q + 1 if q < S - 1 else it * -S + S)
                    if kind == "scatter" and q % 4 == 3:
                        b = q // 4
                        sp.wait_ge(emptied, (it * S + q + 1) * 2 + f0 + F_SCAT + 1)
                        sp.dma_start(g_dram[it * 2 + (cn * CB + b), :, :, :],
                                     stage[:, b, :, :]).then_inc(stored_g[b], 16)

                def weights_stored(cn):
                    for b in range(2):
                        sp.wait_ge(stored_g[b], ((cn + 1) * (CB // 2) + 1) * 16)

                def load_x1(i):
                    if i:
                        sp.wait_ge(x1_used, i)
                    sp.dma_start(x1, x1_dram[i * P:(i + 1) * P, :]).then_inc(x1_in, 16)

                def store_y(i):
                    sp.wait_ge(y_ready, i + 1)
                    sp.dma_start(a["y"][i * P:(i + 1) * P, :], r[:, i % CT, :]).then_inc(y_out, 16)

                def step(n):
                    def at(kind, it, q, m):
                        g = m + n * NEt
                        left = NC * NEt - g if fixed(m) else NEt
                        if left > 3:
                            sp.wait_ge(u_l, g + 2)
                            load_u((q + 1) % 2, m + 3 if not fixed(m) else (m + 3) % NEt)
                        if left > 2:
                            sp.wait_ge(v_l, g + 1)
                            load_v(q % 2, m + 2 if not fixed(m) else (m + 2) % NEt)
                        if q % UB == 0:
                            b = q // UB
                            sp.wait_ge(c_f, g + 1)
                            if not fixed(m):
                                load_g(1 - b, n, (it + (base[n, kind])) * (S // UB) + b + 1)
                            elif m + UB < NEt:
                                load_g(1 - b, n, m // UB + 1)
                            elif n + 1 < NC:
                                load_g(1 - b, n + 1, 0)
                        if kind == "norm" and q % 2 == 0 and q // 2 < CT - 1:
                            load_x1((n - 1) * CT + q // 2 + 1)
                        if kind == "norm" and q % 2 == 1 and q // 2 < CT:
                            store_y((n - 1) * CT + q // 2)
                        if n + 1 < NC:
                            route(kind, it, q, n + 1)
                        if fixed(m) and m == NEt - S:
                            weights_stored(min(n + 1, NC - 1))
                            for dst, src in ((ln_g, a["ln2_g"]), (ln_b, a["ln2_b"]), (gate_0, gate_dram[n, :, :]),
                                             (gate_1, gate_dram[NC, :, :])):
                                sp.dma_start(dst, src).then_inc(ln_in, 16)
                            load_x1(n * CT)
                    return at

                base = {}
                for n in range(NC):
                    k = 0
                    for kind, count in PLAN[n]:
                        base[n, kind] = k
                        k += count
                load_list(0, 0)
                for t in range(2):
                    load_u(t, t)
                    load_v(t, t)
                sp.wait_ge(u_l, 1)
                load_u(0, 2)
                routed(sp, lambda kind, it, q: route(kind, it, q, 0))
                weights_stored(0)
                load_g(0, 0, 0)
                for n in range(NC):
                    schedule(sp, n, step(n))
                for t in range(CT):
                    i = (NC - 1) * CT + t
                    if t + 1 < CT:
                        load_x1(i + 1)
                    store_y(i)
                sp.wait_ge(y_out, NT * 16)
                sp.wait_ge(wl[0], (NC * HS // 2 + 1) * 16)

            @block.gpsimd
            def _(pool):
                pool.memset(zero[:, :].bitcast(F32), 0.0).then_inc(const, 1)
                pool.iota(i16[:, :], pattern=[[1, TOPK]], base=0, channel_multiplier=0,
                          allow_small_or_imprecise_dtypes=True).then_inc(const, 1)
                pool.iota(iota[:, :], pattern=[[1, P]], base=0, channel_multiplier=0,
                          allow_small_or_imprecise_dtypes=True).then_inc(const, 1)

                def split_v(t, g):
                    pool.wait_ge(v_r, g + 1)
                    pool.tensor_tensor(vL[:, t, :], vw[:, t, :], vR[:, t, :].bitcast(F32),
                                       ALU.subtract).then_inc(v_l, 1)

                def norm(i):
                    y = r[:, i % CT, :]
                    pool.wait_ge(n_ready, i + 1)
                    pool.tensor_tensor(y, y, ln_g, ALU.mult).then_inc(y_mul, 1)
                    pool.wait_ge(y_mul, i + 1)
                    pool.tensor_tensor(y, y, ln_b, ALU.add).then_inc(y_ready, 1)

                def step(n):
                    def at(kind, it, q, m):
                        g = m + n * NEt
                        if not fixed(m) or g + 1 < NC * NEt:
                            split_v((q + 1) % 2, g + 1)
                        if kind == "norm" and q % 2 == 0 and q // 2 < CT:
                            norm((n - 1) * CT + q // 2)
                    return at

                split_v(0, 0)
                for n in range(NC):
                    schedule(pool, n, step(n))
                for t in range(CT):
                    norm((NC - 1) * CT + t)

            @block.scalar
            def _(act):
                act.sem_inc(emptied, 1)

                def split_u(t, g, loads):
                    act.wait_ge(ul[t], loads * 16)
                    act.activation(uR[:, t, :, :], uw[:, t, :, :], ACT.Copy).then_inc(u_r, 1)

                def split_v(t, loads):
                    act.wait_ge(vl[t], loads * 16)
                    act.activation(vR[:, t, :], vw[:, t, :], ACT.Copy).then_inc(v_r, 1)

                def split_h(n):
                    act.activation(hR[:, :, :], h2T[:, :, n * CW:(n + 1) * CW], ACT.Copy).then_inc(h_r, 1)

                def gelu(g):
                    act.wait_ge(a_mm, g + 1)
                    if not fixed(g) or g:
                        act.wait_ge(c_l, g)
                    act.activation(ga[:, :], A[:, 0:CW], ACT.Gelu).then_inc(a_ev, 1)

                def route(kind, it, q, cn):
                    f0 = cn * FILLS
                    if kind == "list":
                        f = (it * S + q) * 2 + f0
                        act.wait_ge(filled, f + 1)
                        act.activation(qs[:, :], E[:, 0:CW], ACT.Copy).then_inc(emptied, 1)
                        act.wait_ge(filled, f + 2)
                        act.wait_ge(listed, it * S + q + (cn * HS + 1))
                        act.activation(s[:, q % 2, :, :], E[:, 0:CW].rearrange("p (t k) -> p t k", t=CT),
                                       ACT.Copy).then_inc(emptied, 1)
                    if kind == "head" and q == S - 1:
                        act.wait_ge(e_in, it + cn * CT + 1)
                        act.activation(ex[:, :, :], fs[:, :, :], ACT.Exp).then_inc(e_out, 1)
                        act.wait_ge(filled, it + (f0 + F_HEAD + 1))
                        act.activation(idxT[:, :, bass.ds(it * P, P)],
                                       E[:, 0:3 * P].rearrange("p (w t) -> p w t", w=3), ACT.Copy).then_inc(emptied, 1)
                    if kind == "scatter":
                        b = q // 4
                        if q % 4 == 0:
                            act.wait_ge(stored_g[b], (it + cn * (CB // 2) + 1) * 16)
                        for e in range(2):
                            act.wait_ge(filled, (it * S + q) * 2 + (f0 + F_SCAT + e + 1))
                            at = (q % 4) * U + e * (U // 2)
                            act.activation(stage[:, b, :, at:at + U // 2].rearrange("p i t -> p t i"),
                                           E[:, :].rearrange("p (t i) -> p t i", t=U // 2),
                                           ACT.Copy).then_inc(emptied, 1)

                def norm(i):
                    act.wait_ge(ve_ready, i + 1)
                    act.activation(sd[:, :], ve[:, :], ACT.Sqrt).then_inc(sd_ready, 1)

                def step(n):
                    def at(kind, it, q, m):
                        g = m + n * NEt
                        half = (g - q) // 2 if fixed(m) else (it + base[n, kind]) * (S // 2) + n * NEt // 2
                        left = NC * NEt - g if fixed(m) else NEt
                        if kind == "scatter" and q == 0 and n:
                            act.wait_ge(y_out, n * CT * 16)
                        if fixed(m) and m == NEt - 1 and n + 1 < NC:
                            act.wait_ge(a_mm, g + 1)
                            split_h(n + 1)
                        if left > 2:
                            act.wait_ge(a_mm, g + 1)
                            split_u(q % 2, g + 2, half + (q + 2) // 2 + 1)
                        if left > 1:
                            act.wait_ge(v_mm, g + 1)
                            split_v((q + 1) % 2, half + (q + 1) // 2 + 1)
                        if not fixed(m) or m < NEt - 1:
                            gelu(g + 1)
                        if kind == "norm" and q % 2 == 0 and q // 2 < CT:
                            norm((n - 1) * CT + q // 2)
                        if n + 1 < NC:
                            route(kind, it, q, n + 1)
                    return at

                base = {}
                for n in range(NC):
                    k = 0
                    for kind, count in PLAN[n]:
                        base[n, kind] = k
                        k += count
                split_u(0, 0, 1)
                split_u(1, 1, 1)
                split_v(0, 1)
                split_h(0)
                routed(act, lambda kind, it, q: route(kind, it, q, 0))
                for n in range(NC):
                    gelu(n * NEt)
                    schedule(act, n, step(n))
                for t in range(CT):
                    norm((NC - 1) * CT + t)

            @block.tensor
            def _(pe):
                pe.sem_inc(v_mm, 1)
                pe.wait_ge(const, 3)

                def hidden(t, g):
                    pe.wait_ge(u_l, g + 1)
                    if not fixed(g) or g:
                        pe.wait_ge(a_ev, g)
                    for k in range(DK):
                        for w, h in ((uR, hR), (uR, hL), (uL, hR)):
                            mm = pe.matmul(A[:, 0:CW], w[:, t, k, :], h[:, k, :],
                                           start=(k == 0 and w is uR and h is hR),
                                           stop=(k == DK - 1 and w is uL))
                    mm.then_inc(a_mm, 1)

                def down(t, tiles):
                    for tt in tiles:
                        for w, v in ((cR, vR), (cR, vL), (cL, vR)):
                            for half in range(2):
                                mm = pe.matmul(ACC[2 * tt + half][:, :], w[:, t, tt * P:(tt + 1) * P],
                                               v[:, t, half * 512:(half + 1) * 512], start=False, stop=False,
                                               skip_group_check=True)
                    return mm

                def route(kind, it, q, cn, e):
                    f0 = cn * FILLS
                    if kind == "list":
                        f = (it * S + q) * 2 + (f0 + e)
                        pe.wait_ge(emptied, f + 1)
                        if e == 0:
                            pe.wait_ge(wl[q % 2], (it * (S // 2) + (cn * (HS // 2) + q // 2 + 1)) * 16)
                            for k in range(DK):
                                mm = pe.matmul(E[:, 0:CW], wq[:, q % 2, k, :], h2T[:, k, cn * CW:(cn + 1) * CW],
                                               start=(k == 0), stop=(k == DK - 1))
                        else:
                            for t in range(CT):
                                mm = pe.matmul(E[:, t * NKEY:(t + 1) * NKEY], qs[:, t * P:(t + 1) * P],
                                               wq[:, q % 2, DK, :], start=True, stop=True)
                        mm.then_inc(filled, 1)
                    if kind == "head" and q == S - 1 and e == 1:
                        pe.wait_ge(emptied, it + (f0 + F_HEAD + 1))
                        pe.wait_ge(o_ready, it + (cn * CT + 1))
                        for w in range(3):
                            mm = pe.transpose(E[:, w * P:(w + 1) * P], out[:, w, :], ident[:, :])
                        mm.then_inc(filled, 1)
                    if kind == "scatter":
                        pe.wait_ge(emptied, (it * S + q) * 2 + (f0 + F_SCAT + e + 1))
                        pe.wait_ge(hot, (it * S + q) * 2 + (cn * 2 * UNITS + e + 3))
                        for t in range(U // 2):
                            k = e * (U // 2) + t
                            mm = pe.matmul(E[:, t * P:(t + 1) * P], cb[:, k, :], ra[:, k, :], start=True, stop=True)
                        mm.then_inc(filled, 1)

                def step(n):
                    def at(kind, it, q, m):
                        g = m + n * NEt
                        if not fixed(m) or m < NEt - 1:
                            hidden((q + 1) % 2, g + 1)
                        pe.wait_ge(c_l, g + 1)
                        pe.wait_ge(v_l, g + 1)
                        down(q % 2, (0,))
                        if n + 1 < NC:
                            route(kind, it, q, n + 1, 0)
                        down(q % 2, range(1, CT)).then_inc(v_mm, 1)
                        if n + 1 < NC:
                            route(kind, it, q, n + 1, 1)
                    return at

                def both(kind, it, q):
                    route(kind, it, q, 0, 0)
                    route(kind, it, q, 0, 1)

                routed(pe, both)
                for n in range(NC):
                    pe.wait_ge(h_l, n + 1)
                    hidden(0, n * NEt)
                    if n:
                        pe.wait_ge(acc_read, n)
                    for bank in ACC:
                        pe.matmul(bank[:, :], zero[:, 0:P], zero[:, :], start=True, stop=False, skip_group_check=True)
                    schedule(pe, n, step(n))
                    for bank in ACC:
                        mm = pe.matmul(bank[:, :], zero[:, 0:P], zero[:, :], start=False, stop=True,
                                       skip_group_check=True)
                    mm.then_inc(acc_done, 1)

            @block.vector
            def _(dve):
                dve.sem_inc(listed, 2)
                dve.wait_ge(const, 3)

                def split_u(t, g):
                    dve.wait_ge(u_r, g + 1)
                    dve.tensor_tensor(uL[:, t, :, :], uw[:, t, :, :], uR[:, t, :, :].bitcast(F32),
                                      ALU.subtract).then_inc(u_l, 1)

                def split_h(n):
                    dve.wait_ge(h_r, n + 1)
                    dve.tensor_tensor(hL[:, :, :], h2T[:, :, n * CW:(n + 1) * CW], hR[:, :, :].bitcast(F32),
                                      ALU.subtract).then_inc(h_l, 1)

                def weigh(t, g, q, loads):
                    if loads is not None:
                        dve.wait_ge(gl[loads[0]], loads[1] * 16)
                    slot = (q // UB) % 2
                    dve.wait_ge(a_ev, g + 1)
                    gv = ga[:, :].rearrange("p (c t) -> p c t", c=CB)
                    dve.tensor_tensor(gv, gv, gw[:, slot, :, q % UB, :], ALU.mult).then_inc(c_f, 1)
                    dve.wait_ge(v_mm, g)
                    dve.wait_ge(c_f, g + 1)
                    dve.tensor_copy(cR[:, t, :], ga[:, :]).then_inc(c_r, 1)
                    dve.wait_ge(c_r, g + 1)
                    dve.tensor_tensor(cL[:, t, :], ga[:, :], cR[:, t, :].bitcast(F32), ALU.subtract).then_inc(c_l, 1)

                def route_list(it, q, cn):
                    dve.wait_ge(emptied, (it * S + q) * 2 + (cn * FILLS + 3))
                    ch = Count(dve, chain)
                    for half in range(2):
                        sl = slice(half * 8, half * 8 + 8)
                        for t in range(CT):
                            ins = dve.max(tv[:, t, sl], s[:, q % 2, t, :])
                        ch.step(ins)
                        for t in range(CT):
                            ins = dve.max_index(ti[:, t, sl], tv[:, t, sl], s[:, q % 2, t, :])
                        ch.step(ins)
                        if half == 0:
                            for t in range(CT):
                                ins = dve.match_replace(s[:, q % 2, t, :], tv[:, t, sl], s[:, q % 2, t, :], LOW)
                            ch.step(ins)
                    dve.tensor_copy(top[:, :, it * S + q, :], tv[:, :, :])
                    dve.tensor_copy(itf[:, :, it * S + q, :], ti[:, :, :]).then_inc(listed, 1)
                    dve.wait_ge(listed, it * S + q + (cn * HS + 3))

                def route_head(t, h, cn):
                    dve.tensor_tensor(cand[:, :].rearrange("p (a b) -> p a b", a=TOPK),
                                      top[:, t, 2 * h, :].rearrange("p (a o) -> p a o", o=1).to_broadcast(
                                          [P, TOPK, TOPK]),
                                      top[:, t, 2 * h + 1, :].rearrange("p (o b) -> p o b", o=1).to_broadcast(
                                          [P, TOPK, TOPK]), ALU.add).then_inc(heads, 1)
                    dve.wait_ge(heads, (t * PH + h) + (cn * CT * PH + 1))
                    ch = Count(dve, chain)
                    for half in range(2):
                        sl = slice(half * 8, half * 8 + 8)
                        ch.step(dve.max(fs[:, h, sl], cand[:, :]))
                        ch.step(dve.max_index(fp[:, h, sl], fs[:, h, sl], cand[:, :]))
                        if half == 0:
                            ch.step(dve.match_replace(cand[:, :], fs[:, h, sl], cand[:, :], LOW))
                    dve.tensor_scalar(ab[:, 0, :], fp[:, h, :], 4, None, ALU.logical_shift_right)
                    ch.step(dve.tensor_scalar(ab[:, 1, :], fp[:, h, :], TOPK - 1, None, ALU.bitwise_and))
                    ch.step(dve.tensor_copy(abf[:, :, :], ab[:, :, :]))
                    ch.step(dve.tensor_tensor(
                        eq[:, :, :, :],
                        i16[:, :].rearrange("p (a b k) -> p a b k", a=1, b=1).to_broadcast([P, 2, TOPK, TOPK]),
                        abf[:, :, :].rearrange("p w (k o) -> p w k o", o=1).to_broadcast([P, 2, TOPK, TOPK]),
                        ALU.is_equal))
                    ch.step(dve.tensor_tensor(
                        eq[:, :, :, :], eq[:, :, :, :],
                        itf[:, t, 2 * h:2 * h + 2, :].rearrange("p w (o k) -> p w o k", o=1).to_broadcast(
                            [P, 2, TOPK, TOPK]), ALU.mult))
                    if h == 0:
                        dve.wait_ge(emptied, t + (cn * FILLS + F_HEAD + 1))
                    dve.tensor_reduce(out[:, 0:2, h * TOPK:(h + 1) * TOPK], eq[:, :, :, :], axis=AX.X,
                                      op=ALU.add).then_inc(picked, 1)
                    dve.wait_ge(picked, (t * PH + h) + (cn * CT * PH + 1))

                def route_softmax(t, cn):
                    ch = Count(dve, chain)
                    ch.step(dve.tensor_copy(sm[:, :], fs[:, :, 0]))
                    dve.tensor_tensor(fs[:, :, :], fs[:, :, :],
                                      sm[:, :].rearrange("p (h o) -> p h o", o=1).to_broadcast([P, PH, TOPK]),
                                      ALU.subtract).then_inc(e_in, 1)
                    dve.wait_ge(e_out, t + (cn * CT + 1))
                    ch.step(dve.tensor_reduce(sm[:, :], ex[:, :, :], axis=AX.X, op=ALU.add))
                    ch.step(dve.reciprocal(ri[:, :], sm[:, :]))
                    dve.tensor_tensor(out[:, 2, :].rearrange("p (h k) -> p h k", h=PH), ex[:, :, :],
                                      ri[:, :].rearrange("p (h o) -> p h o", o=1).to_broadcast([P, PH, TOPK]),
                                      ALU.mult).then_inc(o_ready, 1)
                    dve.wait_ge(o_ready, t + (cn * CT + 1))

                def route_scatter(it, q, cn):
                    unit = it * S + q
                    f = unit * 2 + (cn * FILLS + F_SCAT)
                    dve.wait_ge(emptied, cn * FILLS + F_SCAT + 1)
                    dve.wait_ge(hot, unit * 2 + (cn * 2 * UNITS + 2))
                    dve.tensor_copy(idc[:, :, :], idxT[:, :, bass.ds(unit * U, U)]).then_inc(idc_in, 1)
                    dve.wait_ge(idc_in, unit + (cn * UNITS + 1))
                    for e in range(2):
                        dve.wait_ge(filled, f + (e - 1))
                        for k in range(e * (U // 2), (e + 1) * (U // 2)):
                            dve.tensor_scalar(ra[:, k, :], iota[:, :], idc[:, 0, k:k + 1], None, ALU.is_equal)
                            ins = dve.tensor_scalar(cb[:, k, :], iota[:, :], idc[:, 1, k:k + 1],
                                                    idc[:, 2, k:k + 1], ALU.is_equal, ALU.mult)
                        ins.then_inc(hot, 1)

                def norm(i):
                    y = r[:, i % CT, :]
                    ch = Count(dve, chain)
                    dve.wait_ge(x1_in, (i + 1) * 16)
                    dve.scalar_tensor_tensor(y, x1, ALPHA, y, ALU.mult, ALU.add).then_inc(x1_used, 1)
                    dve.wait_ge(x1_used, i + 1)
                    for half in range(2):
                        ins = dve.bn_stats(st[:, half, :], y[:, half * 512:(half + 1) * 512])
                    ch.step(ins)
                    ch.step(dve.bn_aggr(mv[:, :], st[:, :, :].rearrange("p a b -> p (a b)")))
                    dve.tensor_scalar(ve[:, :], mv[:, 1:2], EPS, None, ALU.add).then_inc(ve_ready, 1)
                    dve.wait_ge(sd_ready, i + 1)
                    ch.step(dve.reciprocal(rs[:, :], sd[:, :]))
                    dve.tensor_scalar(y, y, mv[:, 0:1], rs[:, 0:1], ALU.subtract, ALU.mult).then_inc(n_ready, 1)
                    dve.wait_ge(n_ready, i + 1)

                def read_sums(n):
                    dve.wait_ge(acc_done, n + 1)
                    dve.wait_ge(ln_in, (n + 1) * 64)
                    for t in range(CT):
                        gate = gate_1 if t else gate_0
                        for half in range(2):
                            sl = slice(half * 512, (half + 1) * 512)
                            ins = dve.tensor_tensor(r[:, t, sl], gate[:, sl], ACC[2 * t + half][:, :], ALU.mult)
                    ins.then_inc(acc_read, 1)
                    dve.wait_ge(acc_read, n + 1)

                def route(kind, it, q, cn):
                    if kind == "list":
                        route_list(it, q, cn)
                    if kind == "head":
                        route_head(it, q, cn)
                        if q == S - 1:
                            route_softmax(it, cn)
                    if kind == "scatter":
                        route_scatter(it, q, cn)

                def step(n):
                    def at(kind, it, q, m):
                        g = m + n * NEt
                        if not fixed(m) or g + 2 < NC * NEt:
                            split_u(q % 2, g + 2)
                        if n + 1 < NC and kind in ("head", "scatter"):
                            route(kind, it, q, n + 1)
                        if not fixed(m) or m < NEt - 1:
                            loads = None
                            if (q + 1) % UB == 0:
                                b = ((q + 1) // UB) % 2
                                at_ = (m + 1) // S if fixed(m) else it + base[n, kind] + (q + 1) // S
                                loads = (b, at_ + (n * (NEt // S) + 1))
                            weigh((q + 1) % 2, g + 1, q + 1, loads)
                        if kind == "norm" and q % 2 == 0 and q // 2 < CT:
                            norm((n - 1) * CT + q // 2)
                        if n + 1 < NC and kind == "list":
                            route(kind, it, q, n + 1)
                    return at

                base = {}
                for n in range(NC):
                    k = 0
                    for kind, count in PLAN[n]:
                        base[n, kind] = k
                        k += count
                dve.sem_inc(hot, 2)
                split_u(0, 0)
                split_u(1, 1)
                split_h(0)
                routed(dve, lambda kind, it, q: route(kind, it, q, 0))
                for n in range(NC):
                    weigh(0, n * NEt, 0, (0, n * (NEt // S) + 1))
                    schedule(dve, n, step(n))
                    if n + 1 < NC:
                        split_h(n + 1)
                    read_sums(n)
                for t in range(CT):
                    norm((NC - 1) * CT + t)


SHAPES = {"y": [T, D], "new_ckv": [SEQ, KVR], "new_krope": [SEQ, ROPE]}


def kernel(x_prompt, x_sample, cache_ckv, cache_krope, c, c_ctx, w_mod, b_mod, w_in, w_s, b_s,
           g_q, w_qb, g_kv, w_kvb, w_o, ln1_g, ln1_b, w_pq, sub_keys, u_tab, v_tab, ln2_g, ln2_b):
    import concourse.bacc as bacc
    from concourse.bass_utils import run_bass_kernel_spmd

    def rows(w, k):
        return w.reshape(k, P, -1).transpose(1, 0, 2)

    def every_row(v):
        return np.broadcast_to(v.reshape(1, -1), (P, v.size))

    n = {k: np.asarray(v) for k, v in dict(locals()).items() if not callable(v)}
    x = np.concatenate([n["x_prompt"][0], n["x_sample"][0]], axis=0)
    wqb = n["w_qb"][0].reshape(QR, H, NOPE + ROPE)
    wkvb = n["w_kvb"][0].reshape(KVR, H, NOPE + VD)
    f = ROPE // 4
    freq = (1.0 / (np.float32(10000.0) ** (np.arange(f, dtype=np.float32) / np.float32(f)))).astype(np.float32)
    tok = np.arange(DEC)
    ang = [np.float32(v)[:, None] * freq[None, :] for v in ((tok // GRID_W).astype(np.float32),
                                                            (tok % GRID_W).astype(np.float32))]
    cos, sin = [np.cos(v).astype(np.float32) for v in ang], [np.sin(v).astype(np.float32) for v in ang]
    table = np.zeros((NT, P, 2, ROPE), np.float32)
    table[1:, :, 0] = np.concatenate([cos[0], cos[0], cos[1], cos[1]], 1).reshape(NT - 1, P, ROPE)
    table[1:, :, 1] = np.concatenate([-sin[0], sin[0], -sin[1], sin[1]], 1).reshape(NT - 1, P, ROPE)
    arrays = {
        "x": x,
        "xT": x.reshape(NT, P, DK, P).transpose(0, 3, 2, 1),
        "cond": np.stack([n["c_ctx"].reshape(DK, P), n["c"].reshape(DK, P)], -1).transpose(1, 0, 2),
        "w_mod": n["w_mod"][0].reshape(DK, P, 6 * DK, P).transpose(2, 1, 0, 3),
        "b_mod": n["b_mod"][0].reshape(6 * DK, P).T,
        "w_in": rows(n["w_in"][0], DK),
        "w_s": n["w_s"][0].transpose(2, 0, 1),
        "b_s": n["b_s"][0].T,
        "g_q": n["g_q"][0].reshape(QK, P).T,
        "g_kv": every_row(n["g_kv"][0]),
        "w_qn": rows(wqb[:, :, :NOPE].reshape(QR, -1), QK),
        "w_qr": rows(wqb[:, :, NOPE:].reshape(QR, -1), QK),
        "w_kn": rows(wkvb[:, :, :NOPE].reshape(KVR, -1), KK),
        "w_v": rows(wkvb[:, :, NOPE:].reshape(KVR, -1), KK),
        "cckT": rows(n["cache_ckv"][0, 0].T, KK),
        "ckrT": n["cache_krope"][0, 0].T,
        "rot": table,
        "w_o": rows(n["w_o"][0], DK),
        "ln1_g": every_row(n["ln1_g"][0]),
        "ln1_b": every_row(n["ln1_b"][0]),
        "w_pq": np.concatenate([n["w_pq"][0].reshape(DK, P, HS, P).transpose(2, 1, 0, 3),
                                n["sub_keys"][0].reshape(HS, NKEY, 1, P).transpose(0, 3, 2, 1)], axis=2),
        "u": n["u_tab"][0].reshape(NE // P, P, DK, P).transpose(0, 3, 2, 1),
        "v": n["v_tab"][0].reshape(NE // P, P, D),
        "ln2_g": every_row(n["ln2_g"][0]),
        "ln2_b": every_row(n["ln2_b"][0]),
    }
    nc = bacc.Bacc("TRN2", target_bir_lowering=False, num_devices=1)
    ins, aps = {}, {}
    for name, v in arrays.items():
        v = np.ascontiguousarray(v)
        ins[f"in_{name}"] = v
        aps[name] = nc.dram_tensor(f"in_{name}", v.shape, mybir.dt.from_np(v.dtype), kind="ExternalInput").ap()
    for name, shape in SHAPES.items():
        aps[name] = nc.dram_tensor(f"out_{name}", shape, F32, kind="ExternalOutput").ap()
    build(nc, aps)
    got = run_bass_kernel_spmd(nc, [ins], core_ids=[0]).results[0]
    y = got["out_y"]
    return (y[:SEQ].reshape(1, SEQ, D), y[SEQ:].reshape(1, DEC, D),
            got["out_new_ckv"].reshape(1, 1, SEQ, KVR), got["out_new_krope"].reshape(1, 1, SEQ, ROPE))
```

```python
import math
from contextlib import ExitStack

import numpy as np

import concourse.bass as bass
from concourse import mybir

F32 = mybir.dt.float32
F32R = mybir.dt.float32r
U32 = mybir.dt.uint32
ALU = mybir.AluOpType
ACT = mybir.ActivationFunctionType
AX = mybir.AxisListType

P = 128
D = 1024
DK = D // P
SEQ, DEC, PAST = 128, 1024, 128
T = SEQ + DEC
NT = T // P
G, GD = 4, 128
AW = G * GD
H, NOPE, ROPE, VD = 4, 128, 64, 128
QR, KVR = 384, 256
QK, KK = QR // P, KVR // P
IN_COLS = 2 * AW + QR + KVR + ROPE
Z = ((0, AW), (AW, AW), (2 * AW, QR), (2 * AW + QR, KVR + ROPE))
KT = NT + 1
NKS = (KT - 1) * P
CW = 384
SCALE = 1.0 / math.sqrt(NOPE + ROPE)
PH, NKEY, TOPK = 8, 128, 16
HS = 2 * PH
PAIRS = PH * TOPK
NE = NKEY * NKEY
ALPHA = 2.0 ** 0.25
EPS = 1e-6
GRID_W = 64
LOW = -3.0e38
CT = CW // P
NC = T // CW
TB = 32
NTB = T // TB
CB = CW // TB
UB = 4


class Count:

    def __init__(self, eng, sem):
        self.eng, self.sem, self.n = eng, sem, 0
        eng.sem_inc(sem, 1)
        eng.sem_clear(sem)

    def step(self, ins):
        self.n += 1
        ins.then_inc(self.sem, 1)
        self.eng.wait_ge(self.sem, self.n)


def build(nc, a):
    es = ExitStack()
    used = set()

    def sb(stack, name, shape, dt=F32):
        return stack.enter_context(nc.sbuf_tensor(name, shape, dt))

    def sem(name):
        assert name not in used
        used.add(name)
        return es.enter_context(nc.semaphore(name))

    with es:
        x1_dram = nc.dram_tensor("x1_scratch", [T, D], F32, kind="Internal").ap()
        g_dram = nc.dram_tensor("g_scratch", [NTB, P, NKEY, TB], F32, kind="Internal").ap()
        gate_dram = nc.dram_tensor("gate_scratch", [NC + 1, P, D], F32, kind="Internal").ap()
        PS = [es.enter_context(nc.psum_tensor(f"bank{b}", [P, 512], F32)) for b in range(8)]
        ident = sb(es, "ident", [P, P])
        modc = sb(es, "modc", [P, 6 * DK, 2])
        sp1 = sb(es, "sp1", [P, 2, DK, 2])
        big = sb(es, "big", [P, KT * H * P * 2])
        kT = big[:, 0:KT * H * P].rearrange("p (h k) -> p h k", h=H)
        vv = big[:, KT * H * P:2 * KT * H * P].rearrange("p (t c) -> p t c", t=KT)
        h2T = big[:, 0:DK * T].rearrange("p (k t) -> p k t", k=DK)
        silu = sb(es, "silu", [P, DK, 2])
        bmod = sb(es, "bmod", [P, 6 * DK])
        with ExitStack() as mid:
            aoT = sb(mid, "aoT", [P, G, T])
            boT = sb(mid, "boT", [P, H, T])
            with ExitStack() as att:
                qT = sb(att, "qT", [P, H, T])
                qrT = sb(att, "qrT", [P, 2, T])
                krT = sb(att, "krT", [P, KT * P])
                mixer_inputs(nc, a, sb, sem, PS, ident, modc, sp1, silu, bmod, aoT, boT, qT, qrT, krT, kT, vv)
                attention(nc, a, sb, sem, PS, ident, modc, sp1, silu, bmod, boT, qT, qrT, krT, kT, vv)
            residual_one(nc, a, sb, sem, PS, ident, modc, sp1, aoT, boT, h2T, x1_dram, gate_dram)
        experts(nc, a, sb, sem, PS, ident, big, h2T, x1_dram, g_dram, gate_dram)


def mixer_inputs(nc, a, sb, sem, PS, ident, modc, sp1, silu, bmod, aoT, boT, qT, qrT, krT, kT, vv):
    with ExitStack() as c:
        w_in = sb(c, "w_in", [P, DK, IN_COLS])
        w_s = sb(c, "w_s", [P, G, P])
        b_s = sb(c, "b_s", [P, G])
        g_q = sb(c, "g_q", [P, QK])
        g_kv = sb(c, "g_kv", [P, KVR])
        w_qn = sb(c, "w_qn", [P, QK, H * NOPE])
        w_qr = sb(c, "w_qr", [P, QK, H * ROPE])
        w_kn = sb(c, "w_kn", [P, KK, H * NOPE])
        w_v = sb(c, "w_v", [P, KK, H * VD])
        cckT = sb(c, "cckT", [P, KK, P])
        cond = sb(c, "cond", [P, DK, 2])
        xt = sb(c, "xt", [P, DK, P])
        hT = sb(c, "hT", [P, DK, P])
        rot = sb(c, "rot", [P, 2, ROPE])
        u = sb(c, "u", [P, AW])
        vg = sb(c, "vg", [P, AW])
        vst = vg
        aout = u
        ql = sb(c, "ql", [P, QR])
        ckv = sb(c, "ckv", [P, KVR])
        kr = sb(c, "kr", [P, 2, ROPE])
        t1 = sb(c, "t1", [P, H * ROPE])
        t2 = sb(c, "t2", [P, H * ROPE])
        qr = sb(c, "qr", [P, H * ROPE])
        qlT = sb(c, "qlT", [P, QK, P])
        ckT = sb(c, "ckT", [P, KK, P])
        junk = sb(c, "junk", [P, QR])
        st = sb(c, "st", [P, G, 6])
        mv = sb(c, "mv", [P, G, 2])
        var = sb(c, "var", [P, G + 2])
        ssq = sb(c, "ssq", [P, 2])
        sd = sb(c, "sd", [P, G + 2])
        rs = sb(c, "rs", [P, G + 2])

        free = boT[:, :, :].rearrange("p h t -> p (h t)")
        NJ, NW = 2 * DK, 4
        wm = free[:, 0:NW * D].rearrange("p (w k c) -> p w k c", w=NW, k=DK)
        hT1 = free[:, 0:D].rearrange("p (k t) -> p k t", k=DK)
        hs = [hT[:, :, :], hT1]

        cl, wl = sem("a_small"), sem("a_weights")
        ml = [sem(f"a_m{k}") for k in range(NW)]
        silu_ready, m_used, m_made, mod_ready, id0, id1 = (sem(f"a_{n}") for n in (
            "silu", "mused", "mmade", "mod", "id0", "id1"))
        xl, rl = sem("a_x"), sem("a_rot")
        h_ready, z_ready = sem("a_h"), sem("a_z")
        gelu_u, gelu_v, sq_q, sq_kv, sd_ready = (sem(f"a_{n}") for n in ("gu", "gv", "sqq", "sqkv", "sd"))
        chain, var_ready, v_std, lat_ready, gate_ready, mixed = (sem(f"a_{n}") for n in (
            "chain", "var", "vstd", "lat", "gate", "mixed"))
        trl, tra, trq, qlT_ready, ao_ev, q_ev, k_ev, v_ev, qr_ready, qr_ev = (sem(f"a_{n}") for n in (
            "trl", "tra", "trq", "qlT", "ao", "qev", "kev", "vev", "qr", "qrev"))
        q_mm, k_mm, v_mm, r_mm = sem("a_qmm"), sem("a_kmm"), sem("a_vmm"), sem("a_rmm")
        stored = sem("a_stored")
        nw = 12

        with nc.Block() as block:
            @block.sync
            def _(sp):
                sp.dma_start(cond[:, :, :], a["cond"]).then_inc(cl, 16)
                sp.dma_start(bmod[:, :], a["b_mod"]).then_inc(cl, 16)
                sp.dma_start(xt[:, :, :], a["xT"][0, :, :, :]).then_inc(xl, 16)
                sp.dma_start(rot[:, :, :], a["rot"][0, :, :, :]).then_inc(rl, 16)
                with sp.Fori(0, NJ // NW) as j:
                    for k in range(NW):
                        sp.wait_ge(m_used, j * NW + k + 1)
                        sp.dma_start(wm[:, k, :, :], a["w_mod"][j * NW + k, :, :, :]).then_inc(ml[k], 16)
                with sp.Fori(1, NT) as i:
                    sp.wait_ge(h_ready, i)
                    sp.dma_start(xt[:, :, :], a["xT"][i, :, :, :]).then_inc(xl, 16)
                    sp.wait_ge(qr_ready, i)
                    sp.dma_start(rot[:, :, :], a["rot"][i, :, :, :]).then_inc(rl, 16)

            @block.gpsimd
            def _(pool):
                pool.memset(ident[:, :], 0.0).then_inc(id0, 1)
                pool.wait_ge(id0, 1)
                pool.affine_select(out=ident[:, :], in_=ident[:, :], compare_op=ALU.not_equal, fill=1.0,
                                   base=0, pattern=[[-1, P]], channel_multiplier=1).then_inc(id1, 1)
                pool.wait_ge(id1, 1)

            def rotate(dve, out, ps, heads):
                for half in range(2):
                    for part in range(heads):
                        o = out[:, part * ROPE:(part + 1) * ROPE].rearrange("p (a b f) -> p a b f", a=2, b=2)
                        x = ps[:, part * ROPE:(part + 1) * ROPE].rearrange("p (a b f) -> p a b f", a=2, b=2)
                        w = rot[:, 1, :].rearrange("p (a b f) -> p a b f", a=2, b=2)
                        ins = dve.tensor_tensor(o[:, :, half, :], x[:, :, 1 - half, :], w[:, :, half, :], ALU.mult)
                return ins

            def dve_tile(dve, i, m):
                ch = Count(dve, chain)
                dve.wait_ge(gelu_v, i + 1)
                for g in range(G):
                    ins = dve.bn_stats(st[:, g, :], vg[:, g * GD:(g + 1) * GD])
                ch.step(ins)
                for g in range(G):
                    ins = dve.bn_aggr(mv[:, g, :], st[:, g, :])
                ch.step(ins)
                dve.tensor_scalar(var[:, 0:G], mv[:, :, 1], EPS, None, ALU.add)
                dve.wait_ge(sq_kv, i + 1)
                dve.tensor_scalar(var[:, G:G + 1], ssq[:, 0:1], 1.0 / QR, EPS, ALU.mult, ALU.add)
                dve.tensor_scalar(var[:, G + 1:G + 2], ssq[:, 1:2], 1.0 / KVR, EPS, ALU.mult,
                                  ALU.add).then_inc(var_ready, 1)
                dve.wait_ge(sd_ready, i + 1)
                ch.step(dve.reciprocal(rs[:, :], sd[:, :]))
                for g in range(G):
                    part = vg[:, g * GD:(g + 1) * GD]
                    ins = dve.tensor_scalar(part, part, mv[:, g, 0:1], rs[:, g:g + 1], ALU.subtract, ALU.mult)
                ins.then_inc(v_std, 1)
                dve.tensor_scalar(ql[:, :], PS[2][:, 0:QR], rs[:, G:G + 1], None, ALU.mult)
                dve.wait_ge(rl, (i + 1) * 16)
                if m == 0:
                    for half in range(2):
                        ins = dve.tensor_copy(kr[:, half, :], PS[3][:, KVR:KVR + ROPE])
                else:
                    ps = PS[3][:, KVR:KVR + ROPE]
                    dve.tensor_tensor(t1[:, 0:ROPE], ps, rot[:, 0, :], ALU.mult)
                    ch.step(rotate(dve, t2, ps, 1))
                    for half in range(2):
                        ins = dve.tensor_tensor(kr[:, half, :], t1[:, 0:ROPE], t2[:, 0:ROPE], ALU.add)
                dve.scalar_tensor_tensor(ckv[:, :], PS[3][:, 0:KVR], rs[:, G + 1:G + 2], g_kv[:, :],
                                         ALU.mult, ALU.mult).then_inc(lat_ready, 1)
                dve.wait_ge(trl, i + 1)
                for k in range(QK):
                    dve.tensor_scalar(qlT[:, k, :], PS[6][:, k * P:(k + 1) * P], g_q[:, k:k + 1], None, ALU.mult)
                dve.tensor_copy(ckT[:, :, :], PS[7][:, 0:KK * P].rearrange("p (k t) -> p k t", k=KK))
                dst = krT[:, 0:P] if m == 0 else krT[:, bass.ds(i * P + P, P)]
                dve.tensor_copy(dst, PS[6][:, QK * P:(QK + 1) * P]).then_inc(qlT_ready, 1)
                dve.wait_ge(mixed, i + 1)
                dve.wait_ge(gelu_u, i + 1)
                for g in range(G):
                    sl = slice(g * GD, (g + 1) * GD)
                    ins = dve.scalar_tensor_tensor(aout[:, sl], PS[4][:, sl], b_s[:, g:g + 1], u[:, sl],
                                                   ALU.add, ALU.mult)
                ins.then_inc(gate_ready, 1)
                dve.wait_ge(r_mm, i + 1)
                ps = PS[4][:, 0:H * ROPE]
                if m == 0:
                    dve.tensor_copy(qr[:, :], ps).then_inc(qr_ready, 1)
                else:
                    cosb = rot[:, 0:1, :].to_broadcast([P, H, ROPE])
                    dve.tensor_tensor(t1[:, :].rearrange("p (h r) -> p h r", h=H),
                                      ps.rearrange("p (h r) -> p h r", h=H), cosb, ALU.mult)
                    ch.step(rotate(dve, t2, ps, H))
                    dve.tensor_tensor(qr[:, :], t1[:, :], t2[:, :], ALU.add).then_inc(qr_ready, 1)

            @block.vector
            def _(dve):
                dve.wait_ge(cl, 32)
                dve.wait_ge(m_used, NJ + NW)
                bc = bmod[:, 0:NJ].rearrange("p (j o) -> p j o", o=1).to_broadcast([P, NJ, 2])
                dve.tensor_tensor(modc[:, 0:NJ, :], PS[7][:, 0:2 * NJ].rearrange("p (j c) -> p j c", c=2), bc,
                                  ALU.add).then_inc(m_made, 1)
                dve.wait_ge(m_made, 1)
                dve.tensor_scalar(sp1[:, 0, :, :], modc[:, DK:2 * DK, :], 1.0, None, ALU.add).then_inc(mod_ready, 1)
                dve.wait_ge(wl, nw * 16)
                dve_tile(dve, 0, 0)
                with dve.Fori(1, NT) as i:
                    dve_tile(dve, i, 1)

            def mod_h(act, i, slot, m):
                act.wait_ge(xl, (i + 1) * 16)
                for k in range(DK):
                    ins = act.activation(hs[slot][:, k, :], xt[:, k, :], ACT.Identity,
                                         bias=modc[:, k, m:m + 1], scale=sp1[:, 0, k, m:m + 1])
                ins.then_inc(h_ready, 1)

            def act_tile(act, i, slot, first=False, last=False):
                act.wait_ge(z_ready, i * 4 + 1)
                act.wait_ge(tra, i)
                act.activation(u[:, :], PS[0][:, :], ACT.Gelu).then_inc(gelu_u, 1)
                act.wait_ge(z_ready, i * 4 + 2)
                act.wait_ge(mixed, i)
                act.activation(vg[:, :], PS[1][:, :], ACT.Gelu).then_inc(gelu_v, 1)
                act.wait_ge(z_ready, i * 4 + 3)
                act.activation(junk[:, 0:QR], PS[2][:, 0:QR], ACT.Square, accum_out=ssq[:, 0:1]).then_inc(sq_q, 1)
                act.wait_ge(z_ready, i * 4 + 4)
                act.wait_ge(sq_q, i + 1)
                act.activation(junk[:, 0:KVR], PS[3][:, 0:KVR], ACT.Square,
                               accum_out=ssq[:, 1:2]).then_inc(sq_kv, 1)
                act.wait_ge(var_ready, i + 1)
                act.activation(sd[:, :], var[:, :], ACT.Sqrt).then_inc(sd_ready, 1)
                if not last:
                    mod_h(act, i + 2, slot, 1)
                key = 0 if first else i * P + P
                act.wait_ge(q_mm, i + 1)
                act.activation(qT[:, :, bass.ds(i * P, P)], PS[5][:, :].rearrange("p (h t) -> p h t", h=H),
                               ACT.Copy).then_inc(q_ev, 1)
                act.wait_ge(k_mm, i + 2)
                act.activation(kT[:, :, bass.ds(key, P)], PS[7][:, :].rearrange("p (h t) -> p h t", h=H),
                               ACT.Copy).then_inc(k_ev, 1)
                act.wait_ge(v_mm, i + 2)
                row = 0 if first else i + 1
                act.activation(vv[:, row, :], PS[6][:, :], ACT.Copy).then_inc(v_ev, 1)
                act.wait_ge(tra, i + 1)
                act.activation(aoT[:, :, bass.ds(i * P, P)], PS[5][:, :].rearrange("p (g t) -> p g t", g=G),
                               ACT.Copy).then_inc(ao_ev, 1)
                act.wait_ge(trq, i + 1)
                act.activation(qrT[:, :, bass.ds(i * P, P)], PS[7][:, 0:2 * P].rearrange("p (h t) -> p h t", h=2),
                               ACT.Copy).then_inc(qr_ev, 1)

            @block.scalar
            def _(act):
                for dst, src in ((w_in, "w_in"), (w_s, "w_s"), (w_qn, "w_qn"), (w_qr, "w_qr"),
                                 (w_kn, "w_kn"), (w_v, "w_v"), (cckT, "cckT")):
                    act.dma_start(dst[:, :, :], a[src]).then_inc(wl, 16)
                for dst, src in ((b_s, "b_s"), (g_q, "g_q"), (g_kv, "g_kv")):
                    act.dma_start(dst[:, :], a[src]).then_inc(wl, 16)
                for half in range(2):
                    act.dma_start(krT[half * ROPE:(half + 1) * ROPE, P:2 * P], a["ckrT"]).then_inc(wl, 16)
                act.wait_ge(cl, 32)
                act.activation(silu[:, :, :], cond[:, :, :], ACT.Silu).then_inc(silu_ready, 1)
                act.wait_ge(mod_ready, 1)
                mod_h(act, 0, 0, 0)
                mod_h(act, 1, 1, 1)
                act.wait_ge(k_mm, 1)
                act.activation(kT[:, :, P:2 * P], PS[7][:, :].rearrange("p (h t) -> p h t", h=H),
                               ACT.Copy).then_inc(k_ev, 1)
                act.wait_ge(v_mm, 1)
                act.activation(vv[:, 1, :], PS[6][:, :], ACT.Copy).then_inc(v_ev, 1)
                act_tile(act, 0, 0, first=True)
                act.wait_ge(lat_ready, 1)
                act.dma_start(a["new_ckv"], ckv[:, :]).then_inc(stored, 16)
                act.dma_start(a["new_krope"], kr[:, 0, :]).then_inc(stored, 16)
                act.wait_ge(stored, 32)
                with act.Fori(0, (NT - 3) // 2) as j:
                    act_tile(act, j * 2 + 1, 1)
                    act_tile(act, j * 2 + 2, 0)
                act_tile(act, NT - 2, 1, last=True)
                act_tile(act, NT - 1, 0, last=True)

            def keys(pe, ckT_):
                for h in range(H):
                    for k in range(KK):
                        mm = pe.matmul(PS[7][:, h * P:(h + 1) * P], w_kn[:, k, h * NOPE:(h + 1) * NOPE],
                                       ckT_[:, k, :], start=(k == 0), stop=(k == KK - 1))
                mm.then_inc(k_mm, 1)

            def values(pe, ckT_):
                for k in range(KK):
                    mm = pe.matmul(PS[6][:, :], ckT_[:, k, :], w_v[:, k, :], start=(k == 0), stop=(k == KK - 1))
                mm.then_inc(v_mm, 1)

            def project(pe, i, slot):
                pe.wait_ge(h_ready, i + 1)
                for n, (at, w) in enumerate(Z):
                    if n == 0:
                        pe.wait_ge(gelu_u, i)
                    elif n == 1:
                        pe.wait_ge(gelu_v, i)
                    else:
                        pe.wait_ge(lat_ready, i)
                    for k in range(DK):
                        mm = pe.matmul(PS[n][:, 0:w], hs[slot][:, k, :], w_in[:, k, at:at + w],
                                       start=(k == 0), stop=(k == DK - 1))
                    mm.then_inc(z_ready, 1)

            def finish(pe, i):
                pe.wait_ge(lat_ready, i + 1)
                pe.wait_ge(v_ev, i + 1)
                for k in range(QK):
                    pe.transpose(PS[6][:, k * P:(k + 1) * P], ql[:, k * P:(k + 1) * P], ident[:, :])
                pe.transpose(PS[6][:, QK * P:(QK + 1) * P], kr[:, :, :].rearrange("p a r -> p (a r)"), ident[:, :])
                pe.wait_ge(k_ev, i + 1)
                pe.wait_ge(qr_ev, i)
                for k in range(KK):
                    mm = pe.transpose(PS[7][:, k * P:(k + 1) * P], ckv[:, k * P:(k + 1) * P], ident[:, :])
                mm.then_inc(trl, 1)
                pe.wait_ge(v_std, i + 1)
                pe.wait_ge(qr_ready, i)
                for g in range(G):
                    mm = pe.matmul(PS[4][:, g * GD:(g + 1) * GD], w_s[:, g, :], vst[:, g * GD:(g + 1) * GD],
                                   start=True, stop=True)
                mm.then_inc(mixed, 1)
                pe.wait_ge(qlT_ready, i + 1)
                pe.wait_ge(ao_ev, i)
                for h in range(H):
                    for k in range(QK):
                        mm = pe.matmul(PS[5][:, h * P:(h + 1) * P], w_qn[:, k, h * NOPE:(h + 1) * NOPE],
                                       qlT[:, k, :], start=(k == 0), stop=(k == QK - 1))
                mm.then_inc(q_mm, 1)
                keys(pe, ckT)
                values(pe, ckT)
                pe.wait_ge(gate_ready, i + 1)
                for k in range(QK):
                    mm = pe.matmul(PS[4][:, 0:H * ROPE], qlT[:, k, :], w_qr[:, k, :],
                                   start=(k == 0), stop=(k == QK - 1))
                mm.then_inc(r_mm, 1)
                pe.wait_ge(q_ev, i + 1)
                for g in range(G):
                    mm = pe.transpose(PS[5][:, g * P:(g + 1) * P], aout[:, g * GD:(g + 1) * GD], ident[:, :])
                mm.then_inc(tra, 1)
                pe.wait_ge(qr_ready, i + 1)
                pe.wait_ge(k_ev, i + 2)
                for pair in range(2):
                    mm = pe.transpose(PS[7][:, pair * P:(pair + 1) * P], qr[:, pair * P:(pair + 1) * P], ident[:, :])
                mm.then_inc(trq, 1)

            @block.tensor
            def _(pe):
                pe.sem_inc(m_used, NW)
                pe.wait_ge(silu_ready, 1)
                pe.wait_ge(id1, 1)
                acc = PS[7][:, 0:2 * NJ].rearrange("p (j c) -> p j c", c=2)
                with pe.Fori(0, NJ // NW) as j:
                    for w in range(NW):
                        pe.wait_ge(ml[w], (j + 1) * 16)
                        for k in range(DK):
                            mm = pe.matmul(acc[:, j * NW + w, :], wm[:, w, k, :], silu[:, k, :],
                                           start=(k == 0), stop=(k == DK - 1))
                        mm.then_inc(m_used, 1)
                pe.wait_ge(wl, nw * 16)
                pe.wait_ge(mod_ready, 1)
                keys(pe, cckT)
                values(pe, cckT)
                project(pe, 0, 0)
                project(pe, 1, 1)
                finish(pe, 0)
                with pe.Fori(0, (NT - 3) // 2) as j:
                    project(pe, j * 2 + 2, 0)
                    finish(pe, j * 2 + 1)
                    project(pe, j * 2 + 3, 1)
                    finish(pe, j * 2 + 2)
                project(pe, NT - 1, 0)
                finish(pe, NT - 2)
                finish(pe, NT - 1)


def attention(nc, a, sb, sem, PS, ident, modc, sp1, silu, bmod, boT, qT, qrT, krT, kT, vv):
    with ExitStack() as c:
        qc = sb(c, "qc", [P, H, P])
        qrc = sb(c, "qrc", [P, 2, P])
        pr = sb(c, "pr", [P, 2, NKS])
        prT = sb(c, "prT", [P, 2, NKS])
        on = sb(c, "on", [P, 2, VD])
        part = sb(c, "part", [P, 2, 3])
        mx = sb(c, "mx", [P, 2])
        nb = sb(c, "nb", [P, 2])
        sums = sb(c, "sums", [P, 2, 3])
        sm = sb(c, "sm", [P, 2])
        ri = sb(c, "ri", [P, 2])
        wm = sb(c, "wm", [P, 2, DK, P])
        q_ready, s_ready, m_part, m_ready, b_ready, e_ready, r_sum, r_ready, t_ready, t_ev, o_ready, o_ev, n_ready, bo_ev = (
            sem(f"b_{n}") for n in ("q", "s", "mp", "m", "b", "e", "rs", "r", "t", "tev", "o", "oev", "n", "bo"))
        ml = [sem(f"b_m{k}") for k in range(2)]
        m_used, m_made, mod_ready = sem("b_mused"), sem("b_mmade"), sem("b_mod")
        J0 = 2 * DK

        with nc.Block() as block:
            @block.sync
            def _(sp):
                for k in range(2):
                    sp.dma_start(wm[:, k, :, :], a["w_mod"][J0 + k, :, :, :]).then_inc(ml[k], 16)
                with sp.Fori(1, 2 * DK) as j:
                    for k in range(2):
                        sp.wait_ge(m_used, j * 2 + k - 1)
                        sp.dma_start(wm[:, k, :, :], a["w_mod"][j * 2 + (J0 + k), :, :, :]).then_inc(ml[k], 16)

            def inc(nkeys):
                return 3 if nkeys < NKS else 1

            def width(b, nkeys):
                return min(CW, nkeys - b * CW)

            def scores(pe, h, n, nkeys, key0):
                half = (h % 2) * ROPE
                for b in range((nkeys + CW - 1) // CW):
                    if not (isinstance(n, int) and n == 0):
                        pe.wait_ge(e_ready, n * 3 - 2 + b)
                    w = width(b, nkeys)
                    ks = slice(key0 + b * CW, key0 + b * CW + w)
                    pe.matmul(PS[b][:, 0:w], qc[:, h, :], kT[:, h, ks], start=True, stop=False)
                    mm = pe.matmul(PS[b][:, 0:w], qrc[half:half + ROPE, h // 2, :], krT[half:half + ROPE, ks],
                                   start=False, stop=True)
                    mm.then_inc(s_ready, inc(nkeys))

            def outputs(pe, h, n, nkeys, kt0):
                nk = nkeys // P
                for b in range((nk + 2) // 3):
                    pe.wait_ge(e_ready, n * 3 + (b + 1))
                    if not (isinstance(n, int) and n == 0):
                        pe.wait_ge(t_ev, n * 3 - 2 + b)
                    for k in range(min(3, nk - 3 * b)):
                        mm = pe.transpose(PS[3 + b][:, k * P:(k + 1) * P],
                                          pr[:, h % 2, (3 * b + k) * P:(3 * b + k + 1) * P], ident[:, :])
                    mm.then_inc(t_ready, inc(nkeys))

            def values(pe, h, n, nkeys, kt0):
                nk = nkeys // P
                if not (isinstance(n, int) and n == 0):
                    pe.wait_ge(bo_ev, n)
                for k in range(nk):
                    if k % 3 == 0:
                        pe.wait_ge(t_ev, n * 3 + (k // 3 + 1))
                    mm = pe.matmul(PS[6][:, 0:VD], prT[:, h % 2, k * P:(k + 1) * P],
                                   vv[:, kt0 + k, h * VD:(h + 1) * VD], start=(k == 0), stop=(k == nk - 1))
                mm.then_inc(o_ready, 1)

            def back(pe, h, n):
                pe.wait_ge(n_ready, n + 1)
                pe.transpose(PS[6][:, 0:P], on[:, h % 2, :], ident[:, :]).then_inc(o_ev, 1)

            def pe_tile(pe, i, nkeys, key0, sample):
                acc = PS[7][:, 0:2 * 4 * DK].rearrange("p (j c) -> p j c", c=2)
                pe.wait_ge(q_ready, i + 1)
                scores(pe, 0, i * H, nkeys, key0)
                for h in range(H):
                    n = i * H + h
                    if sample:
                        pe.wait_ge(ml[h % 2], (i * 2 + (h // 2 - 1)) * 16)
                        for k in range(DK):
                            mm = pe.matmul(acc[:, i * H + (h - H), :], wm[:, h % 2, k, :], silu[:, k, :],
                                           start=(k == 0), stop=(k == DK - 1))
                        mm.then_inc(m_used, 1)
                    outputs(pe, h, n, nkeys, key0 // P)
                    if h + 1 < H:
                        scores(pe, h + 1, n + 1, nkeys, key0)
                    values(pe, h, n, nkeys, key0 // P)
                    back(pe, h, n)

            @block.tensor
            def _(pe):
                pe_tile(pe, 0, P, 0, False)
                with pe.Fori(1, NT) as i:
                    pe_tile(pe, i, NKS, P, True)

            def dve_tile(dve, i, nkeys):
                if not isinstance(i, int):
                    dve.wait_ge(s_ready, i * (3 * H))
                dve.tensor_copy(qc[:, :, :], qT[:, :, bass.ds(i * P, P)])
                dve.tensor_copy(qrc[:, :, :], qrT[:, :, bass.ds(i * P, P)]).then_inc(q_ready, 1)
                nb_ = (nkeys + CW - 1) // CW
                for h in range(H):
                    n, t = i * H + h, h % 2
                    for b in range(nb_):
                        dve.wait_ge(s_ready, n * 3 + (b + 1))
                        ins = dve.reduce_max(part[:, t, b:b + 1], PS[b][:, 0:width(b, nkeys)], AX.X)
                    ins.then_inc(m_part, 1)
                    dve.wait_ge(m_part, n + 1)
                    dve.reduce_max(mx[:, t:t + 1], part[:, t, 0:nb_], AX.X).then_inc(m_ready, 1)
                    dve.wait_ge(m_ready, n + 1)
                    dve.tensor_scalar(nb[:, t:t + 1], mx[:, t:t + 1], -SCALE, None, ALU.mult).then_inc(b_ready, 1)
                    for b in (0, 2):
                        if b < nb_:
                            w = width(b, nkeys)
                            dve.wait_ge(t_ready, n * 3 + (b + 1))
                            if b == 2:
                                dve.wait_ge(t_ev, n * 3 + 2)
                            dve.tensor_copy(prT[:, t, b * CW:b * CW + w], PS[3 + b][:, 0:w]).then_inc(
                                t_ev, inc(nkeys))
                    dve.wait_ge(e_ready, n * 3 + nb_)
                    dve.reduce_sum(sm[:, t:t + 1], sums[:, t, 0:nb_], AX.X).then_inc(r_sum, 1)
                    dve.wait_ge(r_sum, n + 1)
                    dve.reciprocal(ri[:, t:t + 1], sm[:, t:t + 1]).then_inc(r_ready, 1)
                    dve.wait_ge(r_ready, n + 1)
                    dve.wait_ge(o_ready, n + 1)
                    dve.tensor_scalar(on[:, t, :], PS[6][:, 0:VD], ri[:, t:t + 1], None, ALU.mult).then_inc(n_ready, 1)

            @block.vector
            def _(dve):
                dve_tile(dve, 0, P)
                with dve.Fori(1, NT) as i:
                    dve_tile(dve, i, NKS)
                dve.wait_ge(m_used, 4 * DK)
                bc = bmod[:, J0:].rearrange("p (j o) -> p j o", o=1).to_broadcast([P, 4 * DK, 2])
                dve.tensor_tensor(modc[:, J0:, :], PS[7][:, 0:8 * DK].rearrange("p (j c) -> p j c", c=2), bc,
                                  ALU.add).then_inc(m_made, 1)
                dve.wait_ge(m_made, 1)
                dve.tensor_scalar(sp1[:, 1, :, :], modc[:, 4 * DK:5 * DK, :], 1.0, None,
                                  ALU.add).then_inc(mod_ready, 1)
                dve.wait_ge(mod_ready, 1)

            def act_tile(act, i, nkeys):
                nb_ = (nkeys + CW - 1) // CW
                for h in range(H):
                    n, t = i * H + h, h % 2
                    act.wait_ge(b_ready, n + 1)
                    for b in range(nb_):
                        w = width(b, nkeys)
                        act.activation(pr[:, t, b * CW:b * CW + w], PS[b][:, 0:w], ACT.Exp, bias=nb[:, t:t + 1],
                                       scale=SCALE, accum_out=sums[:, t, b:b + 1]).then_inc(e_ready, inc(nkeys))
                    if nkeys == NKS:
                        act.wait_ge(t_ready, n * 3 + 2)
                        act.wait_ge(t_ev, n * 3 + 1)
                        act.activation(prT[:, t, CW:2 * CW], PS[4][:, 0:CW], ACT.Copy).then_inc(t_ev, 1)
                    act.wait_ge(o_ev, n + 1)
                    act.activation(boT[:, h, bass.ds(i * P, P)], PS[6][:, 0:P], ACT.Copy).then_inc(bo_ev, 1)

            @block.scalar
            def _(act):
                act_tile(act, 0, P)
                with act.Fori(1, NT) as i:
                    act_tile(act, i, NKS)


def residual_one(nc, a, sb, sem, PS, ident, modc, sp1, aoT, boT, h2T, x1_dram, gate_dram):
    with ExitStack() as c:
        w_o = sb(c, "w_o", [P, DK, D])
        ln_g = sb(c, "ln1_g", [P, D])
        ln_b = sb(c, "ln1_b", [P, D])
        gate = sb(c, "gate1", [P, 2, D])
        gcol = sb(c, "gcol1", [P, 2, P])
        ones = sb(c, "ones1", [P, P])
        gate_l = sb(c, "gate_l", [P, 2, D])
        mc = sb(c, "mc", [P, DK, P])
        xt = sb(c, "xr", [P, D])
        r = sb(c, "r1", [P, D])
        y = sb(c, "y1", [P, D])
        x1 = sb(c, "x1", [P, D])
        st = sb(c, "st1", [P, 2, 6])
        mv = sb(c, "mv1", [P, 2])
        ve = sb(c, "ve1", [P, 1])
        sd = sb(c, "sd1", [P, 1])
        rs = sb(c, "rs1", [P, 1])
        wl, xl, ones_ready, g_col, g_mm, g_ev, g_out = (sem(f"c_{n}") for n in (
            "w", "x", "ones", "gcol", "gmm", "gev", "gout"))
        m_ready, mm_ready, xa_ready, ve_ready, sd_ready, chain, x1_ready, tr_ready, h_ev, st1, bank_read = (
            sem(f"c_{n}") for n in ("m", "mm", "xa", "ve", "sd", "chain", "x1", "tr", "hev", "st", "bank"))
        with nc.Block() as block:
            @block.sync
            def _(sp):
                sp.dma_start(w_o[:, :, :], a["w_o"]).then_inc(wl, 16)
                sp.dma_start(ln_g[:, :], a["ln1_g"]).then_inc(wl, 16)
                sp.dma_start(ln_b[:, :], a["ln1_b"]).then_inc(wl, 16)
                sp.dma_start(xt[:, :], a["x"][0:P, :]).then_inc(xl, 16)
                with sp.Fori(1, NT) as i:
                    sp.wait_ge(xa_ready, i)
                    sp.dma_start(xt[:, :], a["x"][bass.ds(i * P, P), :]).then_inc(xl, 16)
                    sp.wait_ge(x1_ready, i)
                    sp.dma_start(x1_dram[bass.ds(i * P - P, P), :], x1[:, :]).then_inc(st1, 16)
                sp.wait_ge(x1_ready, NT)
                sp.dma_start(x1_dram[T - P:T, :], x1[:, :]).then_inc(st1, 16)
                sp.wait_ge(st1, NT * 16)

            @block.gpsimd
            def _(pool):
                pool.memset(ones[:, :], 1.0).then_inc(ones_ready, 1)

            late = gate_rows(5 * DK, 0, gate_l, gcol, ones, modc, ident, PS, g_col, g_mm, g_ev)
            early = gate_rows(2 * DK, 1, gate, gcol, ones, modc, ident, PS, g_col, g_mm, g_ev)

            @block.tensor
            def _(pe):
                late[0](pe)
                early[0](pe)
                pe.wait_ge(wl, 48)

                def mix(i):
                    pe.wait_ge(m_ready, i + 1)
                    pe.wait_ge(bank_read, i)
                    for n in range(2):
                        for k in range(DK):
                            mm = pe.matmul(PS[n][:, :], mc[:, k, :], w_o[:, k, n * 512:(n + 1) * 512],
                                           start=(k == 0), stop=(k == DK - 1))
                    mm.then_inc(mm_ready, 1)

                def turn(i):
                    pe.wait_ge(x1_ready, i + 1)
                    if not (isinstance(i, int) and i == 0):
                        pe.wait_ge(h_ev, i)
                    for k in range(DK):
                        mm = pe.transpose(PS[2 + k // 4][:, (k % 4) * P:(k % 4 + 1) * P], x1[:, k * P:(k + 1) * P],
                                          ident[:, :])
                    mm.then_inc(tr_ready, 1)

                mix(0)
                mix(1)
                turn(0)
                with pe.Fori(2, NT) as i:
                    mix(i)
                    turn(i - 1)
                turn(NT - 1)

            def root(act, i):
                act.wait_ge(ve_ready, i + 1)
                act.activation(sd[:, :], ve[:, :], ACT.Sqrt).then_inc(sd_ready, 1)

            def mod_h2(act, i, m):
                act.wait_ge(tr_ready, i + 1)
                for k in range(DK):
                    ins = act.activation(h2T[:, k, bass.ds(i * P, P)], PS[2 + k // 4][:, (k % 4) * P:(k % 4 + 1) * P],
                                         ACT.Identity, bias=modc[:, 3 * DK + k, m:m + 1],
                                         scale=sp1[:, 1, k, m:m + 1])
                ins.then_inc(h_ev, 1)

            @block.scalar
            def _(act):
                late[1](act)
                act.wait_ge(g_ev, 4)
                for n in range(NC + 1):
                    act.dma_start(gate_dram[n, :, :], gate_l[:, min(n, 1), :]).then_inc(g_out, 16)
                early[1](act)
                root(act, 0)
                mod_h2(act, 0, 0)
                root(act, 1)
                with act.Fori(2, NT) as i:
                    mod_h2(act, i - 1, 1)
                    root(act, i)
                mod_h2(act, NT - 1, 1)
                act.wait_ge(g_out, (NC + 1) * 16)

            def outputs_of(dve, i):
                dve.tensor_copy(mc[:, 0:G, :], aoT[:, :, bass.ds(i * P, P)])
                dve.tensor_copy(mc[:, G:DK, :], boT[:, :, bass.ds(i * P, P)]).then_inc(m_ready, 1)

            def dve_tile(dve, i, m, last=False):
                ch = Count(dve, chain)
                dve.wait_ge(mm_ready, i + 1)
                if not last:
                    outputs_of(dve, i + 1)
                for n in range(2):
                    sl = slice(n * 512, (n + 1) * 512)
                    ins = dve.tensor_tensor(r[:, sl], gate[:, m, sl], PS[n][:, :], ALU.mult)
                ins.then_inc(bank_read, 1)
                dve.wait_ge(bank_read, i + 1)
                dve.wait_ge(xl, (i + 1) * 16)
                dve.scalar_tensor_tensor(y[:, :], xt[:, :], ALPHA, r[:, :], ALU.mult, ALU.add).then_inc(xa_ready, 1)
                dve.wait_ge(xa_ready, i + 1)
                for n in range(2):
                    ins = dve.bn_stats(st[:, n, :], y[:, n * 512:(n + 1) * 512])
                ch.step(ins)
                ch.step(dve.bn_aggr(mv[:, :], st[:, :, :].rearrange("p a b -> p (a b)")))
                dve.tensor_scalar(ve[:, :], mv[:, 1:2], EPS, None, ALU.add).then_inc(ve_ready, 1)
                dve.wait_ge(sd_ready, i + 1)
                ch.step(dve.reciprocal(rs[:, :], sd[:, :]))
                ch.step(dve.tensor_scalar(r[:, :], y[:, :], mv[:, 0:1], rs[:, 0:1], ALU.subtract, ALU.mult))
                ch.step(dve.tensor_tensor(y[:, :], r[:, :], ln_g[:, :], ALU.mult))
                dve.wait_ge(tr_ready, i)
                dve.wait_ge(st1, i * 16)
                dve.tensor_tensor(x1[:, :], y[:, :], ln_b[:, :], ALU.add).then_inc(x1_ready, 1)
                dve.wait_ge(x1_ready, i + 1)

            @block.vector
            def _(dve):
                dve.wait_ge(ones_ready, 1)
                late[2](dve)
                early[2](dve)
                dve.wait_ge(wl, 48)
                outputs_of(dve, 0)
                dve_tile(dve, 0, 0)
                with dve.Fori(1, NT - 1) as i:
                    dve_tile(dve, i, 1)
                dve_tile(dve, NT - 1, 1, last=True)


def gate_rows(at, before, gate, gcol, ones, modc, ident, PS, g_col, g_mm, g_ev):
    n0, q0 = before * 2 * DK, before * 4
    def pe_part(pe):
        for n in range(2 * DK):
            m, k = divmod(n, DK)
            pe.wait_ge(g_col, n0 + n + 1)
            if n % 4 == 0 and n0 + n >= 4:
                pe.wait_ge(g_ev, q0 + n // 4)
            pe.matmul(PS[7][:, (n % 4) * P:(n % 4 + 1) * P], gcol[:, n % 2, :], ident[:, :],
                      start=True, stop=True).then_inc(g_mm, 1)

    def act_part(act):
        for q in range(2 * DK // 4):
            act.wait_ge(g_mm, n0 + 4 * q + 4)
            m, half = divmod(q, 2)
            act.activation(gate[:, m, half * 512:(half + 1) * 512], PS[7][:, :], ACT.Copy).then_inc(g_ev, 1)

    def dve_part(dve):
        for n in range(2 * DK):
            m, k = divmod(n, DK)
            if n0 + n >= 2:
                dve.wait_ge(g_mm, n0 + n - 1)
            dve.tensor_scalar(gcol[:, n % 2, :], ones[:, :], modc[:, at + k, m:m + 1], None,
                              ALU.mult).then_inc(g_col, 1)
        dve.wait_ge(g_ev, q0 + 4)

    return pe_part, act_part, dve_part


def experts(nc, a, sb, sem, PS, ident, big, h2T, x1_dram, g_dram, gate_dram):
    NEt = NE // P
    S = 8
    U = 8
    UNITS = CW // U
    POOL_ROWS = 2
    FILLS = 2 * HS + CT + 2 * UNITS
    F_HEAD, F_SCAT = 2 * HS, 2 * HS + CT
    ROUTE = [("list", HS // S), ("head", 2 * CT), ("scatter", UNITS // S)]
    BUSY = sum(n for _, n in ROUTE)
    PLAN = [ROUTE + [("plain", NEt // S - BUSY)],
            [("norm", 1)] + ROUTE + [("plain", NEt // S - BUSY - 1)],
            [("norm", 1), ("plain", NEt // S - 1)]]
    with ExitStack() as c:
        zero = sb(c, "zero", [P, 512], F32R)
        hR = sb(c, "hR", [P, DK, CW], F32R)
        hL = sb(c, "hL", [P, DK, CW], F32R)
        uw = sb(c, "uw", [P, 2, DK, P])
        vw = sb(c, "vw", [P, 2, D])
        uR = sb(c, "uR", [P, 2, DK, P], F32R)
        uL = sb(c, "uL", [P, 2, DK, P], F32R)
        vR = sb(c, "vR", [P, 2, D], F32R)
        vL = sb(c, "vL", [P, 2, D], F32R)
        gw = sb(c, "gw", [P, 2, CB, UB, TB])
        ga = sb(c, "ga", [P, CW])
        cR = sb(c, "cR", [P, 2, CW], F32R)
        cL = sb(c, "cL", [P, 2, CW], F32R)
        stage = sb(c, "stage", [P, 2, NKEY, TB])
        flat = stage[:, :, :, :].rearrange("p b i t -> p (b i t)")
        ln_g, ln_b, gate_0, gate_1, x1 = (flat[:, n * D:(n + 1) * D] for n in range(5))
        r = flat[:, 5 * D:(5 + CT) * D].rearrange("p (t d) -> p t d", t=CT)
        wq = sb(c, "wq", [P, 2, DK + 1, P])
        qs = sb(c, "qs", [P, CW])
        s = sb(c, "s", [P, 2, CT, NKEY])
        tv = sb(c, "tv", [P, CT, TOPK])
        ti = sb(c, "ti", [P, CT, TOPK], U32)
        top = sb(c, "top", [P, CT, HS, TOPK])
        itf = sb(c, "itf", [P, CT, HS, TOPK])
        cand = sb(c, "cand", [P, TOPK * TOPK])
        fs = sb(c, "fs", [P, PH, TOPK])
        fp = sb(c, "fp", [P, PH, TOPK], U32)
        ab = sb(c, "ab", [P, 2, TOPK], U32)
        abf = sb(c, "abf", [P, 2, TOPK])
        eq = sb(c, "eq", [P, 2, TOPK, TOPK])
        i16 = sb(c, "i16", [P, TOPK])
        out = sb(c, "out", [P, 3, PAIRS])
        ex = sb(c, "ex", [P, PH, TOPK])
        sm = sb(c, "smr", [P, PH])
        ri = sb(c, "rir", [P, PH])
        idxT = sb(c, "idxT", [P, 3, CW])
        iota = sb(c, "iota", [P, P])
        idc = sb(c, "idc", [P, 3, U])
        ra = big[:, DK * T:DK * T + U * P].rearrange("p (t i) -> p t i", t=U)
        cb = sb(c, "cb", [P, U, P])
        st = sb(c, "st2", [P, 2, 6])
        mv = sb(c, "mv2", [P, 2])
        ve = sb(c, "ve2", [P, 1])
        sd = sb(c, "sd2", [P, 1])
        rs = sb(c, "rs2", [P, 1])

        ul, vl, gl, wl, stored_g = ([sem(f"f_{n}{k}") for k in range(2)] for n in ("u", "v", "g", "wq", "stg"))
        ln_in, x1_in, y_out = sem("f_ln"), sem("f_x1"), sem("f_yout")
        const, h_r, h_l, u_r, u_l, v_r, v_l = (sem(f"f_{n}") for n in ("const", "hr", "hl", "ur", "ul", "vr", "vl"))
        a_mm, a_ev, c_f, c_r, c_l, v_mm, acc_done, acc_read = (sem(f"f_{n}") for n in (
            "amm", "aev", "cf", "cr", "cl", "vmm", "acc", "accr"))
        filled, emptied, listed, e_in, e_out, o_ready, hot, hot_row, idc_in, rows_go = (sem(f"f_{n}") for n in (
            "fill", "empty", "listed", "ein", "eout", "o", "hot", "hotr", "idc", "rowsgo"))
        chain, x1_used, ve_ready, sd_ready, n_ready, y_mul, y_ready = (sem(f"f_{n}") for n in (
            "chain", "x1u", "ve", "sd", "n", "ym", "y"))
        heads, picked = sem("f_heads"), sem("f_picked")
        A, E, ACC = PS[0], PS[1], PS[2:8]

        def schedule(eng, n, step):
            at = 0
            for kind, count in PLAN[n]:
                wide = 2 if kind == "head" else 1
                turns = count // wide - (at + count == NEt // S)
                if turns > 1:
                    with eng.Fori(0, turns) as it:
                        for p in range(wide * S):
                            step(kind, it, p, it * wide + (at + p // S))
                elif turns == 1:
                    for p in range(S):
                        step(kind, 0, p, at)
                at += count
            for p in range(S):
                step("plain", 0, p, NEt // S - 1)

        def routed(eng, step):
            for kind, count in ROUTE:
                wide = 2 if kind == "head" else 1
                with eng.Fori(0, count // wide) as it:
                    for p in range(wide * S):
                        step(kind, it, p)

        def fixed(m):
            return isinstance(m, int)

        def spare(alone):
            return (E, A) if alone else (E, E)

        with nc.Block() as block:
            @block.sync
            def _(sp):
                for b in range(2):
                    sp.sem_inc(stored_g[b], 16)

                def load_u(t, tile):
                    sp.dma_start(uw[:, t, :, :], a["u"][tile, :, :, :]).then_inc(ul[t], 16)

                def load_v(t, tile):
                    sp.dma_start(vw[:, t, :], a["v"][tile, :, :]).then_inc(vl[t], 16)

                def load_g(t, n, batch):
                    sp.dma_start(gw[:, t, :, :, :].rearrange("p c u t -> p c (u t)"),
                                 g_dram[n * CB:(n + 1) * CB, :, bass.ds(batch * UB, UB), :].rearrange(
                                     "c p u t -> p c (u t)")).then_inc(gl[t], 16)

                def load_list(t, l):
                    sp.dma_start(wq[:, t, :, :], a["w_pq"][l, :, :, :]).then_inc(wl[t], 16)

                def route(kind, it, q, cn):
                    f0 = cn * FILLS
                    if kind == "list":
                        sp.wait_ge(emptied, (it * S + q) * 2 + f0 + 1)
                        load_list((q + 1) % 2, it * S + q + 1 if q < S - 1 else it * -S + S)
                    if kind == "scatter" and q % 4 == 3:
                        b = q // 4
                        sp.wait_ge(emptied, (it * S + q + 1) * 2 + f0 + F_SCAT + 1)
                        sp.dma_start(g_dram[it * 2 + (cn * CB + b), :, :, :],
                                     stage[:, b, :, :]).then_inc(stored_g[b], 16)

                def weights_stored(cn):
                    for b in range(2):
                        sp.wait_ge(stored_g[b], ((cn + 1) * (CB // 2) + 1) * 16)

                def load_x1(i):
                    if i:
                        sp.wait_ge(x1_used, i)
                    sp.dma_start(x1, x1_dram[i * P:(i + 1) * P, :]).then_inc(x1_in, 16)

                def store_y(i):
                    sp.wait_ge(y_ready, i + 1)
                    sp.dma_start(a["y"][i * P:(i + 1) * P, :], r[:, i % CT, :]).then_inc(y_out, 16)

                def step(n):
                    def at(kind, it, p, body):
                        q, m = p % S, body * S + p % S
                        g = m + n * NEt
                        left = NC * NEt - g if fixed(m) else NEt
                        if left > 3:
                            sp.wait_ge(u_l, g + 2)
                            load_u((q + 1) % 2, m + 3 if not fixed(m) else (m + 3) % NEt)
                        if left > 2:
                            sp.wait_ge(v_l, g + 1)
                            load_v(q % 2, m + 2 if not fixed(m) else (m + 2) % NEt)
                        if q % UB == 0:
                            b = q // UB
                            sp.wait_ge(c_f, g + 1)
                            if not fixed(m):
                                load_g(1 - b, n, body * (S // UB) + (b + 1))
                            elif m + UB < NEt:
                                load_g(1 - b, n, m // UB + 1)
                            elif n + 1 < NC:
                                load_g(1 - b, n + 1, 0)
                        if kind == "norm" and q % 2 == 0 and q // 2 < CT - 1:
                            load_x1((n - 1) * CT + q // 2 + 1)
                        if kind == "norm" and q % 2 == 1 and q // 2 < CT:
                            store_y((n - 1) * CT + q // 2)
                        if n + 1 < NC:
                            route(kind, it, p, n + 1)
                        if fixed(m) and m == NEt - S:
                            weights_stored(min(n + 1, NC - 1))
                            for dst, src in ((ln_g, a["ln2_g"]), (ln_b, a["ln2_b"]), (gate_0, gate_dram[n, :, :]),
                                             (gate_1, gate_dram[NC, :, :])):
                                sp.dma_start(dst, src).then_inc(ln_in, 16)
                            load_x1(n * CT)
                    return at

                load_list(0, 0)
                for t in range(2):
                    load_u(t, t)
                    load_v(t, t)
                sp.wait_ge(u_l, 1)
                load_u(0, 2)
                routed(sp, lambda kind, it, p: route(kind, it, p, 0))
                weights_stored(0)
                load_g(0, 0, 0)
                for n in range(NC):
                    schedule(sp, n, step(n))
                for t in range(CT):
                    i = (NC - 1) * CT + t
                    if t + 1 < CT:
                        load_x1(i + 1)
                    store_y(i)
                sp.wait_ge(y_out, NT * 16)
                sp.wait_ge(wl[0], (NC * HS // 2 + 1) * 16)

            @block.gpsimd
            def _(pool):
                pool.memset(zero[:, :].bitcast(F32), 0.0).then_inc(const, 1)
                pool.iota(i16[:, :], pattern=[[1, TOPK]], base=0, channel_multiplier=0,
                          allow_small_or_imprecise_dtypes=True).then_inc(const, 1)
                pool.iota(iota[:, :], pattern=[[1, P]], base=0, channel_multiplier=0,
                          allow_small_or_imprecise_dtypes=True).then_inc(const, 1)

                def split_v(t, g):
                    pool.wait_ge(v_r, g + 1)
                    pool.tensor_tensor(vL[:, t, :], vw[:, t, :], vR[:, t, :].bitcast(F32),
                                       ALU.subtract).then_inc(v_l, 1)

                def scatter(it, q, cn):
                    unit = it * S + q
                    pool.wait_ge(idc_in, unit + (cn * UNITS + 1))
                    for e in range(2):
                        pool.wait_ge(filled, unit * 2 + (cn * FILLS + F_SCAT + e - 1))
                        pool.sem_inc(rows_go, 1)
                        for k in range(e * (U // 2), e * (U // 2) + POOL_ROWS):
                            ins = pool.tensor_scalar(ra[:, k, :], iota[:, :], idc[:, 0, k:k + 1], None, ALU.is_equal)
                        ins.then_inc(hot_row, 1)

                def norm(i):
                    y = r[:, i % CT, :]
                    pool.wait_ge(n_ready, i + 1)
                    pool.tensor_tensor(y, y, ln_g, ALU.mult).then_inc(y_mul, 1)
                    pool.wait_ge(y_mul, i + 1)
                    pool.tensor_tensor(y, y, ln_b, ALU.add).then_inc(y_ready, 1)

                def step(n):
                    def at(kind, it, p, body):
                        q, m = p % S, body * S + p % S
                        g = m + n * NEt
                        if n + 1 < NC and kind == "scatter":
                            scatter(it, q, n + 1)
                        if not fixed(m) or g + 1 < NC * NEt:
                            split_v((q + 1) % 2, g + 1)
                        if kind == "norm" and q % 2 == 0 and q // 2 < CT:
                            norm((n - 1) * CT + q // 2)
                    return at

                pool.sem_inc(hot_row, 2)
                split_v(0, 0)
                with pool.Fori(0, UNITS // S) as it:
                    for q in range(S):
                        scatter(it, q, 0)
                for n in range(NC):
                    schedule(pool, n, step(n))
                for t in range(CT):
                    norm((NC - 1) * CT + t)

            @block.scalar
            def _(act):
                act.sem_inc(emptied, 1)

                def split_u(t, g, loads):
                    act.wait_ge(ul[t], loads * 16)
                    act.activation(uR[:, t, :, :], uw[:, t, :, :], ACT.Copy).then_inc(u_r, 1)

                def split_v(t, loads):
                    act.wait_ge(vl[t], loads * 16)
                    act.activation(vR[:, t, :], vw[:, t, :], ACT.Copy).then_inc(v_r, 1)

                def split_h(n):
                    act.activation(hR[:, :, :], h2T[:, :, n * CW:(n + 1) * CW], ACT.Copy).then_inc(h_r, 1)

                def gelu(g):
                    act.wait_ge(a_mm, g + 1)
                    if not fixed(g) or g:
                        act.wait_ge(c_l, g)
                    act.activation(ga[:, :], A[:, 0:CW], ACT.Gelu).then_inc(a_ev, 1)

                def route(kind, it, q, cn, alone=False):
                    f0 = cn * FILLS
                    banks = spare(alone)
                    if kind == "list":
                        f = (it * S + q) * 2 + f0
                        act.wait_ge(filled, f + 1)
                        act.activation(qs[:, :], banks[0][:, 0:CW], ACT.Copy).then_inc(emptied, 1)
                        act.wait_ge(filled, f + 2)
                        act.wait_ge(listed, it * S + q + (cn * HS + 1))
                        act.activation(s[:, q % 2, :, :], banks[1][:, 0:CW].rearrange("p (t k) -> p t k", t=CT),
                                       ACT.Copy).then_inc(emptied, 1)
                    if kind == "head" and q == 2 * S - 1:
                        act.wait_ge(e_in, it + cn * CT + 1)
                        act.activation(ex[:, :, :], fs[:, :, :], ACT.Exp).then_inc(e_out, 1)
                        act.wait_ge(filled, it + (f0 + F_HEAD + 1))
                        act.activation(idxT[:, :, bass.ds(it * P, P)],
                                       E[:, 0:3 * P].rearrange("p (w t) -> p w t", w=3), ACT.Copy).then_inc(emptied, 1)
                    if kind == "scatter":
                        b = q // 4
                        if q % 4 == 0:
                            act.wait_ge(stored_g[b], (it + cn * (CB // 2) + 1) * 16)
                        for e in range(2):
                            act.wait_ge(filled, (it * S + q) * 2 + (f0 + F_SCAT + e + 1))
                            at = (q % 4) * U + e * (U // 2)
                            act.activation(stage[:, b, :, at:at + U // 2].rearrange("p i t -> p t i"),
                                           banks[e][:, :].rearrange("p (t i) -> p t i", t=U // 2),
                                           ACT.Copy).then_inc(emptied, 1)

                def norm(i):
                    act.wait_ge(ve_ready, i + 1)
                    act.activation(sd[:, :], ve[:, :], ACT.Sqrt).then_inc(sd_ready, 1)

                def step(n):
                    def at(kind, it, p, body):
                        q, m = p % S, body * S + p % S
                        g = m + n * NEt
                        half = body * (S // 2) + n * NEt // 2
                        left = NC * NEt - g if fixed(m) else NEt
                        if kind == "scatter" and q == 0 and n:
                            act.wait_ge(y_out, n * CT * 16)
                        if fixed(m) and m == NEt - 1 and n + 1 < NC:
                            act.wait_ge(a_mm, g + 1)
                            split_h(n + 1)
                        if left > 2:
                            act.wait_ge(a_mm, g + 1)
                            split_u(q % 2, g + 2, half + (q + 2) // 2 + 1)
                        if left > 1:
                            act.wait_ge(v_mm, g + 1)
                            split_v((q + 1) % 2, half + (q + 1) // 2 + 1)
                        if not fixed(m) or m < NEt - 1:
                            gelu(g + 1)
                        if kind == "norm" and q % 2 == 0 and q // 2 < CT:
                            norm((n - 1) * CT + q // 2)
                        if n + 1 < NC:
                            route(kind, it, p, n + 1)
                    return at

                split_u(0, 0, 1)
                split_u(1, 1, 1)
                split_v(0, 1)
                split_h(0)
                routed(act, lambda kind, it, p: route(kind, it, p, 0, True))
                for n in range(NC):
                    gelu(n * NEt)
                    schedule(act, n, step(n))
                for t in range(CT):
                    norm((NC - 1) * CT + t)

            @block.tensor
            def _(pe):
                pe.sem_inc(v_mm, 1)
                pe.wait_ge(const, 3)

                def hidden(t, g):
                    pe.wait_ge(u_l, g + 1)
                    if not fixed(g) or g:
                        pe.wait_ge(a_ev, g)
                    for k in range(DK):
                        for w, h in ((uR, hR), (uR, hL), (uL, hR)):
                            mm = pe.matmul(A[:, 0:CW], w[:, t, k, :], h[:, k, :],
                                           start=(k == 0 and w is uR and h is hR),
                                           stop=(k == DK - 1 and w is uL))
                    mm.then_inc(a_mm, 1)

                def down(t, tiles):
                    for tt in tiles:
                        for w, v in ((cR, vR), (cR, vL), (cL, vR)):
                            for half in range(2):
                                mm = pe.matmul(ACC[2 * tt + half][:, :], w[:, t, tt * P:(tt + 1) * P],
                                               v[:, t, half * 512:(half + 1) * 512], start=False, stop=False,
                                               skip_group_check=True)
                    return mm

                def route(kind, it, q, cn, e, alone=False):
                    f0 = cn * FILLS
                    bank = spare(alone)[e]
                    if kind == "list":
                        f = (it * S + q) * 2 + (f0 + e)
                        pe.wait_ge(emptied, f + (0 if alone and q and not e else 1))
                        if e == 0:
                            pe.wait_ge(wl[q % 2], (it * (S // 2) + (cn * (HS // 2) + q // 2 + 1)) * 16)
                            for k in range(DK):
                                mm = pe.matmul(bank[:, 0:CW], wq[:, q % 2, k, :], h2T[:, k, cn * CW:(cn + 1) * CW],
                                               start=(k == 0), stop=(k == DK - 1))
                        else:
                            for t in range(CT):
                                mm = pe.matmul(bank[:, t * NKEY:(t + 1) * NKEY], qs[:, t * P:(t + 1) * P],
                                               wq[:, q % 2, DK, :], start=True, stop=True)
                        mm.then_inc(filled, 1)
                    if kind == "head" and q == 2 * S - 1 and e == 1:
                        pe.wait_ge(emptied, it + (f0 + F_HEAD + 1))
                        pe.wait_ge(o_ready, it + (cn * CT + 1))
                        for w in range(3):
                            mm = pe.transpose(E[:, w * P:(w + 1) * P], out[:, w, :], ident[:, :])
                        mm.then_inc(filled, 1)
                    if kind == "scatter":
                        pe.wait_ge(emptied, (it * S + q) * 2 + (f0 + F_SCAT + e + 1 - alone))
                        pe.wait_ge(hot_row, (it * S + q) * 2 + (cn * 2 * UNITS + e + 3))
                        pe.wait_ge(hot, (it * S + q) * 2 + (cn * 2 * UNITS + e + 3))
                        for t in range(U // 2):
                            k = e * (U // 2) + t
                            mm = pe.matmul(bank[:, t * P:(t + 1) * P], cb[:, k, :], ra[:, k, :], start=True, stop=True)
                        mm.then_inc(filled, 1)

                def step(n):
                    def at(kind, it, p, body):
                        q, m = p % S, body * S + p % S
                        g = m + n * NEt
                        if not fixed(m) or m < NEt - 1:
                            hidden((q + 1) % 2, g + 1)
                        pe.wait_ge(c_l, g + 1)
                        pe.wait_ge(v_l, g + 1)
                        down(q % 2, (0,))
                        if n + 1 < NC:
                            route(kind, it, p, n + 1, 0)
                        down(q % 2, range(1, CT)).then_inc(v_mm, 1)
                        if n + 1 < NC:
                            route(kind, it, p, n + 1, 1)
                    return at

                def both(kind, it, p):
                    route(kind, it, p, 0, 0, True)
                    route(kind, it, p, 0, 1, True)

                routed(pe, both)
                pe.wait_ge(emptied, FILLS + 1)
                for n in range(NC):
                    pe.wait_ge(h_l, n + 1)
                    hidden(0, n * NEt)
                    if n:
                        pe.wait_ge(acc_read, n)
                    for bank in ACC:
                        pe.matmul(bank[:, :], zero[:, 0:P], zero[:, :], start=True, stop=False, skip_group_check=True)
                    schedule(pe, n, step(n))
                    for bank in ACC:
                        mm = pe.matmul(bank[:, :], zero[:, 0:P], zero[:, :], start=False, stop=True,
                                       skip_group_check=True)
                    mm.then_inc(acc_done, 1)

            @block.vector
            def _(dve):
                dve.sem_inc(listed, 2)
                dve.wait_ge(const, 3)

                def split_u(t, g):
                    dve.wait_ge(u_r, g + 1)
                    dve.tensor_tensor(uL[:, t, :, :], uw[:, t, :, :], uR[:, t, :, :].bitcast(F32),
                                      ALU.subtract).then_inc(u_l, 1)

                def split_h(n):
                    dve.wait_ge(h_r, n + 1)
                    dve.tensor_tensor(hL[:, :, :], h2T[:, :, n * CW:(n + 1) * CW], hR[:, :, :].bitcast(F32),
                                      ALU.subtract).then_inc(h_l, 1)

                def weigh(t, g, q, loads):
                    if loads is not None:
                        dve.wait_ge(gl[loads[0]], loads[1] * 16)
                    slot = (q // UB) % 2
                    dve.wait_ge(a_ev, g + 1)
                    gv = ga[:, :].rearrange("p (c t) -> p c t", c=CB)
                    dve.tensor_tensor(gv, gv, gw[:, slot, :, q % UB, :], ALU.mult).then_inc(c_f, 1)
                    dve.wait_ge(v_mm, g)
                    dve.wait_ge(c_f, g + 1)
                    dve.tensor_copy(cR[:, t, :], ga[:, :]).then_inc(c_r, 1)
                    dve.wait_ge(c_r, g + 1)
                    dve.tensor_tensor(cL[:, t, :], ga[:, :], cR[:, t, :].bitcast(F32), ALU.subtract).then_inc(c_l, 1)

                def route_list(it, q, cn):
                    dve.wait_ge(emptied, (it * S + q) * 2 + (cn * FILLS + 3))
                    ch = Count(dve, chain)
                    for half in range(2):
                        sl = slice(half * 8, half * 8 + 8)
                        for t in range(CT):
                            ins = dve.max(tv[:, t, sl], s[:, q % 2, t, :])
                        ch.step(ins)
                        for t in range(CT):
                            ins = dve.max_index(ti[:, t, sl], tv[:, t, sl], s[:, q % 2, t, :])
                        ch.step(ins)
                        if half == 0:
                            for t in range(CT):
                                ins = dve.match_replace(s[:, q % 2, t, :], tv[:, t, sl], s[:, q % 2, t, :], LOW)
                            ch.step(ins)
                    dve.tensor_copy(top[:, :, it * S + q, :], tv[:, :, :])
                    dve.tensor_copy(itf[:, :, it * S + q, :], ti[:, :, :]).then_inc(listed, 1)
                    dve.wait_ge(listed, it * S + q + (cn * HS + 3))

                def head_values(t, h, cn):
                    dve.tensor_tensor(cand[:, :].rearrange("p (a b) -> p a b", a=TOPK),
                                      top[:, t, 2 * h, :].rearrange("p (a o) -> p a o", o=1).to_broadcast(
                                          [P, TOPK, TOPK]),
                                      top[:, t, 2 * h + 1, :].rearrange("p (o b) -> p o b", o=1).to_broadcast(
                                          [P, TOPK, TOPK]), ALU.add).then_inc(heads, 1)
                    dve.wait_ge(heads, (t * PH + h) + (cn * CT * PH + 1))
                    ch = Count(dve, chain)
                    for half in range(2):
                        sl = slice(half * 8, half * 8 + 8)
                        ch.step(dve.max(fs[:, h, sl], cand[:, :]))
                        ch.step(dve.max_index(fp[:, h, sl], fs[:, h, sl], cand[:, :]))
                        if half == 0:
                            ch.step(dve.match_replace(cand[:, :], fs[:, h, sl], cand[:, :], LOW))

                def head_keys(t, h, cn):
                    ch = Count(dve, chain)
                    dve.tensor_scalar(ab[:, 0, :], fp[:, h, :], 4, None, ALU.logical_shift_right)
                    ch.step(dve.tensor_scalar(ab[:, 1, :], fp[:, h, :], TOPK - 1, None, ALU.bitwise_and))
                    ch.step(dve.tensor_copy(abf[:, :, :], ab[:, :, :]))
                    ch.step(dve.tensor_tensor(
                        eq[:, :, :, :],
                        i16[:, :].rearrange("p (a b k) -> p a b k", a=1, b=1).to_broadcast([P, 2, TOPK, TOPK]),
                        abf[:, :, :].rearrange("p w (k o) -> p w k o", o=1).to_broadcast([P, 2, TOPK, TOPK]),
                        ALU.is_equal))
                    ch.step(dve.tensor_tensor(
                        eq[:, :, :, :], eq[:, :, :, :],
                        itf[:, t, 2 * h:2 * h + 2, :].rearrange("p w (o k) -> p w o k", o=1).to_broadcast(
                            [P, 2, TOPK, TOPK]), ALU.mult))
                    if h == 0:
                        dve.wait_ge(emptied, t + (cn * FILLS + F_HEAD + 1))
                    dve.tensor_reduce(out[:, 0:2, h * TOPK:(h + 1) * TOPK], eq[:, :, :, :], axis=AX.X,
                                      op=ALU.add).then_inc(picked, 1)
                    dve.wait_ge(picked, (t * PH + h) + (cn * CT * PH + 1))

                def route_softmax(t, cn):
                    ch = Count(dve, chain)
                    ch.step(dve.tensor_copy(sm[:, :], fs[:, :, 0]))
                    dve.tensor_tensor(fs[:, :, :], fs[:, :, :],
                                      sm[:, :].rearrange("p (h o) -> p h o", o=1).to_broadcast([P, PH, TOPK]),
                                      ALU.subtract).then_inc(e_in, 1)
                    dve.wait_ge(e_out, t + (cn * CT + 1))
                    ch.step(dve.tensor_reduce(sm[:, :], ex[:, :, :], axis=AX.X, op=ALU.add))
                    ch.step(dve.reciprocal(ri[:, :], sm[:, :]))
                    dve.tensor_tensor(out[:, 2, :].rearrange("p (h k) -> p h k", h=PH), ex[:, :, :],
                                      ri[:, :].rearrange("p (h o) -> p h o", o=1).to_broadcast([P, PH, TOPK]),
                                      ALU.mult).then_inc(o_ready, 1)
                    dve.wait_ge(o_ready, t + (cn * CT + 1))

                def route_scatter(it, q, cn):
                    unit = it * S + q
                    f = unit * 2 + (cn * FILLS + F_SCAT)
                    dve.wait_ge(emptied, cn * FILLS + F_SCAT + 1)
                    dve.wait_ge(hot, unit * 2 + (cn * 2 * UNITS + 2))
                    dve.wait_ge(hot_row, unit * 2 + (cn * 2 * UNITS + 2))
                    dve.tensor_copy(idc[:, :, :], idxT[:, :, bass.ds(unit * U, U)]).then_inc(idc_in, 1)
                    dve.wait_ge(idc_in, unit + (cn * UNITS + 1))
                    for e in range(2):
                        dve.wait_ge(filled, f + (e - 1))
                        for k in range(e * (U // 2), (e + 1) * (U // 2)):
                            if k % (U // 2) >= POOL_ROWS:
                                dve.tensor_scalar(ra[:, k, :], iota[:, :], idc[:, 0, k:k + 1], None, ALU.is_equal)
                            ins = dve.tensor_scalar(cb[:, k, :], iota[:, :], idc[:, 1, k:k + 1],
                                                    idc[:, 2, k:k + 1], ALU.is_equal, ALU.mult)
                        ins.then_inc(hot, 1)

                def norm(i):
                    y = r[:, i % CT, :]
                    ch = Count(dve, chain)
                    dve.wait_ge(x1_in, (i + 1) * 16)
                    dve.scalar_tensor_tensor(y, x1, ALPHA, y, ALU.mult, ALU.add).then_inc(x1_used, 1)
                    dve.wait_ge(x1_used, i + 1)
                    for half in range(2):
                        ins = dve.bn_stats(st[:, half, :], y[:, half * 512:(half + 1) * 512])
                    ch.step(ins)
                    ch.step(dve.bn_aggr(mv[:, :], st[:, :, :].rearrange("p a b -> p (a b)")))
                    dve.tensor_scalar(ve[:, :], mv[:, 1:2], EPS, None, ALU.add).then_inc(ve_ready, 1)
                    dve.wait_ge(sd_ready, i + 1)
                    ch.step(dve.reciprocal(rs[:, :], sd[:, :]))
                    dve.tensor_scalar(y, y, mv[:, 0:1], rs[:, 0:1], ALU.subtract, ALU.mult).then_inc(n_ready, 1)
                    dve.wait_ge(n_ready, i + 1)

                def read_sums(n):
                    dve.wait_ge(acc_done, n + 1)
                    dve.wait_ge(ln_in, (n + 1) * 64)
                    for t in range(CT):
                        gate = gate_1 if t else gate_0
                        for half in range(2):
                            sl = slice(half * 512, (half + 1) * 512)
                            ins = dve.tensor_tensor(r[:, t, sl], gate[:, sl], ACC[2 * t + half][:, :], ALU.mult)
                    ins.then_inc(acc_read, 1)
                    dve.wait_ge(acc_read, n + 1)

                def route(kind, it, q, cn):
                    if kind == "list":
                        route_list(it, q, cn)
                    if kind == "head":
                        (head_keys if q % 2 else head_values)(it, q // 2, cn)
                        if q == 2 * S - 1:
                            route_softmax(it, cn)
                    if kind == "scatter":
                        route_scatter(it, q, cn)

                def step(n):
                    def at(kind, it, p, body):
                        q, m = p % S, body * S + p % S
                        g = m + n * NEt
                        if n + 1 < NC and kind == "scatter":
                            route(kind, it, p, n + 1)
                        if not fixed(m) or g + 2 < NC * NEt:
                            split_u(q % 2, g + 2)
                        if not fixed(m) or m < NEt - 1:
                            loads = None
                            if (q + 1) % UB == 0:
                                b = ((q + 1) // UB) % 2
                                at_ = body + (q + 1) // S
                                loads = (b, at_ + (n * (NEt // S) + 1))
                            weigh((q + 1) % 2, g + 1, q + 1, loads)
                        if kind == "norm" and q % 2 == 0 and q // 2 < CT:
                            norm((n - 1) * CT + q // 2)
                        if n + 1 < NC and kind in ("list", "head"):
                            route(kind, it, p, n + 1)
                    return at

                dve.sem_inc(hot, 2)
                split_u(0, 0)
                split_u(1, 1)
                split_h(0)
                routed(dve, lambda kind, it, p: route(kind, it, p, 0))
                for n in range(NC):
                    weigh(0, n * NEt, 0, (0, n * (NEt // S) + 1))
                    schedule(dve, n, step(n))
                    if n + 1 < NC:
                        split_h(n + 1)
                    read_sums(n)
                for t in range(CT):
                    norm((NC - 1) * CT + t)


SHAPES = {"y": [T, D], "new_ckv": [SEQ, KVR], "new_krope": [SEQ, ROPE]}


def kernel(x_prompt, x_sample, cache_ckv, cache_krope, c, c_ctx, w_mod, b_mod, w_in, w_s, b_s,
           g_q, w_qb, g_kv, w_kvb, w_o, ln1_g, ln1_b, w_pq, sub_keys, u_tab, v_tab, ln2_g, ln2_b):
    import concourse.bacc as bacc
    from concourse.bass_utils import run_bass_kernel_spmd

    def rows(w, k):
        return w.reshape(k, P, -1).transpose(1, 0, 2)

    def every_row(v):
        return np.broadcast_to(v.reshape(1, -1), (P, v.size))

    n = {k: np.asarray(v) for k, v in dict(locals()).items() if not callable(v)}
    x = np.concatenate([n["x_prompt"][0], n["x_sample"][0]], axis=0)
    wqb = n["w_qb"][0].reshape(QR, H, NOPE + ROPE)
    wkvb = n["w_kvb"][0].reshape(KVR, H, NOPE + VD)
    f = ROPE // 4
    freq = (1.0 / (np.float32(10000.0) ** (np.arange(f, dtype=np.float32) / np.float32(f)))).astype(np.float32)
    tok = np.arange(DEC)
    ang = [np.float32(v)[:, None] * freq[None, :] for v in ((tok // GRID_W).astype(np.float32),
                                                            (tok % GRID_W).astype(np.float32))]
    cos, sin = [np.cos(v).astype(np.float32) for v in ang], [np.sin(v).astype(np.float32) for v in ang]
    table = np.zeros((NT, P, 2, ROPE), np.float32)
    table[1:, :, 0] = np.concatenate([cos[0], cos[0], cos[1], cos[1]], 1).reshape(NT - 1, P, ROPE)
    table[1:, :, 1] = np.concatenate([-sin[0], sin[0], -sin[1], sin[1]], 1).reshape(NT - 1, P, ROPE)
    arrays = {
        "x": x,
        "xT": x.reshape(NT, P, DK, P).transpose(0, 3, 2, 1),
        "cond": np.stack([n["c_ctx"].reshape(DK, P), n["c"].reshape(DK, P)], -1).transpose(1, 0, 2),
        "w_mod": n["w_mod"][0].reshape(DK, P, 6 * DK, P).transpose(2, 1, 0, 3),
        "b_mod": n["b_mod"][0].reshape(6 * DK, P).T,
        "w_in": rows(n["w_in"][0], DK),
        "w_s": n["w_s"][0].transpose(2, 0, 1),
        "b_s": n["b_s"][0].T,
        "g_q": n["g_q"][0].reshape(QK, P).T,
        "g_kv": every_row(n["g_kv"][0]),
        "w_qn": rows(wqb[:, :, :NOPE].reshape(QR, -1), QK),
        "w_qr": rows(wqb[:, :, NOPE:].reshape(QR, -1), QK),
        "w_kn": rows(wkvb[:, :, :NOPE].reshape(KVR, -1), KK),
        "w_v": rows(wkvb[:, :, NOPE:].reshape(KVR, -1), KK),
        "cckT": rows(n["cache_ckv"][0, 0].T, KK),
        "ckrT": n["cache_krope"][0, 0].T,
        "rot": table,
        "w_o": rows(n["w_o"][0], DK),
        "ln1_g": every_row(n["ln1_g"][0]),
        "ln1_b": every_row(n["ln1_b"][0]),
        "w_pq": np.concatenate([n["w_pq"][0].reshape(DK, P, HS, P).transpose(2, 1, 0, 3),
                                n["sub_keys"][0].reshape(HS, NKEY, 1, P).transpose(0, 3, 2, 1)], axis=2),
        "u": n["u_tab"][0].reshape(NE // P, P, DK, P).transpose(0, 3, 2, 1),
        "v": n["v_tab"][0].reshape(NE // P, P, D),
        "ln2_g": every_row(n["ln2_g"][0]),
        "ln2_b": every_row(n["ln2_b"][0]),
    }
    nc = bacc.Bacc("TRN2", target_bir_lowering=False, num_devices=1)
    ins, aps = {}, {}
    for name, v in arrays.items():
        v = np.ascontiguousarray(v)
        ins[f"in_{name}"] = v
        aps[name] = nc.dram_tensor(f"in_{name}", v.shape, mybir.dt.from_np(v.dtype), kind="ExternalInput").ap()
    for name, shape in SHAPES.items():
        aps[name] = nc.dram_tensor(f"out_{name}", shape, F32, kind="ExternalOutput").ap()
    build(nc, aps)
    got = run_bass_kernel_spmd(nc, [ins], core_ids=[0]).results[0]
    y = got["out_y"]
    return (y[:SEQ].reshape(1, SEQ, D), y[SEQ:].reshape(1, DEC, D),
            got["out_new_ckv"].reshape(1, 1, SEQ, KVR), got["out_new_krope"].reshape(1, 1, SEQ, ROPE))
```
